# Optimizing a Trainium2 kernel written in Bass

```python
import jax, jax.numpy as jnp
from jax import lax
import numpy as np
import math

D_MODEL = 1024
BATCH = 1
SEQ = 512
DEPTH = 2

HEAD_DIM = 64
ATTN_HEADS = 8
ATTN_KV_HEADS = 2
ATTN_GROUP = ATTN_HEADS // ATTN_KV_HEADS
WINDOW = 128
ATTN_BLOCK = 128
ROPE_THETA = 10000.0

RET_HEADS = 4
RET_DK = 64
RET_DV = 64
RET_CHUNK = 128

GLA_HEADS = 4
GLA_DK = 32
GLA_DV = 64
GLA_CHUNK = 64
GLA_GATE_RANK = 16
GLA_GATE_NORMALIZER = 16.0

EPS = 1e-6

ATTN_W = ATTN_HEADS * HEAD_DIM
RET_W = RET_HEADS * RET_DV
GLA_W = GLA_HEADS * GLA_DV
D_MIX = ATTN_W + RET_W + GLA_W

IN_SIZES = (
    ATTN_HEADS * HEAD_DIM, ATTN_KV_HEADS * HEAD_DIM, ATTN_KV_HEADS * HEAD_DIM, ATTN_W,
    RET_HEADS * RET_DK, RET_HEADS * RET_DK, RET_HEADS * RET_DV, RET_W,
    GLA_HEADS * GLA_DK, GLA_HEADS * GLA_DK, GLA_HEADS * GLA_DV, GLA_W,
    GLA_GATE_RANK,
)
D_IN = sum(IN_SIZES)
IN_SPLITS = [int(s) for s in np.cumsum(IN_SIZES)[:-1]]


def rms_norm(x, gain=None):
    xf = x.astype(jnp.float32)
    y = xf * lax.rsqrt(jnp.mean(xf * xf, axis=-1, keepdims=True) + EPS)
    if gain is not None:
        y = y * gain.astype(jnp.float32)
    return y.astype(x.dtype)

def apply_rotary(x, positions, inv_freq):
    ang = positions.astype(jnp.float32)[..., None] * inv_freq
    cos = jnp.cos(ang)[:, :, None, :]
    sin = jnp.sin(ang)[:, :, None, :]
    x1, x2 = jnp.split(x.astype(jnp.float32), 2, axis=-1)
    out = jnp.concatenate([x1 * cos - x2 * sin, x2 * cos + x1 * sin], axis=-1)
    return out.astype(x.dtype)

def sliding_window_attention(q, k, v, sinks):
    B, S, H, D = q.shape
    nb = S // ATTN_BLOCK
    qb = q.reshape(B, nb, ATTN_BLOCK, ATTN_KV_HEADS, ATTN_GROUP, D)
    kb = k.reshape(B, nb, ATTN_BLOCK, ATTN_KV_HEADS, D)
    vb = v.reshape(B, nb, ATTN_BLOCK, ATTN_KV_HEADS, D)

    def with_prev(t):
        prev = jnp.pad(t, ((0, 0), (1, 0), (0, 0), (0, 0), (0, 0)))[:, :-1]
        return jnp.concatenate([prev, t], axis=2)

    kk, vv = with_prev(kb), with_prev(vb)
    s = jnp.einsum('bnqhgd,bnkhd->bnhgqk', qb, kk).astype(jnp.float32) * (D ** -0.5)
    i = jnp.arange(ATTN_BLOCK)[:, None]
    j = jnp.arange(2 * ATTN_BLOCK)[None, :]
    rel = i + ATTN_BLOCK - j
    kpos = (jnp.arange(nb)[:, None] - 1) * ATTN_BLOCK + jnp.arange(2 * ATTN_BLOCK)[None, :]
    valid = ((rel >= 0) & (rel < WINDOW))[None] & (kpos >= 0)[:, None, :]
    s = jnp.where(valid[None, :, None, None], s, -1e30)
    sink = sinks.astype(jnp.float32).reshape(ATTN_KV_HEADS, ATTN_GROUP)[None, None, :, :, None, None]
    sink = jnp.broadcast_to(sink, s.shape[:-1] + (1,))
    p = jax.nn.softmax(jnp.concatenate([s, sink], axis=-1), axis=-1)[..., :-1]
    o = jnp.einsum('bnhgqk,bnkhd->bnqhgd', p.astype(v.dtype), vv)
    return o.reshape(B, S, H * D)

def retention(q, k, v):
    B, S, H, Dk = q.shape
    Dv = v.shape[-1]
    C = RET_CHUNK
    nc = S // C
    f32 = jnp.float32
    log_g = jnp.log(1.0 - 2.0 ** (-5.0 - jnp.arange(H, dtype=f32)))
    idx = jnp.arange(C, dtype=f32)
    diff = idx[:, None] - idx[None, :]
    dmask = jnp.where(diff >= 0, jnp.exp(log_g[:, None, None] * jnp.maximum(diff, 0.0)), 0.0)
    q_decay = jnp.exp(log_g[:, None] * (idx + 1.0))[..., None]
    k_decay = jnp.exp(log_g[:, None] * (C - 1.0 - idx))[..., None]
    chunk_decay = jnp.exp(log_g * C)[:, None, None]

    def to_chunks(t):
        return t.astype(f32).reshape(B, nc, C, H, t.shape[-1]).transpose(1, 0, 3, 2, 4)

    qc, kc, vc = to_chunks(q), to_chunks(k * (Dk ** -0.5)), to_chunks(v)

    def step(state, inp):
        qi, ki, vi = inp
        sc = jnp.einsum('bhid,bhjd->bhij', qi, ki) * dmask
        intra = jnp.einsum('bhij,bhjv->bhiv', sc, vi)
        inter = jnp.einsum('bhid,bhdv->bhiv', qi * q_decay, state)
        new_state = chunk_decay * state + jnp.einsum('bhjd,bhjv->bhdv', ki * k_decay, vi)
        return new_state, intra + inter

    state0 = jnp.zeros((B, H, Dk, Dv), f32)
    _, out = lax.scan(step, state0, (qc, kc, vc))
    return out.transpose(1, 0, 3, 2, 4).reshape(B, S, H, Dv).astype(v.dtype)

def gated_linear_attention(q, k, v, log_a):
    B, S, H, Dk = q.shape
    Dv = v.shape[-1]
    C = GLA_CHUNK
    nc = S // C
    f32 = jnp.float32

    def to_chunks(t):
        return t.astype(f32).reshape(B, nc, C, H, t.shape[-1]).transpose(1, 0, 3, 2, 4)

    qc, kc, vc, gc = to_chunks(q * (Dk ** -0.5)), to_chunks(k), to_chunks(v), to_chunks(log_a)
    causal = jnp.tril(jnp.ones((C, C), dtype=bool))[..., None]

    def step(state, inp):
        qi, ki, vi, gi = inp
        b = jnp.cumsum(gi, axis=2)
        rel = b[:, :, :, None, :] - b[:, :, None, :, :]
        decay = jnp.where(causal, jnp.exp(jnp.minimum(rel, 0.0)), 0.0)
        sc = jnp.einsum('bhid,bhijd,bhjd->bhij', qi, decay, ki)
        intra = jnp.einsum('bhij,bhjv->bhiv', sc, vi)
        inter = jnp.einsum('bhid,bhdv->bhiv', qi * jnp.exp(b), state)
        b_last = b[:, :, -1:, :]
        new_state = (jnp.exp(b_last)[:, :, 0, :, None] * state
                     + jnp.einsum('bhjd,bhjv->bhdv', ki * jnp.exp(b_last - b), vi))
        return new_state, intra + inter

    state0 = jnp.zeros((B, H, Dk, Dv), f32)
    _, out = lax.scan(step, state0, (qc, kc, vc, gc))
    return out.transpose(1, 0, 3, 2, 4).reshape(B, S, H, Dv).astype(v.dtype)

def hybrid_layer(x, c_act, positions, w_mod, b_mod, pre_gain, post_gain, w_in, sinks,
                 gla_gate_w, gla_gate_b, gla_norm_gain, w_out):
    B, S, _ = x.shape
    mod = c_act @ w_mod + b_mod
    shift, scale, gate = jnp.split(mod[:, None, :], 3, axis=-1)
    h = rms_norm(x, pre_gain) * (1.0 + scale) + shift
    proj = h @ w_in
    (aq, ak, av, ag, rq, rk, rv, rg, gq, gk, gv, gg, ga) = jnp.split(proj, IN_SPLITS, axis=-1)

    rope_freq = ROPE_THETA ** (-jnp.arange(0, HEAD_DIM, 2, dtype=jnp.float32) / HEAD_DIM)
    aq = apply_rotary(aq.reshape(B, S, ATTN_HEADS, HEAD_DIM), positions, rope_freq)
    ak = apply_rotary(ak.reshape(B, S, ATTN_KV_HEADS, HEAD_DIM), positions, rope_freq)
    av = av.reshape(B, S, ATTN_KV_HEADS, HEAD_DIM)
    a_out = sliding_window_attention(aq, ak, av, sinks) * jax.nn.silu(ag)

    ret_freq = 1.0 / (10000.0 ** jnp.linspace(0.0, 1.0, RET_DK // 2, dtype=jnp.float32))
    rq = apply_rotary(rq.reshape(B, S, RET_HEADS, RET_DK), positions, ret_freq)
    rk = apply_rotary(rk.reshape(B, S, RET_HEADS, RET_DK), positions, ret_freq)
    r = retention(rq, rk, rv.reshape(B, S, RET_HEADS, RET_DV))
    r_out = rms_norm(r).reshape(B, S, RET_W) * jax.nn.silu(rg)

    gate_logits = (ga @ gla_gate_w + gla_gate_b).astype(jnp.float32)
    log_a = (jax.nn.log_sigmoid(gate_logits) / GLA_GATE_NORMALIZER).reshape(B, S, GLA_HEADS, GLA_DK)
    g = gated_linear_attention(gq.reshape(B, S, GLA_HEADS, GLA_DK), gk.reshape(B, S, GLA_HEADS, GLA_DK),
                               gv.reshape(B, S, GLA_HEADS, GLA_DV), log_a)
    g_out = rms_norm(g, gla_norm_gain).reshape(B, S, GLA_W) * jax.nn.silu(gg)

    y = jnp.concatenate([a_out, r_out, g_out], axis=-1) @ w_out
    return x + gate * rms_norm(y, post_gain)

def first_inputs(seed: int = 0) -> dict:
    key = jax.random.key(seed)
    ks = jax.random.split(key, 16)
    f32 = jnp.float32
    x = jax.random.normal(ks[0], (BATCH, SEQ, D_MODEL), f32)
    c = jax.random.normal(ks[1], (BATCH, D_MODEL), f32)
    positions = jnp.broadcast_to(jnp.arange(SEQ, dtype=jnp.int32)[None, :], (BATCH, SEQ))
    w_mod = jax.random.normal(ks[2], (DEPTH, D_MODEL, 3 * D_MODEL), f32) * (0.5 * D_MODEL ** -0.5)
    b_mod = jax.random.normal(ks[3], (DEPTH, 3 * D_MODEL), f32) * 0.01
    pre_norm_gain = 1.0 + 0.02 * jax.random.normal(ks[4], (DEPTH, D_MODEL), f32)
    post_norm_gain = 1.0 + 0.02 * jax.random.normal(ks[5], (DEPTH, D_MODEL), f32)
    w_in = jax.random.normal(ks[6], (DEPTH, D_MODEL, D_IN), f32) * (D_MODEL ** -0.5)
    attn_sinks = 0.5 * jax.random.normal(ks[7], (DEPTH, ATTN_HEADS), f32)
    gla_gate_w = jax.random.normal(ks[8], (DEPTH, GLA_GATE_RANK, GLA_HEADS * GLA_DK), f32) * (GLA_GATE_RANK ** -0.5)
    gla_gate_b = 0.01 * jax.random.normal(ks[9], (DEPTH, GLA_HEADS * GLA_DK), f32)
    gla_norm_gain = 1.0 + 0.02 * jax.random.normal(ks[10], (DEPTH, GLA_DV), f32)
    w_out = jax.random.normal(ks[11], (DEPTH, D_MIX, D_MODEL), f32) * (D_MIX ** -0.5)
    return {"x": x, "c": c, "positions": positions, "w_mod": w_mod, "b_mod": b_mod,
            "pre_norm_gain": pre_norm_gain, "post_norm_gain": post_norm_gain, "w_in": w_in,
            "attn_sinks": attn_sinks, "gla_gate_w": gla_gate_w, "gla_gate_b": gla_gate_b,
            "gla_norm_gain": gla_norm_gain, "w_out": w_out}

def first_block(x, c, positions, w_mod, b_mod, pre_norm_gain, post_norm_gain, w_in,
              attn_sinks, gla_gate_w, gla_gate_b, gla_norm_gain, w_out):
    c_act = jax.nn.silu(c)
    for l in range(DEPTH):
        x = hybrid_layer(x, c_act, positions, w_mod[l], b_mod[l], pre_norm_gain[l], post_norm_gain[l],
                         w_in[l], attn_sinks[l], gla_gate_w[l], gla_gate_b[l], gla_norm_gain[l], w_out[l])
    return x


GRID_W = 64
CTX_LEN = 256
Q_BLOCK = 128
NEG_INF = -1e30

A_Q_HEADS = 8
A_KV_HEADS = 2
A_GROUP = A_Q_HEADS // A_KV_HEADS
B_HEADS = 8
B_Q_RANK = 256
B_KV_RANK = 128
B_NOPE = 64
B_ROPE = 32
B_V = 64
C_Q_HEADS = 8
C_KV_HEADS = 2
C_GROUP = C_Q_HEADS // C_KV_HEADS
D_HEADS = 4
D_V = 2 * HEAD_DIM

EVEN_SIZES = (A_Q_HEADS * HEAD_DIM, A_KV_HEADS * HEAD_DIM, A_KV_HEADS * HEAD_DIM, B_Q_RANK, B_KV_RANK, B_ROPE)
ODD_SIZES = (C_Q_HEADS * HEAD_DIM, C_KV_HEADS * HEAD_DIM, C_KV_HEADS * HEAD_DIM,
             D_HEADS * 2 * HEAD_DIM, D_HEADS * 2 * HEAD_DIM, D_HEADS * D_V)
EVEN_IN = sum(EVEN_SIZES)
ODD_IN = sum(ODD_SIZES)
MIX_WIDTH = A_Q_HEADS * HEAD_DIM + B_HEADS * B_V
FFN_HIDDEN = -(-8 * D_MODEL // (3 * 256)) * 256
N_EVEN = (DEPTH + 1) // 2
N_ODD = DEPTH // 2


def rms_norm_2(x, g):
    xf = x.astype(jnp.float32)
    y = xf * lax.rsqrt(jnp.mean(xf * xf, axis=-1, keepdims=True) + EPS)
    return (y * g.astype(jnp.float32)).astype(x.dtype)

def split_cols(p, sizes):
    return jnp.split(p, [int(v) for v in np.cumsum(sizes)[:-1]], axis=-1)

def rope_1d(x, pos):
    half = x.shape[-1] // 2
    freqs = ROPE_THETA ** (-jnp.arange(half, dtype=jnp.float32) / half)
    ang = pos.astype(jnp.float32)[:, None] * freqs[None, :]
    ang = ang.reshape((ang.shape[0],) + (1,) * (x.ndim - 3) + (half,))
    cos, sin = jnp.cos(ang), jnp.sin(ang)
    x1 = x[..., :half].astype(jnp.float32)
    x2 = x[..., half:].astype(jnp.float32)
    return jnp.concatenate([x1 * cos - x2 * sin, x2 * cos + x1 * sin], axis=-1).astype(x.dtype)

def rope_2d(x, rows, cols):
    h = x.shape[-1] // 2
    return jnp.concatenate([rope_1d(x[..., :h], rows), rope_1d(x[..., h:], cols)], axis=-1)

def sweep_query_blocks(fn, q):
    B, S = q.shape[:2]
    nb = S // Q_BLOCK
    qb = jnp.moveaxis(q.reshape((B, nb, Q_BLOCK) + q.shape[2:]), 1, 0)
    ob = lax.map(fn, qb)
    return jnp.moveaxis(ob, 0, 1).reshape((B, S) + ob.shape[3:])

def gqa_attend(q, k, v, scale):
    s = jnp.einsum('bqhgd,bkhd->bhgqk', q, k, preferred_element_type=jnp.float32) * scale
    p = jax.nn.softmax(s, axis=-1)
    return jnp.einsum('bhgqk,bkhd->bqhgd', p.astype(v.dtype), v)

def sink_attend(q, k, v, sink):
    Hk, G, d = q.shape[2], q.shape[3], q.shape[4]
    s = jnp.einsum('bqhgd,bkhd->bhgqk', q, k, preferred_element_type=jnp.float32) * d ** -0.5
    sk = jnp.broadcast_to(sink.astype(jnp.float32).reshape(Hk, G, 1, 1), s.shape[:-1] + (1,))
    p = jax.nn.softmax(jnp.concatenate([s, sk], axis=-1), axis=-1)[..., :-1]
    return jnp.einsum('bhgqk,bkhd->bqhgd', p.astype(v.dtype), v)

def windowed_sink_attention(q, k, v, k_ctx, v_ctx, sink):
    B, S, Hk, G, d = q.shape
    nb = S // Q_BLOCK
    L = 3 * Q_BLOCK
    scale = d ** -0.5
    qb = q.reshape(B, nb, Q_BLOCK, Hk, G, d)

    def band(t):
        tb = t.reshape(B, nb, Q_BLOCK, Hk, t.shape[-1])
        tp = jnp.pad(tb, ((0, 0), (1, 1), (0, 0), (0, 0), (0, 0)))
        return jnp.concatenate([tp[:, :-2], tp[:, 1:-1], tp[:, 2:]], axis=2)

    kw, vw = band(k), band(v)
    blk = jnp.arange(nb)[:, None, None]
    q_pos = blk * Q_BLOCK + jnp.arange(Q_BLOCK)[None, :, None]
    k_pos = (blk - 1) * Q_BLOCK + jnp.arange(L)[None, None, :]
    valid = (jnp.abs(q_pos - k_pos) <= WINDOW) & (k_pos >= 0) & (k_pos < S)
    s_loc = jnp.einsum('bnqhgd,bnkhd->bnhgqk', qb, kw, preferred_element_type=jnp.float32) * scale
    s_loc = jnp.where(valid[None, :, None, None, :, :], s_loc, NEG_INF)
    s_ctx = jnp.einsum('bnqhgd,bchd->bnhgqc', qb, k_ctx, preferred_element_type=jnp.float32) * scale
    sk = jnp.broadcast_to(sink.astype(jnp.float32).reshape(Hk, G, 1, 1), s_loc.shape[:-1] + (1,))
    p = jax.nn.softmax(jnp.concatenate([s_loc, s_ctx, sk], axis=-1), axis=-1)
    C = k_ctx.shape[1]
    o = (jnp.einsum('bnhgqk,bnkhd->bnqhgd', p[..., :L].astype(v.dtype), vw)
         + jnp.einsum('bnhgqc,bchd->bnqhgd', p[..., L:L + C].astype(v.dtype), v_ctx))
    return o.reshape(B, S, Hk, G, v.shape[-1])

def diff_attend(q, k, v, lam):
    s = jnp.einsum('bqhid,bkhid->bhiqk', q, k, preferred_element_type=jnp.float32) * q.shape[-1] ** -0.5
    p = jax.nn.softmax(s, axis=-1)
    a = p[:, :, 0] - lam * p[:, :, 1]
    return jnp.einsum('bhqk,bkhd->bqhd', a.astype(v.dtype), v)

def even_project(t, rope, w_in, q_norm, w_uq, kv_norm, w_ukv):
    B, L, _ = t.shape
    qa, ka, va, cq, ckv, kpe = split_cols(t @ w_in, EVEN_SIZES)
    qa = rope(qa.reshape(B, L, A_KV_HEADS, A_GROUP, HEAD_DIM))
    ka = rope(ka.reshape(B, L, A_KV_HEADS, HEAD_DIM))
    va = va.reshape(B, L, A_KV_HEADS, HEAD_DIM)
    qb = (rms_norm_2(cq, q_norm) @ w_uq).reshape(B, L, B_HEADS, B_NOPE + B_ROPE)
    qb = jnp.concatenate([qb[..., :B_NOPE], rope(qb[..., B_NOPE:])], axis=-1)[:, :, :, None, :]
    kvb = (rms_norm_2(ckv, kv_norm) @ w_ukv).reshape(B, L, B_HEADS, B_NOPE + B_V)
    kpe = jnp.broadcast_to(rope(kpe[:, :, None, :]), (B, L, B_HEADS, B_ROPE))
    kb = jnp.concatenate([kvb[..., :B_NOPE], kpe], axis=-1)
    vb = kvb[..., B_NOPE:]
    return qa, ka, va, qb, kb, vb

def mixer_even(h, hc, rows, cols, w_in, sink, q_norm, w_uq, kv_norm, w_ukv, w_out, need_ctx):
    B, S = h.shape[:2]
    qa, ka, va, qb, kb, vb = even_project(h, lambda t: rope_2d(t, rows, cols), w_in, q_norm, w_uq, kv_norm, w_ukv)
    qa_c, ka_c, va_c, qb_c, kb_c, vb_c = even_project(hc, lambda t: t, w_in, q_norm, w_uq, kv_norm, w_ukv)
    scale_b = (B_NOPE + B_ROPE) ** -0.5
    oa = windowed_sink_attention(qa, ka, va, ka_c, va_c, sink)
    kb_all = jnp.concatenate([kb_c, kb], axis=1)
    vb_all = jnp.concatenate([vb_c, vb], axis=1)
    ob = sweep_query_blocks(lambda qq: gqa_attend(qq, kb_all, vb_all, scale_b), qb)
    y = jnp.concatenate([oa.reshape(B, S, -1), ob.reshape(B, S, -1)], axis=-1) @ w_out
    yc = None
    if need_ctx:
        C = hc.shape[1]
        oa_c = sink_attend(qa_c, ka_c, va_c, sink)
        ob_c = gqa_attend(qb_c, kb_c, vb_c, scale_b)
        yc = jnp.concatenate([oa_c.reshape(B, C, -1), ob_c.reshape(B, C, -1)], axis=-1) @ w_out
    return y, yc

def odd_project(t, rope, w_in, qk_norm):
    B, L, _ = t.shape
    qc, kc, vc, qd, kd, vd = split_cols(t @ w_in, ODD_SIZES)
    qc = rope(rms_norm_2(qc.reshape(B, L, C_KV_HEADS, C_GROUP, HEAD_DIM), qk_norm[0]))
    kc = rope(rms_norm_2(kc.reshape(B, L, C_KV_HEADS, HEAD_DIM), qk_norm[1]))
    vc = vc.reshape(B, L, C_KV_HEADS, HEAD_DIM)
    qd = rope(qd.reshape(B, L, D_HEADS, 2, HEAD_DIM))
    kd = rope(kd.reshape(B, L, D_HEADS, 2, HEAD_DIM))
    vd = vd.reshape(B, L, D_HEADS, D_V)
    return qc, kc, vc, qd, kd, vd

def mixer_odd(h, hc, rows, cols, w_in, qk_norm, lam_p, subln, w_out, lam_init, need_ctx):
    B, S = h.shape[:2]
    qc, kc, vc, qd, kd, vd = odd_project(h, lambda t: rope_2d(t, rows, cols), w_in, qk_norm)
    qc_c, kc_c, vc_c, qd_c, kd_c, vd_c = odd_project(hc, lambda t: t, w_in, qk_norm)
    lp = lam_p.astype(jnp.float32)
    lam = jnp.exp(jnp.sum(lp[0] * lp[1])) - jnp.exp(jnp.sum(lp[2] * lp[3])) + lam_init
    scale_c = HEAD_DIM ** -0.5
    kc_all = jnp.concatenate([kc_c, kc], axis=1)
    vc_all = jnp.concatenate([vc_c, vc], axis=1)
    kd_all = jnp.concatenate([kd_c, kd], axis=1)
    vd_all = jnp.concatenate([vd_c, vd], axis=1)
    oc = sweep_query_blocks(lambda qq: gqa_attend(qq, kc_all, vc_all, scale_c), qc)
    od = sweep_query_blocks(lambda qq: diff_attend(qq, kd_all, vd_all, lam), qd)
    od = rms_norm_2(od, subln) * (1.0 - lam_init)
    y = jnp.concatenate([oc.reshape(B, S, -1), od.reshape(B, S, -1)], axis=-1) @ w_out
    yc = None
    if need_ctx:
        C = hc.shape[1]
        oc_c = gqa_attend(qc_c, kc_c, vc_c, scale_c)
        od_c = rms_norm_2(diff_attend(qd_c, kd_c, vd_c, lam), subln) * (1.0 - lam_init)
        yc = jnp.concatenate([oc_c.reshape(B, C, -1), od_c.reshape(B, C, -1)], axis=-1) @ w_out
    return y, yc

def swiglu(h, w_in, w_out):
    g, u = jnp.split(h @ w_in, 2, axis=-1)
    return (jax.nn.silu(g) * u) @ w_out

def diff_lambda_init(layer):
    return 0.8 - 0.6 * math.exp(-0.3 * layer)

def second_inputs(seed: int = 0) -> dict:
    key = jax.random.key(seed)
    ks = jax.random.split(key, 24)
    D = D_MODEL

    def nrm(k, shape, scale):
        return jax.random.normal(k, shape, jnp.float32) * scale

    return {
        "x": nrm(ks[0], (BATCH, SEQ, D), 1.0),
        "c": nrm(ks[1], (BATCH, D), 1.0),
        "ctx": nrm(ks[2], (BATCH, CTX_LEN, D), 1.0),
        "c_ctx": nrm(ks[3], (D,), 1.0),
        "ada_w": nrm(ks[4], (DEPTH, D, 6 * D), 0.5 * D ** -0.5),
        "ada_b": nrm(ks[5], (DEPTH, 6 * D), 0.02),
        "norm_g": 1.0 + nrm(ks[6], (DEPTH, 4, D), 0.1),
        "ffn_w_in": nrm(ks[7], (DEPTH, D, 2 * FFN_HIDDEN), D ** -0.5),
        "ffn_w_out": nrm(ks[8], (DEPTH, FFN_HIDDEN, D), FFN_HIDDEN ** -0.5),
        "ev_w_in": nrm(ks[9], (N_EVEN, D, EVEN_IN), D ** -0.5),
        "ev_sink": nrm(ks[10], (N_EVEN, A_Q_HEADS), 0.5),
        "ev_q_norm": 1.0 + nrm(ks[11], (N_EVEN, B_Q_RANK), 0.1),
        "ev_w_uq": nrm(ks[12], (N_EVEN, B_Q_RANK, B_HEADS * (B_NOPE + B_ROPE)), B_Q_RANK ** -0.5),
        "ev_kv_norm": 1.0 + nrm(ks[13], (N_EVEN, B_KV_RANK), 0.1),
        "ev_w_ukv": nrm(ks[14], (N_EVEN, B_KV_RANK, B_HEADS * (B_NOPE + B_V)), B_KV_RANK ** -0.5),
        "ev_w_out": nrm(ks[15], (N_EVEN, MIX_WIDTH, D), MIX_WIDTH ** -0.5),
        "od_w_in": nrm(ks[16], (N_ODD, D, ODD_IN), D ** -0.5),
        "od_qk_norm": 1.0 + nrm(ks[17], (N_ODD, 2, HEAD_DIM), 0.1),
        "od_lambda": nrm(ks[18], (N_ODD, 4, HEAD_DIM), 0.1),
        "od_subln": 1.0 + nrm(ks[19], (N_ODD, D_V), 0.1),
        "od_w_out": nrm(ks[20], (N_ODD, MIX_WIDTH, D), MIX_WIDTH ** -0.5),
    }

def second_block(x, c, ctx, c_ctx, ada_w, ada_b, norm_g, ffn_w_in, ffn_w_out,
              ev_w_in, ev_sink, ev_q_norm, ev_w_uq, ev_kv_norm, ev_w_ukv, ev_w_out,
              od_w_in, od_qk_norm, od_lambda, od_subln, od_w_out):
    B, S, _ = x.shape
    ROWS = S // GRID_W
    rows = jnp.repeat(jnp.arange(ROWS), GRID_W)
    cols = jnp.tile(jnp.arange(GRID_W), ROWS)
    s_c = jax.nn.silu(c)
    s_cc = jax.nn.silu(c_ctx)
    xc = ctx
    for l in range(DEPTH):
        need_ctx = l < DEPTH - 1
        mod = (s_c @ ada_w[l] + ada_b[l])[:, None, :]
        mod_c = s_cc @ ada_w[l] + ada_b[l]
        sh1, sc1, g1, sh2, sc2, g2 = jnp.split(mod, 6, axis=-1)
        csh1, csc1, cg1, csh2, csc2, cg2 = jnp.split(mod_c, 6, axis=-1)
        h = rms_norm_2(x, norm_g[l, 0]) * (1.0 + sc1) + sh1
        hc = rms_norm_2(xc, norm_g[l, 0]) * (1.0 + csc1) + csh1
        if l % 2 == 0:
            e = l // 2
            y, yc = mixer_even(h, hc, rows, cols, ev_w_in[e], ev_sink[e], ev_q_norm[e], ev_w_uq[e],
                               ev_kv_norm[e], ev_w_ukv[e], ev_w_out[e], need_ctx)
        else:
            o = l // 2
            y, yc = mixer_odd(h, hc, rows, cols, od_w_in[o], od_qk_norm[o], od_lambda[o], od_subln[o],
                              od_w_out[o], diff_lambda_init(l), need_ctx)
        x = x + g1 * rms_norm_2(y, norm_g[l, 1])
        h = rms_norm_2(x, norm_g[l, 2]) * (1.0 + sc2) + sh2
        x = x + g2 * rms_norm_2(swiglu(h, ffn_w_in[l], ffn_w_out[l]), norm_g[l, 3])
        if need_ctx:
            xc = xc + cg1 * rms_norm_2(yc, norm_g[l, 1])
            hc = rms_norm_2(xc, norm_g[l, 2]) * (1.0 + csc2) + csh2
            xc = xc + cg2 * rms_norm_2(swiglu(hc, ffn_w_in[l], ffn_w_out[l]), norm_g[l, 3])
    return x


def setup_inputs(seed=0):
    out = dict(first_inputs(seed))
    for name, value in second_inputs(seed + 1).items():
        if name != "x":
            out[name + "_2"] = value
    return out


def reference(
    x, c, positions, w_mod, b_mod, pre_norm_gain, post_norm_gain, w_in, attn_sinks, gla_gate_w,
    gla_gate_b, gla_norm_gain, w_out, c_2, ctx_2, c_ctx_2, ada_w_2, ada_b_2, norm_g_2,
    ffn_w_in_2, ffn_w_out_2, ev_w_in_2, ev_sink_2, ev_q_norm_2, ev_w_uq_2, ev_kv_norm_2,
    ev_w_ukv_2, ev_w_out_2, od_w_in_2, od_qk_norm_2, od_lambda_2, od_subln_2, od_w_out_2,
):
    x = first_block(
        x, c, positions, w_mod, b_mod, pre_norm_gain, post_norm_gain, w_in, attn_sinks,
        gla_gate_w, gla_gate_b, gla_norm_gain, w_out,
    )
    return second_block(
        x, c_2, ctx_2, c_ctx_2, ada_w_2, ada_b_2, norm_g_2, ffn_w_in_2, ffn_w_out_2, ev_w_in_2,
        ev_sink_2, ev_q_norm_2, ev_w_uq_2, ev_kv_norm_2, ev_w_ukv_2, ev_w_out_2, od_w_in_2,
        od_qk_norm_2, od_lambda_2, od_subln_2, od_w_out_2,
    )


_drawn_inputs = setup_inputs


def setup_inputs(seed=0):
    import zlib

    import numpy as np

    out = dict(_drawn_inputs(seed))
    spreads = {}
    factors = {'b_mod': 2.86,
     'pre_norm_gain': 3.553,
     'post_norm_gain': 6.371,
     'attn_sinks': 8.0,
     'gla_gate_b': 8.0,
     'gla_norm_gain': 8.0,
     'ev_sink_2': 8.0,
     'ev_q_norm_2': 6.237,
     'od_qk_norm_2': 8.0,
     'od_lambda_2': 8.0,
     'od_subln_2': 2.746}
    for name, (base, spread) in spreads.items():
        noise = np.random.default_rng([zlib.crc32(name.encode()), seed]).standard_normal(out[name].shape)
        drawn = base * np.exp(spread * noise) if base else spread * noise
        out[name] = __import__('jax').numpy.asarray(drawn.astype(out[name].dtype))
    for name, factor in factors.items():
        out[name] = (out[name] * factor).astype(out[name].dtype)
    return out
```

```python
from contextlib import ExitStack
import math

import numpy as np

import concourse.bass as bass
from concourse import mybir

F32 = mybir.dt.float32
F32R = mybir.dt.float32r
BF16 = mybir.dt.bfloat16
I32 = mybir.dt.int32
U32 = mybir.dt.uint32
ALU = mybir.AluOpType
ACT = mybir.ActivationFunctionType
AX = mybir.AxisListType.X

P = 128
D = 1024
KT = D // P
S = 512
CTX = 256
XT = S // P
CT = CTX // P
TOK = S + CTX
DEPTH = 2
EPS = 1e-6
NEG = -1e30
HALF = 512

AQ, AK, AV, AG = 0, 512, 640, 768
RQ, RK, RV, RG = 1280, 1536, 1792, 2048
GQ, GK, GV, GG, GA = 2304, 2432, 2560, 2816, 3072
IN1 = 3088
GLA_C = 64
GATE_NORM = 16.0
LEVELS = (32, 16, 8, 4, 2, 1)

EV_IN, OD_IN = 1184, 2304
FFN = 2816
LAM_INIT = 0.8 - 0.6 * math.exp(-0.3)

def _layout(widths):
    at, cols = 0, {}
    for name, n in widths:
        cols[name] = (at, at + n)
        at += n
    return cols, at


STATIC_COLS, STATIC_W = _layout([("ident", P), ("blockrows", 2 * P)])
ONE_COLS, ONE_W = _layout([
    ("window", 2 * P), ("tri", P), ("levels", 7 * P), ("rdecay", 4 * P), ("rqdecay", 2 * P),
    ("rkdecay", 4), ("rchunk", 2), ("rblock", P), ("gblock", 2 * P), ("freqs", 2 * 64)])
TWO_COLS, TWO_W = _layout([("window", 2 * P), ("cos64", 4 * 64), ("sin64", 4 * 64), ("cos32", 4 * 32),
                           ("sin32", 4 * 32)])


def static_constants():
    t = np.zeros((P, STATIC_W), np.float32)
    t[:, slice(*STATIC_COLS["ident"])] = np.eye(P)
    rows = np.zeros((P, 2, P), np.float32)
    rows[0, 0], rows[1, 1] = 1.0, 1.0
    t[:, slice(*STATIC_COLS["blockrows"])] = rows.reshape(P, -1)
    return t


def block_one_constants():
    t = np.zeros((P, ONE_W), np.float32)
    put = lambda name, v: t.__setitem__((slice(None), slice(*ONE_COLS[name])), np.asarray(v).reshape(P, -1))
    i, j = np.arange(P)[:, None], np.arange(P)[None, :]
    put("window", np.concatenate([np.where(j > i, 0, NEG), np.where(j <= i, 0, NEG)], 1))
    src, dst = np.arange(P)[:, None], np.arange(P)[None, :]
    put("tri", (src <= dst) & (src // GLA_C == dst // GLA_C))
    lv = [(src // (2 * s) == dst // (2 * s)) & (src % (2 * s) < s) & (dst % (2 * s) >= s) for s in LEVELS]
    put("levels", np.stack(lv + [src == dst], 1).astype(np.float32))
    log_g = np.log(1.0 - 2.0 ** (-5.0 - np.arange(4)))
    diff = dst - src
    dm = np.where(diff >= 0, np.exp(log_g[:, None, None] * np.maximum(diff, 0)), 0.0) * 64 ** -0.5
    put("rdecay", np.stack([dm[0], dm[2], dm[1], dm[3]], 1))
    part = np.arange(P)[:, None] // 64
    qd = [np.exp(log_g[2 * pair + part] * (np.arange(P)[None, :] + 1.0)) for pair in range(2)]
    put("rqdecay", np.stack(qd, 1))
    put("rkdecay", np.exp(log_g[None, :] * (P - 1.0 - np.arange(P)[:, None])) * 64 ** -0.5)
    put("rchunk", np.concatenate([np.exp(log_g[2 * pair + part] * P) for pair in range(2)], 1))
    put("rblock", src // 64 == dst // 64)
    put("gblock", src // 32 == np.arange(2 * P)[None, :] // 64)
    rope = (np.float32(10000.0) ** (-np.arange(0, 64, 2, dtype=np.float32) / np.float32(64))).astype(np.float32)
    ret = (1.0 / (np.float32(10000.0) ** np.linspace(0.0, 1.0, 32, dtype=np.float32))).astype(np.float32)
    put("freqs", np.tile(np.concatenate([rope, rope, ret, ret])[None], (P, 1)))
    return t


def block_two_constants():
    t = np.zeros((P, TWO_W), np.float32)
    put = lambda name, v: t.__setitem__((slice(None), slice(*TWO_COLS[name])), np.asarray(v).reshape(P, -1))
    i, j = np.arange(P)[:, None], np.arange(P)[None, :]
    put("window", np.concatenate([np.where(j >= i, 0, NEG), np.where(j <= i, 0, NEG)], 1))
    tok = np.arange(S)
    for width in (64, 32):
        half = width // 4
        fr = (np.float32(10000.0) ** (-np.arange(half, dtype=np.float32) / np.float32(half))).astype(np.float32)
        cos, sin = [], []
        for pos in (tok // 64, tok % 64):
            a = pos.astype(np.float32)[:, None] * fr[None]
            cos += [np.cos(a), np.cos(a)]
            sin += [-np.sin(a), np.sin(a)]
        for name, parts in (("cos", cos), ("sin", sin)):
            full = np.concatenate(parts, 1).reshape(XT, P, width).transpose(1, 0, 2)
            put(f"{name}{width}", full)
    return t


class Signal:

    def __init__(self, sem):
        self.sem, self.planned = sem, 0

    def plan(self, n):
        before = self.planned
        self.planned += n
        return before


class Steps:

    def __init__(self, eng, sem):
        self.eng, self.sem, self.n = eng, sem, 0

    def mark(self, ins):
        self.n += 1
        ins.then_inc(self.sem, 1)
        return self.n

    def chain(self, ins):
        self.eng.wait_ge(self.sem, self.mark(ins))


def build(nc, a, out, stop=None):
    with ExitStack() as ctx:
        base = (nc.sbuf_base + 31) // 32 * 32
        room = nc.sbuf_usable_end - base
        place = [0]

        def at(name, shape, dt, offset):
            assert offset + int(np.prod(shape[1:])) * mybir.dt.size(dt) <= room, (name, offset)
            return nc.alloc_sbuf_tensor_at(name, shape, dt, offset=base + offset)

        def static(name, shape, dt=F32):
            t = at(name, shape, dt, place[0])
            place[0] += (int(np.prod(shape[1:])) * mybir.dt.size(dt) + 31) // 32 * 32
            return t

        def region(start):
            where = [start]

            def take(name, shape, dt=F32):
                t = at(name, shape, dt, where[0])
                where[0] += (int(np.prod(shape[1:])) * mybir.dt.size(dt) + 31) // 32 * 32
                return t
            take.where = where
            return take

        def signal(name):
            return Signal(ctx.enter_context(nc.semaphore(name)))

        ps = ctx.enter_context(nc.psum_tensor("ps", [P, 8, HALF], F32))

        X = static("x_tokens", [P, XT + CT, D])
        ht_at = place[0]
        HT = static("h_transposed", [P, 2, KT, TOK], F32R)
        ht_end = place[0]
        w_raw = static("w_raw", [P, 4, 1024])
        w_hi = static("w_hi", [P, 2, 1024], F32R)
        w_lo = static("w_lo", [P, 2, 1024], F32R)
        mod_raw_at = place[0]
        mod_raw = static("mod_raw", [P, 3, 2, HALF])
        con = static("static_constants", [P, STATIC_W])
        gate_rows_at = place[0]
        gate_rows = static("gate_rows", [P, 4, D])
        mod_cols = static("mod_columns", [P, 4, KT, 2])
        c_raw = static("c_raw", [P, 3, KT])
        c_act = static("c_act", [P, 2, KT, 2])
        mod_bias = static("mod_bias", [2, HALF])
        mod_gain = static("mod_gain", [2, HALF])
        mod_row = static("mod_row", [2, HALF])
        sumsq = static("sumsq", [P, 8])
        meansq = static("meansq", [P, 8])
        rstd = static("rstd", [P, 32])
        minus_half = static("minus_half", [P, 32])
        identb = static("ident_bf16", [P, P], BF16)
        window = static("window_bf16", [P, 2 * P], BF16)
        small_at, SMALL = place[0], 5440
        arena = small_at + SMALL
        ident = con[:, slice(*STATIC_COLS["ident"])]
        blockrows = con[:, slice(*STATIC_COLS["blockrows"])].rearrange("p (r n) -> p r n", r=2)

        take = region(arena)
        xn = take("x_normed", [P, XT + CT, D])
        junk = take("square_junk", [P, D])
        h_full = take("h_full", [P, 2, HALF])
        take = region(arena)
        Y = take("y_tokens", [P, XT + CT, D])
        act_t = take("ffn_hidden", [P, 2, 6, TOK], F32R)
        res_junk = at("residual_junk", [P, D], F32, arena + (XT + CT) * D * 4)

        dve_s = act_s = pool_s = None

        load_in = signal("inputs_landed")
        w_landed = [signal(f"w_landed{i}") for i in range(4)]
        w_hi_ready, w_lo_ready, w_used = signal("w_hi_ready"), signal("w_lo_ready"), signal("w_used")
        phase_done = signal("phase_done")
        out_landed = signal("out_landed")
        dve_step, act_step, pool_step = signal("dve_step"), signal("act_step"), signal("pool_step")
        units_done = {"sp": 0, "act": 0, "pool": 0, "pe": 0}
        phases_done = {"pe": 0, "act": 0, "dve": 0, "pool": 0}

        def phase_end(eng, name):
            phases_done[name] += 1
            eng.drain().then_inc(phase_done.sem, 1)
            eng.wait_ge(phase_done.sem, 4 * phases_done[name])

        def sp_waits_phase(sp, n):
            sp.wait_ge(phase_done.sem, 4 * n)

        def weights_load(sp, src, k, n):
            u = units_done["sp"]
            units_done["sp"] += 1
            if u >= 4:
                sp.wait_ge(w_lo_ready.sem, u - 3)
            dst = w_raw[:, u % 4, 0:k * n].rearrange("p (k n) -> p k n", k=k)
            sp.dma_start(dst, src.rearrange("(k p) n -> p k n", p=P)).then_inc(w_landed[u % 4].sem, 16)

        def weights_high(act, k, n):
            u = units_done["act"]
            units_done["act"] += 1
            act.wait_ge(w_landed[u % 4].sem, 16 * (u // 4 + 1))
            if u >= 2:
                act.wait_ge(w_used.sem, u - 1)
            act.activation(w_hi[:, u % 2, 0:k * n], w_raw[:, u % 4, 0:k * n], ACT.Copy).then_inc(w_hi_ready.sem, 1)

        def weights_low(pool, k, n):
            u = units_done["pool"]
            units_done["pool"] += 1
            pool.wait_ge(w_hi_ready.sem, u + 1)
            pool.tensor_tensor(w_lo[:, u % 2, 0:k * n], w_raw[:, u % 4, 0:k * n],
                               w_hi[:, u % 2, 0:k * n].bitcast(F32), ALU.subtract).then_inc(w_lo_ready.sem, 1)

        def weights_use(pe, k, n):
            u = units_done["pe"]
            units_done["pe"] += 1
            pe.wait_ge(w_lo_ready.sem, u + 1)
            return [w[:, u % 2, 0:k * n].rearrange("p (k n) -> p k n", k=k) for w in (w_hi, w_lo)]

        def matmul3(pe, acc, left, right, start, stop):
            pe.matmul(acc, left[0], right[0], start=start, stop=False)
            pe.matmul(acc, left[0], right[1], start=False, stop=False)
            return pe.matmul(acc, left[1], right[0], start=False, stop=stop)

        mod_landed = [signal(f"mod_landed{i}") for i in range(3)]
        mod_side = signal("mod_side")
        mod_unit, mod_rowed, mod_turned, mod_kept = (signal(n) for n in ("mod_unit", "mod_rowed", "mod_turned", "mod_kept"))

        class Modulation:

            def __init__(self, w, bias, vectors, cond):
                self.w, self.bias, self.vectors, self.cond = w, bias, vectors, cond
                self.chunks = [(kind, gain, slot, half) for kind, gain, slot in vectors for half in range(2)]
                self.u0 = mod_unit.plan(4 * len(self.chunks))
                self.k0 = mod_rowed.plan(len(self.chunks))
                mod_turned.plan(len(self.chunks))
                mod_kept.plan(len(self.chunks))
                self.side = []
                for n, (kind, gain, slot, half) in enumerate(self.chunks):
                    landing = 16 + 16 * (gain is not None)
                    self.side.append(mod_side.plan(landing) + landing)

            def sync(self, sp):
                for n, (kind, gain, slot, half) in enumerate(self.chunks):
                    k = self.k0 + n
                    cols = slice(n * HALF, (n + 1) * HALF)
                    if k >= 1:
                        sp.wait_ge(mod_rowed.sem, k)
                    sp.dma_start(mod_bias[:, :], self.bias[cols].partition_broadcast(2)).then_inc(mod_side.sem, 16)
                    if gain is not None:
                        sp.dma_start(mod_gain[:, :], gain[half * HALF:(half + 1) * HALF].partition_broadcast(2)).then_inc(mod_side.sem, 16)
                    for q in range(4):
                        u = self.u0 + 4 * n + q
                        if u >= 3:
                            sp.wait_ge(mod_unit.sem, u - 2)
                        sp.dma_start(mod_raw[:, u % 3], self.w[q * 256:(q + 1) * 256, cols].rearrange("(k p) n -> p k n", p=P))\
                          .then_inc(mod_landed[u % 3].sem, 16)

            def turn(self, pe, n):
                kind, gain, slot, half = self.chunks[n]
                k = self.k0 + n
                pe.wait_ge(mod_rowed.sem, k + 1)
                if k >= 2:
                    pe.wait_ge(mod_kept.sem, k - 1)
                b = 2 * (k % 2)
                if kind != "gate":
                    for j in range(4):
                        ins = pe.matmul(ps[:, b, 2 * j:2 * j + 2], mod_row[:, j * P:(j + 1) * P], ident[0:2, 0:2],
                                        start=True, stop=True)
                else:
                    for r, g in enumerate(slot):
                        ins = pe.matmul(ps[:, b + r, :], blockrows[0:2, r, :], mod_row[:, :], start=True, stop=True)
                ins.then_inc(mod_turned.sem, 1)

            def tensor(self, pe):
                for n in range(len(self.chunks)):
                    k = self.k0 + n
                    if k >= 2:
                        pe.wait_ge(mod_rowed.sem, k - 1)
                    for q in range(4):
                        u = self.u0 + 4 * n + q
                        pe.wait_ge(mod_landed[u % 3].sem, 16 * (u // 3 + 1))
                        for j in range(2):
                            ins = pe.matmul(ps[0:2, 6 + k % 2, :], c_act[:, self.cond, 2 * q + j, :], mod_raw[:, u % 3, j, :],
                                            start=(q == 0 and j == 0), stop=(q == 3 and j == 1))
                        ins.then_inc(mod_unit.sem, 1)
                    if n >= 1:
                        self.turn(pe, n - 1)
                self.turn(pe, len(self.chunks) - 1)

            def vector(self, dve):
                for n, (kind, gain, slot, half) in enumerate(self.chunks):
                    k = self.k0 + n
                    dve.wait_ge(mod_unit.sem, self.u0 + 4 * n + 4)
                    dve.wait_ge(mod_side.sem, self.side[n])
                    if k >= 1:
                        dve.wait_ge(mod_turned.sem, k)
                    row = mod_row[:, :]
                    ins = dve.tensor_tensor(row, ps[0:2, 6 + k % 2, :], mod_bias[:, :], ALU.add)
                    if kind == "scale":
                        dve_s.chain(ins)
                        ins = dve.scalar_tensor_tensor(out=row, in0=row, scalar=1.0, in1=mod_gain[:, :], op0=ALU.add, op1=ALU.mult)
                    elif kind == "gate":
                        dve_s.chain(ins)
                        ins = dve.tensor_tensor(row, row, mod_gain[:, :], ALU.mult)
                    ins.then_inc(mod_rowed.sem, 1)

            def scalar(self, act):
                for n, (kind, gain, slot, half) in enumerate(self.chunks):
                    k = self.k0 + n
                    act.wait_ge(mod_turned.sem, k + 1)
                    b = 2 * (k % 2)
                    if kind != "gate":
                        ins = act.activation(mod_cols[:, slot, 4 * half:4 * half + 4, :],
                                             ps[:, b, 0:8].rearrange("p (j r) -> p j r", r=2), ACT.Copy)
                    else:
                        for r, g in enumerate(slot):
                            ins = act.activation(gate_rows[:, g, half * HALF:(half + 1) * HALF], ps[:, b + r, :], ACT.Copy)
                    ins.then_inc(mod_kept.sem, 1)

            def gpsimd(self, pool):
                pass

        sq_ready, ms_ready, rstd_ready, xn_ready = (signal(n) for n in ("squares_ready", "meansq_ready", "rstd_ready", "xn_ready"))
        ht_turned, ht_high, ht_full, ht_low = (signal(n) for n in ("ht_turned", "ht_high", "ht_full", "ht_low"))

        class NormTransposed:
            def __init__(self, with_ctx, shift, scale):
                self.T = XT + (CT if with_ctx else 0)
                self.shift, self.scale = shift, scale
                self.q0, self.m0, self.r0 = sq_ready.plan(self.T), ms_ready.plan(1), rstd_ready.plan(1)
                self.x0 = xn_ready.plan(self.T)
                self.groups = [(kt, 0, range(0, XT)) for kt in range(KT)]
                if with_ctx:
                    self.groups += [(kt, 1, range(XT, XT + CT)) for kt in range(KT)]
                self.g0 = ht_turned.plan(len(self.groups))
                for s in (ht_high, ht_low):
                    s.plan(len(self.groups))
                self.f0 = ht_full.plan(len(self.groups))

            def scalar(self, act):
                for t in range(self.T):
                    if t:
                        act.wait_ge(sq_ready.sem, self.q0 + t)
                    act.activation(junk[:, :], X[:, t, :], ACT.Square, accum_out=sumsq[:, t:t + 1]).then_inc(sq_ready.sem, 1)
                for g, (kt, r, tiles) in enumerate(self.groups):
                    n = len(tiles) * P
                    act.wait_ge(ht_full.sem, self.f0 + g + 1)
                    act.activation(HT[:, 0, kt, tiles[0] * P:tiles[0] * P + n], h_full[:, g % 2, 0:n], ACT.Copy).then_inc(ht_high.sem, 1)

            def vector(self, dve):
                dve.wait_ge(sq_ready.sem, self.q0 + self.T)
                dve.tensor_scalar(meansq[:, 0:self.T], sumsq[:, 0:self.T], 1.0 / D, EPS, ALU.mult, ALU.add).then_inc(ms_ready.sem, 1)
                dve.wait_ge(rstd_ready.sem, self.r0 + 1)
                for t in range(self.T):
                    dve.tensor_scalar(xn[:, t, :], X[:, t, :], rstd[:, t:t + 1], None, ALU.mult).then_inc(xn_ready.sem, 1)
                for g, (kt, r, tiles) in enumerate(self.groups):
                    n = len(tiles) * P
                    dve.wait_ge(ht_turned.sem, self.g0 + g + 1)
                    if g >= 2:
                        dve.wait_ge(ht_low.sem, self.g0 + g - 1)
                    dve.tensor_scalar(h_full[:, g % 2, 0:n], ps[:, g % 8, 0:n], mod_cols[:, self.scale, kt, r:r + 1],
                                      mod_cols[:, self.shift, kt, r:r + 1], ALU.mult, ALU.add).then_inc(ht_full.sem, 1)

            def gpsimd(self, pool):
                pool.wait_ge(ms_ready.sem, self.m0 + 1)
                pool.tensor_tensor(rstd[:, 0:self.T], meansq[:, 0:self.T], minus_half[:, 0:self.T], ALU.pow).then_inc(rstd_ready.sem, 1)
                for g, (kt, r, tiles) in enumerate(self.groups):
                    n = len(tiles) * P
                    hi = HT[:, 0, kt, tiles[0] * P:tiles[0] * P + n]
                    pool.wait_ge(ht_full.sem, self.f0 + g + 1)
                    pool.wait_ge(ht_high.sem, self.g0 + g + 1)
                    pool.tensor_tensor(HT[:, 1, kt, tiles[0] * P:tiles[0] * P + n], h_full[:, g % 2, 0:n], hi.bitcast(F32),
                                       ALU.subtract).then_inc(ht_low.sem, 1)

            def tensor(self, pe):
                for g, (kt, r, tiles) in enumerate(self.groups):
                    if g >= 8:
                        pe.wait_ge(ht_full.sem, self.f0 + g - 7)
                    for i, t in enumerate(tiles):
                        if kt == 0:
                            pe.wait_ge(xn_ready.sem, self.x0 + t + 1)
                        ins = pe.transpose(ps[:, g % 8, i * P:(i + 1) * P], xn[:, t, kt * P:(kt + 1) * P], ident)
                    ins.then_inc(ht_turned.sem, 1)

            def sync(self, sp):
                pass

        class MixTransposed:
            def __init__(self, src, tiles):
                self.src = src
                self.groups = [(kt, range(0, XT)) for kt in range(KT)]
                if tiles > XT:
                    self.groups += [(kt, range(XT, tiles)) for kt in range(KT)]
                self.g0 = ht_turned.plan(len(self.groups))
                for s in (ht_high, ht_low):
                    s.plan(len(self.groups))

            def tensor(self, pe):
                for g, (kt, tiles) in enumerate(self.groups):
                    if g >= 8:
                        pe.wait_ge(ht_low.sem, self.g0 + g - 7)
                    for i, t in enumerate(tiles):
                        ins = pe.transpose(ps[:, g % 8, i * P:(i + 1) * P], self.src(t, kt), ident)
                    ins.then_inc(ht_turned.sem, 1)

            def scalar(self, act):
                for g, (kt, tiles) in enumerate(self.groups):
                    n = len(tiles) * P
                    act.wait_ge(ht_turned.sem, self.g0 + g + 1)
                    act.activation(HT[:, 0, kt, tiles[0] * P:tiles[0] * P + n], ps[:, g % 8, 0:n], ACT.Copy).then_inc(ht_high.sem, 1)

            def vector(self, dve):
                for g, (kt, tiles) in enumerate(self.groups):
                    n = len(tiles) * P
                    dve.wait_ge(ht_high.sem, self.g0 + g + 1)
                    dve.tensor_tensor(HT[:, 1, kt, tiles[0] * P:tiles[0] * P + n], ps[:, g % 8, 0:n],
                                      HT[:, 0, kt, tiles[0] * P:tiles[0] * P + n].bitcast(F32), ALU.subtract).then_inc(ht_low.sem, 1)

            def gpsimd(self, pool):
                pass

            def sync(self, sp):
                pass

        acc_ready, acc_free = signal("acc_ready"), signal("acc_free")

        class Linear:

            def __init__(self, w, chunks, dst):
                self.w, self.chunks, self.dst = w, chunks, dst
                self.a0 = acc_ready.plan(sum(len(t) - 1 for _, _, t in chunks))
                self.f0 = acc_free.plan(sum(len(t) for _, _, t in chunks))
                self.w0 = w_used.plan(4 * len(chunks))

            def sync(self, sp):
                for c0, n, tiles in self.chunks:
                    for q in range(4):
                        weights_load(sp, self.w[q * 256:(q + 1) * 256, c0:c0 + n], 2, n)

            def scalar(self, act):
                for c0, n, tiles in self.chunks:
                    for q in range(4):
                        weights_high(act, 2, n)

            def gpsimd(self, pool):
                for c0, n, tiles in self.chunks:
                    for q in range(4):
                        weights_low(pool, 2, n)

            def tensor(self, pe):
                last, i = {}, 0
                for c0, n, tiles in self.chunks:
                    for q in range(4):
                        w = weights_use(pe, 2, n)
                        for t in tiles:
                            if q == 0 and t in last:
                                pe.wait_ge(acc_free.sem, self.f0 + last[t] + 1)
                            for j in range(2):
                                kt = 2 * q + j
                                ins = matmul3(pe, ps[:, t, 0:n], [HT[:, s, kt, t * P:(t + 1) * P] for s in range(2)],
                                              [w[s][:, j, :] for s in range(2)], start=(kt == 0), stop=(kt == KT - 1))
                            if q == 3:
                                last[t] = i
                                i += 1
                                if t != tiles[-1]:
                                    ins.then_inc(acc_ready.sem, 1)
                        ins.then_inc(w_used.sem, 1)

            def vector(self, dve):
                i = 0
                for c, (c0, n, tiles) in enumerate(self.chunks):
                    for t in tiles:
                        if t != tiles[-1]:
                            i += 1
                            dve.wait_ge(acc_ready.sem, self.a0 + i)
                        else:
                            dve.wait_ge(w_used.sem, self.w0 + 4 * (c + 1))
                        dve.tensor_copy(self.dst(t, c0, n), ps[:, t, 0:n]).then_inc(acc_free.sem, 1)

        y_gated = signal("y_gated")

        class Residual:
            def __init__(self, gates):
                self.gates, self.T = gates, len(gates)
                self.q0, self.m0, self.r0 = sq_ready.plan(self.T), ms_ready.plan(1), rstd_ready.plan(1)
                self.y0 = y_gated.plan(self.T)

            def scalar(self, act):
                for t in range(self.T):
                    if t:
                        act.wait_ge(sq_ready.sem, self.q0 + t)
                    act.activation(res_junk[:, :], Y[:, t, :], ACT.Square, accum_out=sumsq[:, t:t + 1]).then_inc(sq_ready.sem, 1)

            def gpsimd(self, pool):
                pool.wait_ge(ms_ready.sem, self.m0 + 1)
                pool.tensor_tensor(rstd[:, 0:self.T], meansq[:, 0:self.T], minus_half[:, 0:self.T], ALU.pow).then_inc(rstd_ready.sem, 1)
                for t in range(1, self.T, 3):
                    pool.wait_ge(y_gated.sem, self.y0 + t + 1)
                    pool.tensor_tensor(X[:, t, :], X[:, t, :], Y[:, t, :], ALU.add)

            def vector(self, dve):
                dve.wait_ge(sq_ready.sem, self.q0 + self.T)
                dve.tensor_scalar(meansq[:, 0:self.T], sumsq[:, 0:self.T], 1.0 / D, EPS, ALU.mult, ALU.add).then_inc(ms_ready.sem, 1)
                dve.wait_ge(rstd_ready.sem, self.r0 + 1)
                for t, g in enumerate(self.gates):
                    dve.scalar_tensor_tensor(out=Y[:, t, :], in0=Y[:, t, :], scalar=rstd[:, t:t + 1], in1=gate_rows[:, g, :],
                                             op0=ALU.mult, op1=ALU.mult).then_inc(y_gated.sem, 1)
                for t in range(self.T):
                    if t % 3 != 1:
                        dve.wait_ge(y_gated.sem, self.y0 + t + 1)
                        dve.tensor_tensor(X[:, t, :], X[:, t, :], Y[:, t, :], ALU.add)

            def tensor(self, pe):
                pass

            def sync(self, sp):
                pass

        s_scored, s_max, s_exp, s_turned, s_kept_a, s_kept_v, s_summed, s_out = (signal("att_" + n) for n in (
            "scored", "max", "exp", "turned", "kept_act", "kept_dve", "summed", "out"))

        class Attention:

            def __init__(self, units, probs, probs_t, stats, neg_sinks=None, sinks=None, neg_lambda=None):
                self.units, self.probs, self.probs_t, self.stats = units, probs, probs_t, stats
                self.neg_sinks, self.sinks, self.neg_lambda = neg_sinks, sinks, neg_lambda
                n = len(units)
                self.b = {s: s.plan(n) for s in (s_scored, s_max, s_exp, s_turned, s_summed, s_out)}
                self.ka = s_kept_a.plan((n + 1) // 2)
                self.kv = s_kept_v.plan(n // 2)

            def wait(self, eng, s, count):
                if count > 0:
                    eng.wait_ge(s.sem, self.b[s] + count)

            def wait_kept(self, eng, u):
                if u >= 0:
                    s, before = ((s_kept_a, self.ka), (s_kept_v, self.kv))[u % 2]
                    eng.wait_ge(s.sem, before + u // 2 + 1)

            def scores(self, u):
                return ps[:, 2 * (u % 2):2 * (u % 2) + 2, :].rearrange("p b n -> p (b n)")

            def tensor(self, pe):
                n = len(self.units)
                for step in range(n + 3):
                    u = step
                    if u < n:
                        un, sc = self.units[u], self.scores(u)
                        self.wait(pe, s_exp, u - 1)
                        for bank in range(2):
                            parts = [(k, c) for k, c in un["keys"] if c // HALF == bank]
                            masks = [(m, c) for m, c in un["mask"] if c // HALF == bank]
                            for i, (k, c) in enumerate(parts):
                                mk = [m for m, mc in masks if mc == c]
                                ins = pe.matmul(sc[:, c:c + k.shape[1]], un["q"], k, start=True, stop=not mk)
                                if mk:
                                    ins = pe.matmul(sc[:, c:c + P], identb[:, :], mk[0], start=False, stop=True)
                        ins.then_inc(s_scored.sem, 1)
                    u = step - 2
                    if 0 <= u < n:
                        blocks = len(self.units[u]["values"])
                        self.wait(pe, s_exp, u + 1)
                        self.wait_kept(pe, u - 1)
                        for b in range(blocks):
                            ins = pe.transpose(ps[:, 4 + b // 4, (b % 4) * P:(b % 4 + 1) * P],
                                               self.probs[:, u % 2, b * P:(b + 1) * P], ident)
                        ins.then_inc(s_turned.sem, 1)
                    u = step - 3
                    if 0 <= u < n:
                        vals = self.units[u]["values"]
                        self.wait_kept(pe, u)
                        self.wait(pe, s_out, u - 1)
                        for b, v in enumerate(vals):
                            ins = pe.matmul(ps[:, 6 + u % 2, 0:v.shape[1]], self.probs_t[:, u % 2, b * P:(b + 1) * P], v,
                                            start=(b == 0), stop=(b == len(vals) - 1))
                        ins.then_inc(s_summed.sem, 1)

            def copy_probs(self, eng, act, u, sig):
                w = len(self.units[u]["values"]) * P
                eng.wait_ge(s_turned.sem, self.b[s_turned] + u + 1)
                self.wait(eng, s_summed, u - 1)
                src = ps[:, 4:6, :].rearrange("p b n -> p (b n)")[:, 0:w]
                dst = self.probs_t[:, u % 2, 0:w]
                (eng.activation(dst, src, ACT.Copy) if act else eng.tensor_copy(dst, src)).then_inc(sig.sem, 1)

            def scalar(self, act):
                n, st = len(self.units), self.stats
                for step in range(n + 2):
                    u = step
                    if u < n:
                        un = self.units[u]
                        w, r = len(un["values"]) * P, u % 4
                        act.wait_ge(s_max.sem, self.b[s_max] + u + 1)
                        self.wait(act, s_turned, u - 1)
                        if u >= 4:
                            self.wait(act, s_out, u - 3)
                        ins = act.activation(self.probs[:, u % 2, 0:w], self.scores(u)[:, 0:w], ACT.Exp, bias=st[:, 1, r:r + 1],
                                             scale=un["scale"], accum_out=st[:, 2, r:r + 1])
                        if un["sink"] is not None:
                            h = un["sink"]
                            ins = act.activation(st[:, 3, r:r + 1], st[:, 1, r:r + 1], ACT.Exp, bias=self.sinks[:, h:h + 1])
                        ins.then_inc(s_exp.sem, 1)
                    u = step - 2
                    if 0 <= u < n and u % 2 == 0:
                        self.copy_probs(act, True, u, s_kept_a)

            def vector(self, dve):
                n, st = len(self.units), self.stats
                for step in range(n + 3):
                    u = step
                    if u < n:
                        un = self.units[u]
                        w, r = len(un["values"]) * P, u % 4
                        dve.wait_ge(s_scored.sem, self.b[s_scored] + u + 1)
                        dve_s.chain(dve.tensor_reduce(st[:, 0, r:r + 1], self.scores(u)[:, 0:w], AX, ALU.max))
                        if un["sink"] is not None:
                            h = un["sink"]
                            ins = dve.tensor_scalar(st[:, 1, r:r + 1], st[:, 0, r:r + 1], -un["scale"], self.neg_sinks[:, h:h + 1],
                                                    ALU.mult, ALU.min)
                        else:
                            ins = dve.tensor_scalar(st[:, 1, r:r + 1], st[:, 0, r:r + 1], -un["scale"], None, ALU.mult)
                        ins.then_inc(s_max.sem, 1)
                    u = step - 2
                    if 0 <= u < n and u % 2 == 1:
                        self.copy_probs(dve, False, u, s_kept_v)
                    u = step - 3
                    if 0 <= u < n:
                        un = self.units[u]
                        r, dv = u % 4, un["values"][0].shape[1]
                        total, inv = st[:, 2, r:r + 1], st[:, 5, r:r + 1]
                        dve.wait_ge(s_exp.sem, self.b[s_exp] + u + 1)
                        if un["sink"] is not None:
                            dve_s.chain(dve.tensor_tensor(st[:, 4, r:r + 1], total, st[:, 3, r:r + 1], ALU.add))
                            total = st[:, 4, r:r + 1]
                        dve_s.chain(dve.reciprocal(inv, total))
                        kind, dst, other = un["finish"]
                        if kind == "minus_lambda":
                            dve_s.chain(dve.tensor_tensor(st[:, 6, r:r + 1], inv, self.neg_lambda, ALU.mult))
                            inv = st[:, 6, r:r + 1]
                        dve.wait_ge(s_summed.sem, self.b[s_summed] + u + 1)
                        o = ps[:, 6 + u % 2, 0:dv]
                        if kind == "plain":
                            ins = dve.tensor_scalar(dst, o, inv, None, ALU.mult)
                        else:
                            op = ALU.mult if kind == "gated" else ALU.add
                            if kind == "minus_lambda":
                                dve.wait_ge(s_out.sem, self.b[s_out] + u)
                            ins = dve.scalar_tensor_tensor(out=dst, in0=o, scalar=inv, in1=other, op0=ALU.mult, op1=op)
                        ins.then_inc(s_out.sem, 1)

            def gpsimd(self, pool):
                pass

            def sync(self, sp):
                pass

        def rotate(eng, steps, dst, src, cos, sin, heads, groups, half, tmp):
            w = groups * 2 * half
            v = lambda z: z.rearrange("p (h w) -> p h w", w=w)
            cb = cos.unsqueeze(1).to_broadcast([P, heads, w])
            full = lambda z: z.rearrange("p (h g s d) -> p h g s d", g=groups, s=2, d=half)
            sb_ = sin.rearrange("p (g s d) -> p g s d", s=2, d=half)
            n = heads * w
            for s in range(2):
                sc = sb_[:, :, s, :].unsqueeze(1).to_broadcast([P, heads, groups, half])
                a_, b_ = full(tmp[:, 0:n])[:, :, :, s, :], full(src)[:, :, :, 1 - s, :]
                ins = eng.tensor_tensor(a_, b_, sc, ALU.mult)
            steps.chain(ins)
            steps.chain(eng.tensor_tensor(v(dst), v(src), cb, ALU.mult))
            return eng.tensor_tensor(dst, dst, tmp[:, 0:n], ALU.add)

        made, kept_a, kept_v = signal("piece_made"), signal("piece_kept_act"), signal("piece_kept_dve")

        def turn(srcs):
            return [("turn", s.shape[1], i * P, s) for i, s in enumerate(srcs)]

        class Pieces:

            def __init__(self, groups):
                self.groups = groups
                self.t0 = made.plan(len(groups))
                self.kept = []
                free = 0
                for g in groups:
                    if "mask" in g or free % 2:
                        s = kept_v
                    else:
                        s = kept_a
                    free += "mask" not in g
                    self.kept.append((s, s.plan(1) + 1))

            def tensor(self, pe):
                for g, group in enumerate(self.groups):
                    if g >= 8:
                        sig, count = self.kept[g - 8]
                        pe.wait_ge(sig.sem, count)
                    b = g % 8
                    for op in group["ops"]:
                        if op[0] == "turn":
                            _, m, col, src = op
                            ins = pe.transpose(ps[0:m, b, col:col + P], src, ident)
                        else:
                            _, (p0, p1), col, n, pairs = op[:5]
                            first, last = op[5] if len(op) > 5 else (True, True)
                            for i, (l, r) in enumerate(pairs):
                                ins = pe.matmul(ps[p0:p1, b, col:col + n], l, r, start=(i == 0 and first),
                                                stop=(i == len(pairs) - 1 and last), skip_group_check=len(op) > 5)
                    ins.then_inc(made.sem, 1)

            def keep(self, eng, sig):
                for g, group in enumerate(self.groups):
                    if self.kept[g][0] is not sig:
                        continue
                    eng.wait_ge(made.sem, self.t0 + g + 1)
                    for p0, p1, dst in group["dsts"]:
                        n = int(np.prod(dst.shape[1:]))
                        src = ps[p0:p1, g % 8, 0:n]
                        if len(dst.shape) == 3:
                            src = src.rearrange("p (a b) -> p a b", b=dst.shape[2])
                        if "mask" in group:
                            ins = eng.tensor_tensor(dst, src, group["mask"], ALU.mult)
                        elif sig is kept_a:
                            ins = eng.activation(dst, src, ACT.Copy, scale=group.get("scale", 1.0))
                        elif "scale" in group:
                            ins = eng.tensor_scalar(dst, src, group["scale"], None, ALU.mult)
                        else:
                            ins = eng.tensor_copy(dst, src)
                    ins.then_inc(sig.sem, 1)

            def scalar(self, act):
                self.keep(act, kept_a)

            def vector(self, dve):
                self.keep(dve, kept_v)

            def gpsimd(self, pool):
                pass

            def sync(self, sp):
                pass

        class Work:

            def __init__(self, act=None, dve=None, pool=None, sp=None):
                none = lambda eng: None
                self.scalar, self.vector, self.gpsimd, self.sync = act or none, dve or none, pool or none, sp or none

            def tensor(self, pe):
                pass

        f_silu, f_full, f_high, f_low = (signal("ffn_" + n) for n in ("silu", "full", "high", "low"))
        f_out, f_added = signal("ffn_out_ready"), signal("ffn_out_added")
        GROUP = 256
        GROUPS = FFN // GROUP
        silu_t = at("ffn_silu", [P, 2, TOK], F32, mod_raw_at)
        full_t = at("ffn_full", [P, 2, TOK], F32, mod_raw_at + 2 * TOK * 4)

        class FeedForward:

            def __init__(self, w_in, w_out, tiles):
                self.w_in, self.w_out, self.T = w_in, w_out, tiles
                self.segs = [(0, HALF)] if tiles == XT else [(0, 384), (384, 384)]
                self.parts = [range(i, min(i + 3, GROUPS)) for i in range(0, GROUPS, 3)]
                self.b = {s: s.plan(n) for s, n in ((f_silu, GROUPS), (f_full, 2 * GROUPS), (f_high, 2 * GROUPS), (f_low, 2 * GROUPS),
                                                    (f_out, len(self.parts) * 2 * (tiles - 1)), (f_added, len(self.parts) * 2 * tiles))}
                self.w0 = w_used.plan(6 * GROUPS)
                self.gate_unit, self.up_unit, self.out_unit, u = {}, {}, {}, 0
                for p, part in enumerate(self.parts):
                    for g in part:
                        self.gate_unit[g], self.up_unit[g] = self.w0 + u + 2, self.w0 + u + 4
                        u += 4
                    for h in range(2):
                        u += len(part)
                        self.out_unit[p, h] = self.w0 + u

            def wait(self, eng, s, n):
                if n > 0:
                    eng.wait_ge(s.sem, self.b[s] + n)

            def sync(self, sp):
                for part in self.parts:
                    for g in part:
                        for off in (0, FFN):
                            for half in range(2):
                                weights_load(sp, self.w_in[half * HALF:(half + 1) * HALF, off + g * GROUP:off + (g + 1) * GROUP], 4, GROUP)
                    for n in range(2):
                        for g in part:
                            weights_load(sp, self.w_out[g * GROUP:(g + 1) * GROUP, n * HALF:(n + 1) * HALF], 2, HALF)

            def split_hidden(self, eng, g, act):
                n, lane = self.T * P, g % 3
                for a in range(2):
                    full = full_t[:, a, 0:n]
                    high, low = (act_t[:, s, 2 * lane + a, 0:n] for s in range(2))
                    self.wait(eng, f_full, 2 * g + a + 1)
                    if act:
                        eng.activation(high, full, ACT.Copy).then_inc(f_high.sem, 1)
                    else:
                        self.wait(eng, f_high, 2 * g + a + 1)
                        eng.tensor_tensor(low, full, high.bitcast(F32), ALU.subtract).then_inc(f_low.sem, 1)

            def scalar(self, act):
                n, before = self.T * P, None
                w, k = self.segs[0][1], len(self.segs)
                for p, part in enumerate(self.parts):
                    for g in part:
                        weights_high(act, 4, GROUP)
                        weights_high(act, 4, GROUP)
                        if before is not None:
                            self.split_hidden(act, before, True)
                        weights_high(act, 4, GROUP)
                        weights_high(act, 4, GROUP)
                        act.wait_ge(w_used.sem, self.gate_unit[g])
                        self.wait(act, f_full, 2 * g)
                        for a in range(2):
                            ins = act.activation(silu_t[:, a, 0:n].rearrange("p (s w) -> p s w", w=w), ps[:, a * k:(a + 1) * k, 0:w], ACT.Silu)
                        ins.then_inc(f_silu.sem, 1)
                        before = g
                    self.split_hidden(act, before, True)
                    before = None
                    for _ in range(2 * len(part)):
                        weights_high(act, 2, HALF)

            def gpsimd(self, pool):
                before = None
                for part in self.parts:
                    for g in part:
                        weights_low(pool, 4, GROUP)
                        weights_low(pool, 4, GROUP)
                        if before is not None:
                            self.split_hidden(pool, before, False)
                        weights_low(pool, 4, GROUP)
                        weights_low(pool, 4, GROUP)
                        before = g
                    self.split_hidden(pool, before, False)
                    before = None
                    for _ in range(2 * len(part)):
                        weights_low(pool, 2, HALF)

            def vector(self, dve):
                w, k, i = self.segs[0][1], len(self.segs), 0
                n = self.T * P
                for p, part in enumerate(self.parts):
                    for g in part:
                        self.wait(dve, f_silu, g + 1)
                        dve.wait_ge(w_used.sem, self.up_unit[g])
                        self.wait(dve, f_low, 2 * g)
                        for a in range(2):
                            view = lambda z: z[:, a, 0:n].rearrange("p (s w) -> p s w", w=w)
                            dve.tensor_tensor(view(full_t), ps[:, 4 + a * k:4 + (a + 1) * k, 0:w], view(silu_t), ALU.mult)\
                               .then_inc(f_full.sem, 1)
                    for h in range(2):
                        for t in range(self.T):
                            i += 1
                            y = Y[:, t, h * HALF:(h + 1) * HALF]
                            if t < self.T - 1:
                                self.wait(dve, f_out, i - (2 * p + h))
                            else:
                                dve.wait_ge(w_used.sem, self.out_unit[p, h])
                            if p == 0:
                                ins = dve.tensor_copy(y, ps[:, t, :])
                            else:
                                self.wait(dve, f_added, i - 2 * self.T)
                                ins = dve.tensor_tensor(y, y, ps[:, t, :], ALU.add)
                            ins.then_inc(f_added.sem, 1)

            def tensor(self, pe):
                k, i = len(self.segs), 0
                for p, part in enumerate(self.parts):
                    for g in part:
                        for what, free in ((0, f_silu), (4, f_full)):
                            for half in range(2):
                                w = weights_use(pe, 4, GROUP)
                                if half == 0:
                                    self.wait(pe, free, g if free is f_silu else 2 * g)
                                    self.wait(pe, f_added, i)
                                for a in range(2):
                                    for s, (c0, n) in enumerate(self.segs):
                                        for j in range(4):
                                            kt = 4 * half + j
                                            ins = matmul3(pe, ps[:, what + a * k + s, 0:n], [z[:, j, a * P:(a + 1) * P] for z in w],
                                                          [HT[:, z, kt, c0:c0 + n] for z in range(2)], kt == 0, kt == KT - 1)
                                ins.then_inc(w_used.sem, 1)
                    for h in range(2):
                        for m, g in enumerate(part):
                            w = weights_use(pe, 2, HALF)
                            self.wait(pe, f_low, 2 * g + 2)
                            for t in range(self.T):
                                if m == 0:
                                    self.wait(pe, f_added, i - self.T + t + 1) if h else self.wait(pe, f_full, 2 * part[-1] + 2)
                                for j in range(2):
                                    lane = 2 * (g % 3) + j
                                    ins = matmul3(pe, ps[:, t, :], [act_t[:, z, lane, t * P:(t + 1) * P] for z in range(2)],
                                                  [z[:, j, :] for z in w], m == 0 and j == 0, m == len(part) - 1 and j == 1)
                                if m == len(part) - 1 and t < self.T - 1:
                                    ins.then_inc(f_out.sem, 1)
                            ins.then_inc(w_used.sem, 1)
                        i += self.T

        def heads_view(z, h):
            return z.rearrange("p (h d) -> p h d", h=h)

        c1 = np.float32(6.28125)
        c2 = np.float32(np.round((2 * math.pi - 6.28125) * 2 ** 19) / 2 ** 19)
        c3 = np.float32(np.round((2 * math.pi - float(c1) - float(c2)) * 2 ** 31) / 2 ** 31)
        c4 = np.float32(2 * math.pi - float(c1) - float(c2) - float(c3))
        MAGIC = 1.5 * 2.0 ** 23

        take = region(arena)
        P1 = take("proj_one", [P, XT, IN1])
        cos1 = take("cos_one", [P, XT, 2, 64])
        sin1 = take("sin_one", [P, XT, 2, 64])
        take = region(mod_raw_at)
        gqT, gkT = take("gla_q_t", [P, S]), take("gla_k_t", [P, S])
        gaT = take("gla_a_t", [16, S])
        one_end = take.where[0]
        con1 = at("constants_one", [P, ONE_W], F32, gate_rows_at + 4 * D)
        assert ONE_W * 4 <= 3 * 4 * D
        c1t = lambda name: con1[:, slice(*ONE_COLS[name])]
        small = region(small_at)
        pos_i, pos_f = small("positions_int", [P, XT], I32), small("positions", [P, XT])
        sinks = small("sinks", [P, 8])
        neg_sinks = small("neg_sinks", [P, 8])
        stats = small("attention_stats", [P, 7, 4])
        gate_w = small("gla_gate_w", [16, P])
        gate_b = small("gla_gate_b", [P, 1])
        gla_gain = small("gla_gain", [P, 64])
        headsq = small("head_squares", [P, 64])
        headms = small("head_meansq", [P, 64])
        headr = small("head_rstd", [P, 64])
        half64 = small("minus_half64", [P, 64])
        gla_decay = small("gla_chunk_decay", [P, 8])
        qn_col = small("latent_q_gain", [P, 2])
        kvn_col = small("latent_kv_gain", [P, 1])
        qk_gain = small("qk_gain", [P, 2, 64])
        sub_gain = small("sub_gain", [P, P])
        lam_in = small("lambda_in", [P, 4, 64])
        lam_prod = small("lambda_products", [P, 2, 64])
        lam_sum = small("lambda_sums", [P, 2])
        neg_lam = small("neg_lambda", [P, 1])
        assert small.where[0] <= small_at + SMALL, small.where[0] - small_at
        take = region(ht_at)
        angle = take("angle", [P, XT, 2, 64])
        turns = take("turns", [P, XT, 2, 64])
        reduced = take("reduced", [P, 2, XT, 2, 64])
        take = region(ht_at)
        qT, kT = take("att_q_t", [P, 4, S]), take("att_k_t", [P, 2, S])
        probs1, probs1_t = take("att_probs_one", [P, 2, 2 * P]), take("att_probs_t_one", [P, 2, 2 * P])
        qrT, krT, qdT = take("ret_q_t", [P, 2, S]), take("ret_k_t", [P, 2, S]), take("ret_qdecay_t", [P, 2, S])
        ret_k = take("ret_k_decayed", [P, XT, 256])
        ret_a = take("ret_scores_t", [P, XT, 2, 256])
        ret_u = take("ret_updates", [P, XT, 2, P])
        ret_s = take("ret_states", [P, XT, 2, P])
        assert take.where[0] <= ht_end
        rope_tmp_v = at("rope_tmp_dve", [P, 1024], F32, ht_at)
        rope_tmp_p = at("rope_tmp_pool", [P, 1024], F32, ht_at + 4096)
        take = region(ht_at)
        B = take("gla_log_decay_sums", [P, S])
        gla_a = take("gla_scores_t", [P, 4, S])
        g_dist, g_exp = take("gla_distance", [P, 2, S]), take("gla_factor", [P, 2, S])
        g_q, g_k = take("gla_q_level", [P, 2, S]), take("gla_k_level", [P, 2, S])
        g_kd, g_kdt, g_qe = take("gla_k_decayed_t", [P, S]), take("gla_k_decayed", [P, XT, P]), take("gla_q_decayed_t", [P, S])
        gla_u = take("gla_updates", [P, 8, 256])
        assert take.where[0] <= ht_end
        gla_s = at("gla_states", [P, 8, 256], F32, ht_at + 4 * (S + 4 * S))
        z_t, z_abs, z_min, z_exp = (g_q[:, 0], g_q[:, 1], g_k[:, 0], g_k[:, 1])
        log_a, log_a_tok = g_kd[:, :], g_kdt

        def tok(t):
            return slice(t * P, (t + 1) * P)

        schedule = []

        def setup_phases():
            n_loads = [0]
            loads = [
                (con[:, :], a["static"]), (con1[:, :], a["one"]),
                (X[:, 0:XT, :], a["x"][0].rearrange("(t p) d -> p t d", p=P)),
                (X[:, XT:, :], a["ctx_2"][0].rearrange("(t p) d -> p t d", p=P)),
                (c_raw[:, 0, :], a["c"][0].rearrange("(k p) -> p k", p=P)),
                (c_raw[:, 1, :], a["c_2"][0].rearrange("(k p) -> p k", p=P)),
                (c_raw[:, 2, :], a["c_ctx_2"].rearrange("(k p) -> p k", p=P)),
                (pos_i[:, :], a["positions"][0].rearrange("(t p) -> p t", p=P)),
            ]
            total = load_in.plan(16 * len(loads)) + 16 * len(loads)

            def sp(eng):
                for dst, src in loads:
                    eng.dma_start(dst, src, allow_slow_non_contiguous=True).then_inc(load_in.sem, 16)

            def act(eng):
                eng.wait_ge(load_in.sem, total)
                for cond, r, raw in ((0, 0, 0), (0, 1, 0), (1, 0, 1), (1, 1, 2)):
                    eng.activation(c_act[:, cond, :, r], c_raw[:, raw, :], ACT.Silu)

            def dve(eng):
                eng.memset(minus_half[:, :], -0.5)
                eng.memset(half64[:, :], -0.5)
                eng.memset(headsq[:, :], 1.0)
                eng.memset(headms[:, :], 1.0)
                eng.wait_ge(load_in.sem, total)
                eng.tensor_copy(identb[:, :], ident)
                eng.tensor_copy(window[:, :], c1t("window"))
                dve_s.chain(eng.tensor_copy(pos_f[:, :], pos_i[:, :]))
                f = c1t("freqs").rearrange("p (k n) -> p k n", k=2)
                for t in range(XT):
                    ins = eng.tensor_scalar(angle[:, t], f, pos_f[:, t:t + 1], None, ALU.mult)
                dve_s.chain(ins)
                for which, quarter in ((0, 0.0), (1, 0.25)):
                    r = reduced[:, which]
                    dve_s.chain(eng.tensor_scalar(turns[:], angle[:], 1.0 / (2 * math.pi), quarter, ALU.mult, ALU.add))
                    dve_s.chain(eng.tensor_scalar(turns[:], turns[:], MAGIC, None, ALU.add))
                    dve_s.chain(eng.tensor_scalar(turns[:], turns[:], MAGIC, None, ALU.subtract))
                    flat = lambda z: z.rearrange("p t k n -> p (t k n)")
                    for i, part in enumerate((c1, c2, c3, c4)):
                        dve_s.chain(eng.scalar_tensor_tensor(out=flat(r), in0=flat(turns[:]), scalar=-float(part),
                                                             in1=flat(angle[:] if i == 0 else r), op0=ALU.mult, op1=ALU.add))
                    dve_s.chain(eng.tensor_scalar(r, r, math.pi / 2 * which, 3.1415925, ALU.add, ALU.min))
                    dve_s.chain(eng.tensor_scalar(r, r, -3.1415925, None, ALU.max))

            schedule.append(Work(act=act, dve=dve, sp=sp))

            def sines(eng):
                eng.activation(cos1[:], reduced[:, 1], ACT.Sin)
                for s, sign in ((0, -1.0), (1, 1.0)):
                    eng.activation(sin1[:, :, :, 32 * s:32 * s + 32], reduced[:, 0, :, :, 32 * s:32 * s + 32], ACT.Sin, scale=sign)

            schedule.append(Work(act=sines))

        def layer_one(l):
            small_loads = [
                (sinks[:, :], a["attn_sinks"][l].partition_broadcast(P)), (gate_w[:, :], a["gla_gate_w"][l]),
                (gate_b[:, :], a["gla_gate_b"][l].rearrange("(p o) -> p o", o=1)),
                (gla_gain[:, :], a["gla_norm_gain"][l].partition_broadcast(P)),
            ]
            loaded = load_in.plan(16 * len(small_loads)) + 16 * len(small_loads)
            barrier = len(schedule)

            def sp(eng):
                if barrier:
                    sp_waits_phase(eng, barrier)
                for dst, src in small_loads:
                    eng.dma_start(dst, src, allow_slow_non_contiguous=True).then_inc(load_in.sem, 16)

            def dve(eng):
                eng.wait_ge(load_in.sem, loaded)
                eng.tensor_scalar(neg_sinks[:, :], sinks[:, :], -1.0, None, ALU.mult)

            schedule.append(Work(sp=sp, dve=dve))
            schedule.append(Modulation(a["w_mod"][l], a["b_mod"][l],
                                       [("shift", None, 0), ("scale", a["pre_norm_gain"][l], 1), ("gate", a["post_norm_gain"][l], [0])], 0))
            schedule.append(NormTransposed(False, 0, 1))
            chunks = [(n * HALF, min(HALF, IN1 - n * HALF), range(XT)) for n in range(-(-IN1 // HALF))]
            schedule.append(Linear(a["w_in"][l], chunks, lambda t, c0, n: P1[:, t, c0:c0 + n]))

            def act(eng):
                for t in range(XT):
                    for c0, n in ((AG, 512), (RG, 256), (GG, 256)):
                        eng.activation(P1[:, t, c0:c0 + n], P1[:, t, c0:c0 + n], ACT.Silu)

            def dve(eng):
                for t in range(XT):
                    x = P1[:, t, AQ:AV]
                    dve_s.chain(rotate(eng, dve_s, x, x, cos1[:, t, 0], sin1[:, t, 0], 10, 1, 32, rope_tmp_v))

            def pool(eng):
                for t in range(XT):
                    x = P1[:, t, RQ:RV]
                    pool_s.chain(rotate(eng, pool_s, x, x, cos1[:, t, 1], sin1[:, t, 1], 8, 1, 32, rope_tmp_p))

            schedule.append(Work(act=act, dve=dve, pool=pool))

            def tiles_of(c0, m):
                return turn([P1[:, t, c0:c0 + m] for t in range(XT)])

            groups = [dict(ops=tiles_of(AQ + pair * P, P), dsts=[(0, P, qT[:, pair, :])]) for pair in range(4)]
            groups += [dict(ops=tiles_of(AK + g * 64, 64), dsts=[(0, 64, kT[0:64, g, :]), (0, 64, kT[64:P, g, :])]) for g in range(2)]
            groups += [dict(ops=tiles_of(c + pair * P, P), dsts=[(0, P, z[:, pair, :])]) for c, z in ((RQ, qrT), (RK, krT)) for pair in range(2)]
            groups += [dict(ops=tiles_of(GQ, P), dsts=[(0, P, gqT[:, :])], scale=32 ** -0.5), dict(ops=tiles_of(GK, P), dsts=[(0, P, gkT[:, :])]),
                       dict(ops=tiles_of(GA, 16), dsts=[(0, 16, gaT[:, :])])]
            schedule.append(Pieces(groups))

            units = []
            for t in range(XT):
                for h in range(8):
                    r0 = 64 * (h % 2)
                    first = max(t - 1, 0)
                    blocks = list(range(first, t + 1))
                    keys = [(kT[r0:r0 + 64, h // 4, tok(b)], i * P) for i, b in enumerate(blocks)]
                    mask = [(window[:, (0 if b < t else P):(P if b < t else 2 * P)], i * P) for i, b in enumerate(blocks)]
                    o = P1[:, t, AQ + h * 64:AQ + h * 64 + 64]
                    units.append(dict(q=qT[r0:r0 + 64, h // 2, tok(t)], keys=keys, mask=mask,
                                      values=[P1[:, b, AV + 64 * (h // 4):AV + 64 * (h // 4) + 64] for b in blocks], scale=0.125, sink=h,
                                      finish=("gated", o, P1[:, t, AG + h * 64:AG + h * 64 + 64])))
            schedule.append(Attention(units, probs1, probs1_t, stats, neg_sinks, sinks))

            def dve(eng):
                for pair in range(2):
                    v = lambda z: z[:, pair, :].rearrange("p (t n) -> p t n", n=P)
                    eng.tensor_tensor(v(qdT), v(qrT), c1t("rqdecay")[:, pair * P:(pair + 1) * P].unsqueeze(1).to_broadcast([P, XT, P]), ALU.mult)

            def pool(eng):
                eng.memset(ret_s[:, 0], 0.0)
                for t in range(XT):
                    eng.tensor_tensor(heads_view(ret_k[:, t], 4), heads_view(P1[:, t, RK:RV], 4),
                                      c1t("rkdecay").unsqueeze(2).to_broadcast([P, 4, 64]), ALU.mult)

            schedule.append(Work(dve=dve, pool=pool))
            groups = []
            for t in range(XT):
                for par in range(2):
                    rows = slice(64 * par, 64 * par + 64)
                    groups.append(dict(ops=[("product", (0, P), pair * P, P, [(krT[rows, pair, tok(t)], qrT[rows, pair, tok(t)])]) for pair in range(2)],
                                       dsts=[(0, P, ret_a[:, t, par])], mask=c1t("rdecay")[:, par * 256:(par + 1) * 256]))
                if t < XT - 1:
                    groups.append(dict(ops=[("product", (0, P), pair * P, P, [(ret_k[:, t, tok(pair)], P1[:, t, RV + pair * P:RV + (pair + 1) * P])])
                                            for pair in range(2)], dsts=[(0, P, ret_u[:, t])],
                                       mask=c1t("rblock").unsqueeze(1).to_broadcast([P, 2, P])))
            schedule.append(Pieces(groups))

            def dve(eng):
                for t in range(XT - 1):
                    for pair in range(2):
                        ins = eng.scalar_tensor_tensor(out=ret_s[:, t + 1, pair], in0=ret_s[:, t, pair], scalar=c1t("rchunk")[:, pair:pair + 1],
                                                       in1=ret_u[:, t, pair], op0=ALU.mult, op1=ALU.add)
                    dve_s.chain(ins)

            schedule.append(Work(dve=dve))
            groups = []
            for t in range(XT):
                ops = [("product", (0, P), pair * P, P, [(qdT[:, pair, tok(t)], ret_s[:, t, pair])],
                        (pair == 0, False)) for pair in range(2)]
                ops += [("product", (0, P), h * 64, 64, [(ret_a[:, t, h % 2, (h // 2) * P:(h // 2 + 1) * P], P1[:, t, RV + h * 64:RV + h * 64 + 64])],
                         (False, h == 3)) for h in range(4)]
                groups.append(dict(ops=ops, dsts=[(0, P, P1[:, t, RQ:RQ + 256])]))
            schedule.append(Pieces(groups))

            schedule.append(Pieces([dict(ops=[("product", (0, P), 0, S, [(gate_w[:, :], gaT[:, :])])], dsts=[(0, P, z_t)])]))

            def dve(eng):
                eng.tensor_scalar(z_min, z_t, gate_b[:, 0:1], 0.0, ALU.add, ALU.min)

            schedule.append(Work(dve=dve))

            def act(eng):
                act_s.chain(eng.activation(z_abs, z_t, ACT.Abs, bias=gate_b[:, 0:1]))
                act_s.chain(eng.activation(z_exp, z_abs, ACT.Exp, scale=-1.0))
                eng.activation(z_t, z_exp, ACT.Ln, bias=1.0)

            schedule.append(Work(act=act))
            schedule.append(Work(dve=lambda eng: eng.tensor_tensor(log_a, z_min, z_t, ALU.subtract)))
            schedule.append(Pieces([dict(ops=turn([log_a[:, tok(t)] for t in range(XT)]), dsts=[(0, P, log_a_tok[:, :, :])])]))
            schedule.append(Pieces([dict(ops=[("product", (0, P), t * P, P, [(log_a_tok[:, t], c1t("tri"))]) for t in range(XT)],
                                         dsts=[(0, P, B[:, :])])]))
            schedule.append(GlaLevels())

            chunk_view = lambda z: z.rearrange("p (c n) -> p c n", n=GLA_C)
            dist, fac, fac2 = g_q[:, 0], g_q[:, 1], g_k[:, 0]

            def dve(eng):
                b = chunk_view(B[:, :])
                eng.tensor_tensor(chunk_view(dist), b, b[:, :, GLA_C - 1:GLA_C].to_broadcast([P, 8, GLA_C]), ALU.subtract)

            def act(eng):
                eng.activation(fac2, B[:, :], ACT.Exp, scale=1.0 / GATE_NORM)
                eng.activation(gla_decay[:, :], B[:, GLA_C - 1::GLA_C], ACT.Exp, scale=1.0 / GATE_NORM)

            schedule.append(Work(dve=dve, act=act, pool=lambda eng: eng.memset(gla_s[:, 0], 0.0)))
            schedule.append(Work(act=lambda eng: eng.activation(fac, dist, ACT.Exp, scale=-1.0 / GATE_NORM),
                                 dve=lambda eng: eng.tensor_tensor(g_qe[:, :], gqT[:, :], fac2, ALU.mult)))
            schedule.append(Work(dve=lambda eng: eng.tensor_tensor(g_kd[:, :], gkT[:, :], fac, ALU.mult)))
            schedule.append(Pieces([dict(ops=turn([g_kd[:, tok(t)] for t in range(XT)]), dsts=[(0, P, g_kdt[:, :, :])])]))
            groups = []
            for par in range(2):
                for two in range(2):
                    cs = [2 * t + par for t in (2 * two, 2 * two + 1)]
                    rows = slice(GLA_C * par, GLA_C * par + GLA_C)
                    groups.append(dict(ops=[("product", (0, P), i * 256, 256, [(g_kdt[rows, c // 2, :], P1[rows, c // 2, GV:GV + 256])])
                                            for i, c in enumerate(cs)],
                                       dsts=[(0, P, gla_u[:, cs[0]:cs[1] + 1:2, :])], mask=c1t("gblock").unsqueeze(1).to_broadcast([P, 2, 256])))
            schedule.append(Pieces(groups))

            def dve(eng):
                for c in range(7):
                    dve_s.chain(eng.scalar_tensor_tensor(out=gla_s[:, c + 1], in0=gla_s[:, c], scalar=gla_decay[:, c:c + 1], in1=gla_u[:, c],
                                                         op0=ALU.mult, op1=ALU.add))

            schedule.append(Work(dve=dve))
            groups = []
            for t in range(XT):
                ops = []
                for par in range(2):
                    c = 2 * t + par
                    ops.append(("product", (64 * par, 64 * par + 64), 0, 256, [(g_qe[:, c * GLA_C:(c + 1) * GLA_C], gla_s[:, c])], (True, False)))
                ops += [("product", (0, P), h * 64, 64, [(gla_a[:, h, tok(t)], P1[:, t, GV + h * 64:GV + h * 64 + 64])], (False, h == 3)) for h in range(4)]
                groups.append(dict(ops=ops, dsts=[(0, P, P1[:, t, GQ:GQ + 256])]))
            schedule.append(Pieces(groups))

            sq = at(f"head_sq_{l}", [P, 2, XT, 256], F32, ht_at)

            def dve(eng):
                for i, c0 in enumerate((RQ, GQ)):
                    dve_s.chain(eng.tensor_tensor(sq[:, i], P1[:, :, c0:c0 + 256], P1[:, :, c0:c0 + 256], ALU.mult))
                    dve_s.chain(eng.tensor_reduce(headsq[:, 16 * i:16 * i + 16], sq[:, i].rearrange("p t (h d) -> p (t h) d", d=64), AX, ALU.add))
                eng.tensor_scalar(headms[:, 0:32], headsq[:, 0:32], 1.0 / 64, EPS, ALU.mult, ALU.add)

            def pool(eng):
                for t in range(XT):
                    g = heads_view(P1[:, t, GG:GG + 256], 4)
                    eng.tensor_tensor(g, g, gla_gain[:, :].unsqueeze(1).to_broadcast([P, 4, 64]), ALU.mult)

            schedule.append(Work(dve=dve, pool=pool))
            schedule.append(Work(pool=lambda eng: eng.tensor_tensor(headr[:, 0:32], headms[:, 0:32], half64[:, 0:32], ALU.pow)))

            def dve(eng):
                for t in range(XT):
                    for i, (c0, gc) in enumerate(((RQ, RG), (GQ, GG))):
                        z = P1[:, t, c0:c0 + 256]
                        r = headr[:, 16 * i + 4 * t:16 * i + 4 * t + 4].unsqueeze(2).to_broadcast([P, 4, 64])
                        dve_s.chain(eng.tensor_tensor(heads_view(z, 4), heads_view(z, 4), r, ALU.mult))
                        eng.tensor_tensor(z, z, P1[:, t, gc:gc + 256], ALU.mult)

            schedule.append(Work(dve=dve))
            cols = [0, 128, 256, 384, RQ, RQ + 128, GQ, GQ + 128]
            schedule.append(MixTransposed(lambda t, kt: P1[:, t, cols[kt]:cols[kt] + P], XT))
            schedule.append(Linear(a["w_out"][l], [(n * HALF, HALF, range(XT)) for n in range(2)], lambda t, c0, n: Y[:, t, c0:c0 + n]))
            schedule.append(Residual([0] * XT))

        g_ref, g_fac, g_ql, g_kl, g_mm, g_cp = (signal("gla_" + n) for n in ("distance", "factor", "q_level", "k_level", "scored", "placed"))

        class GlaLevels:

            def __init__(self):
                n = len(LEVELS)
                self.b = {s: s.plan(n) for s in (g_ref, g_fac, g_ql, g_kl)}
                self.b[g_mm], self.b[g_cp] = g_mm.plan(n + 1), g_cp.plan(n + 1)

            def wait(self, eng, s, n):
                if n > 0:
                    eng.wait_ge(s.sem, self.b[s] + n)

            def place(self, dve, l):
                mask = c1t("levels")[:, l * P:(l + 1) * P].bitcast(U32).unsqueeze(1).to_broadcast([P, XT, P])
                self.wait(dve, g_mm, l + 1)
                self.wait(dve, g_cp, l)
                for h in range(4):
                    v = lambda z: z.rearrange("p (t n) -> p t n", n=P)
                    ins = dve.copy_predicated(v(gla_a[:, h]), mask, v(ps[:, 4 * (l % 2) + h, :]))
                ins.then_inc(g_cp.sem, 1)

            def vector(self, dve):
                n = len(LEVELS)
                dve_s.mark(dve.memset(gla_a[:].rearrange("p h s -> p (h s)"), 0.0))
                dve.wait_ge(dve_s.sem, dve_s.n)
                for step in range(n + 2):
                    if step < n:
                        s = LEVELS[step]
                        v = lambda z: z.rearrange("p (b n) -> p b n", n=2 * s)
                        b = v(B[:, :])
                        dist = g_dist[:, step % 2]
                        self.wait(dve, g_fac, step - 1)
                        dve_s.chain(dve.tensor_tensor(v(dist), b, b[:, :, s - 1:s].to_broadcast([P, S // (2 * s), 2 * s]), ALU.subtract))
                        dve.scalar_tensor_tensor(out=dist, in0=dist, scalar=-1.0, in1=dist, op0=ALU.mult, op1=ALU.max).then_inc(g_ref.sem, 1)
                    l = step - 1
                    if 0 <= l < n:
                        self.wait(dve, g_fac, l + 1)
                        self.wait(dve, g_mm, l - 1)
                        dve.tensor_tensor(g_q[:, l % 2], gqT[:, :], g_exp[:, l % 2], ALU.mult).then_inc(g_ql.sem, 1)
                    if step - 2 >= 0:
                        self.place(dve, step - 2)
                self.place(dve, n)

            def scalar(self, act):
                for l in range(len(LEVELS)):
                    self.wait(act, g_ref, l + 1)
                    self.wait(act, g_ql, l - 1)
                    self.wait(act, g_kl, l - 1)
                    act.activation(g_exp[:, l % 2], g_dist[:, l % 2], ACT.Exp, scale=-1.0 / GATE_NORM).then_inc(g_fac.sem, 1)

            def gpsimd(self, pool):
                for l in range(len(LEVELS)):
                    self.wait(pool, g_fac, l + 1)
                    self.wait(pool, g_mm, l - 1)
                    pool.tensor_tensor(g_k[:, l % 2], gkT[:, :], g_exp[:, l % 2], ALU.mult).then_inc(g_kl.sem, 1)

            def tensor(self, pe):
                n = len(LEVELS)
                for l in range(n + 1):
                    if l < n:
                        self.wait(pe, g_ql, l + 1)
                        self.wait(pe, g_kl, l + 1)
                    self.wait(pe, g_cp, l - 1)
                    q, k = (g_q[:, l % 2], g_k[:, l % 2]) if l < n else (gqT[:, :], gkT[:, :])
                    for h in range(4):
                        rows = slice(32 * h, 32 * h + 32)
                        for t in range(XT):
                            ins = pe.matmul(ps[:, 4 * (l % 2) + h, tok(t)], k[rows, tok(t)], q[rows, tok(t)], start=True, stop=True)
                    ins.then_inc(g_mm.sem, 1)

            def sync(self, sp):
                pass

        con2 = at("constants_two", [P, TWO_W], F32, mod_raw_at)
        c2t = lambda name: con2[:, slice(*TWO_COLS[name])]
        take = region(arena)
        PE_ = take("proj_even", [P, XT + CT, EV_IN])
        take = region(take.where[0])
        cqT, ckvT = take("latent_q_t", [P, 2, TOK]), take("latent_kv_t", [P, TOK])
        w_uq, w_ukv = take("w_uq", [P, 2, D * 3 // 4]), take("w_ukv", [P, D])
        qpe = take("latent_q_rope", [P, XT + CT, 256])
        EV_END = take.where[0]
        take = region(ht_at)
        rope_v2, rope_p2 = take("rope_tmp_dve_two", [P, 1024]), take("rope_tmp_pool_two", [P, 1024])
        norm_junk = take("latent_squares", [P, XT + CT, 384])
        take = region(ht_at)
        qaT, kaT = take("even_q_t", [P, 4, TOK]), take("even_k_t", [P, 2, TOK])
        probs2, probs2_t = take("att_probs_two", [P, 2, TOK]), take("att_probs_t_two", [P, 2, TOK])
        assert take.where[0] <= ht_end
        take = region(ht_at + 2 * 2 * TOK * 4)
        probsb, probsb_t = (at(n, [P, 2, TOK], F32, ht_at + i * 2 * TOK * 4) for i, n in enumerate(("att_probs_lat", "att_probs_t_lat")))
        vb = take("latent_values", [P, XT + CT, HALF])
        take = region(take.where[0])
        kbT, qbT = take("latent_k_t", [96, 4, TOK]), take("latent_q_heads_t", [96, 4, TOK])
        assert take.where[0] <= ht_end, (take.where[0], ht_end)
        take = region(arena)
        PO = take("proj_odd", [P, XT + CT, OD_IN])
        take = region(ht_at)
        probs3 = take("att_probs_three", [P, 2, TOK])
        probs3_t = take("att_probs_t_three", [P, 2, TOK])
        qcT, kcT = take("odd_q_t", [P, 4, S]), take("odd_k_t", [P, 2, TOK])
        qfT, kfT = take("diff_q_t", [P, 4, S]), take("diff_k_t", [P, 4, TOK])
        assert take.where[0] <= ht_end

        def rows_of(src, kt, tiles):
            return [src(t)[:, kt] for t in tiles]

        def both(src, dst, m=P, dsts=None, **more):
            out = []
            for tiles in (range(XT), range(XT, XT + CT)):
                cols = slice(tiles[0] * P, tiles[-1] * P + P)
                out.append(dict(ops=turn([src(t) for t in tiles]), dsts=[(p0, p1, d(cols)) for p0, p1, d in dst], **more))
            return out

        def tables(width, t):
            return (c2t(f"cos{width}")[:, t * width:(t + 1) * width], c2t(f"sin{width}")[:, t * width:(t + 1) * width])

        def tables_phase():
            barrier, loaded = len(schedule), load_in.plan(16) + 16

            def sp(eng):
                sp_waits_phase(eng, barrier)
                eng.dma_start(con2[:, :], a["two"]).then_inc(load_in.sem, 16)

            def dve(eng):
                eng.wait_ge(load_in.sem, loaded)
                eng.tensor_copy(window[:, :], c2t("window"))

            schedule.append(Work(sp=sp, dve=dve))

        def layer_even():
            barrier = len(schedule)
            small_loads = [
                (sinks[:, :], a["ev_sink_2"][0].partition_broadcast(P)),
                (qn_col[:, :], a["ev_q_norm_2"][0].rearrange("(k p) -> p k", p=P)),
                (kvn_col[:, :], a["ev_kv_norm_2"][0].rearrange("(p o) -> p o", o=1)),
            ]
            loaded = load_in.plan(16 * len(small_loads)) + 16 * len(small_loads)

            def sp(eng):
                sp_waits_phase(eng, barrier)
                for dst, src in small_loads:
                    eng.dma_start(dst, src, allow_slow_non_contiguous=True).then_inc(load_in.sem, 16)

            def dve(eng):
                eng.wait_ge(load_in.sem, loaded)
                eng.tensor_scalar(neg_sinks[:, :], sinks[:, :], -1.0, None, ALU.mult)

            schedule.append(Work(sp=sp, dve=dve))
            g = lambda i: a["norm_g_2"][0, i]
            schedule.append(Modulation(a["ada_w_2"][0], a["ada_b_2"][0], [
                ("shift", None, 0), ("scale", g(0), 1), ("gate", g(1), [0, 1]),
                ("shift", None, 2), ("scale", g(2), 3), ("gate", g(3), [2, 3])], 1))
            tables_phase()
            schedule.append(NormTransposed(True, 0, 1))
            allt = range(XT + CT)
            schedule.append(Linear(a["ev_w_in_2"][0], [(0, 512, allt), (512, 512, allt), (1024, 160, allt)],
                                   lambda t, c0, n: PE_[:, t, c0:c0 + n]))
            barrier2 = len(schedule)
            loaded2 = load_in.plan(32) + 32

            def sp(eng):
                sp_waits_phase(eng, barrier2)
                eng.dma_start(w_uq[:, :, :], a["ev_w_uq_2"][0].rearrange("(k p) n -> p k n", p=P)).then_inc(load_in.sem, 16)
                eng.dma_start(w_ukv[:, :], a["ev_w_ukv_2"][0]).then_inc(load_in.sem, 16)

            def act(eng):
                for t in allt:
                    eng.activation(norm_junk[:, t, 0:256], PE_[:, t, 768:1024], ACT.Square, accum_out=headsq[:, t:t + 1])
                    eng.activation(norm_junk[:, t, 256:384], PE_[:, t, 1024:1152], ACT.Square, accum_out=headsq[:, 8 + t:9 + t])

            def dve(eng):
                for t in range(XT):
                    x = PE_[:, t, 0:640]
                    dve_s.chain(rotate(eng, dve_s, x, x, *tables(64, t), 10, 2, 16, rope_v2))

            def pool(eng):
                for t in range(XT):
                    x = PE_[:, t, 1152:1184]
                    pool_s.chain(rotate(eng, pool_s, x, x, *tables(32, t), 1, 2, 8, rope_p2))

            schedule.append(Work(act=act, dve=dve, pool=pool, sp=sp))

            def dve(eng):
                eng.tensor_scalar(headms[:, 0:6], headsq[:, 0:6], 1.0 / 256, EPS, ALU.mult, ALU.add)
                eng.tensor_scalar(headms[:, 8:14], headsq[:, 8:14], 1.0 / 128, EPS, ALU.mult, ALU.add)

            schedule.append(Work(dve=dve))
            schedule.append(Work(pool=lambda eng: eng.tensor_tensor(headr[:, 0:16], headms[:, 0:16], half64[:, 0:16], ALU.pow)))

            def dve(eng):
                eng.wait_ge(load_in.sem, loaded2)
                for t in allt:
                    for c0, c1_, s in ((768, 1024, 0), (1024, 1152, 8)):
                        z = PE_[:, t, c0:c1_]
                        eng.tensor_scalar(z, z, headr[:, s + t:s + t + 1], None, ALU.mult)

            schedule.append(Work(dve=dve))
            groups = []
            for pair in range(4):
                groups += both(lambda t: PE_[:, t, pair * P:(pair + 1) * P], [(0, P, lambda c, pair=pair: qaT[:, pair, c])])
            for kv in range(2):
                groups += both(lambda t: PE_[:, t, 512 + 64 * kv:576 + 64 * kv],
                               [(0, 64, lambda c, kv=kv: kaT[0:64, kv, c]), (0, 64, lambda c, kv=kv: kaT[64:P, kv, c])])
                groups += both(lambda t: PE_[:, t, 768 + P * kv:768 + P * (kv + 1)], [(0, P, lambda c, kv=kv: cqT[:, kv, c])],
                               scale=qn_col[:, kv:kv + 1])
            groups += both(lambda t: PE_[:, t, 1024:1152], [(0, P, lambda c: ckvT[:, c])], scale=kvn_col[:, 0:1])
            schedule.append(Pieces(groups))

            units = []
            for t in allt:
                for h in range(8):
                    r0 = 64 * (h % 2)
                    local = [b for b in (t - 1, t, t + 1) if 0 <= b < XT] if t < XT else []
                    blocks = local + [XT, XT + 1]
                    mask = [(window[:, (0 if b < t else P):(P if b < t else 2 * P)], i * P) for i, b in enumerate(local) if b != t]
                    units.append(dict(q=qaT[r0:r0 + 64, h // 2, tok(t)], keys=[(kaT[r0:r0 + 64, h // 4, tok(b)], i * P) for i, b in enumerate(blocks)],
                                      mask=mask, values=[PE_[:, b, 640 + 64 * (h // 4):704 + 64 * (h // 4)] for b in blocks], scale=0.125, sink=h,
                                      finish=("plain", PE_[:, t, h * 64:h * 64 + 64], None)))
            schedule.append(Attention(units, probs2, probs2_t, stats, neg_sinks, sinks))

            w_kv = w_ukv[:, :].rearrange("p (h n) -> p h n", h=8)
            w_q = w_uq[:, :, :].rearrange("p k (h n) -> p k h n", h=8)
            groups = []
            for t in allt:
                groups.append(dict(ops=[("product", (0, P), 0, HALF, [(ckvT[:, tok(t)], w_kv[:, :, 64:128])])], dsts=[(0, P, vb[:, t, :])]))
                groups.append(dict(ops=[("product", (0, P), 0, 256, [(cqT[:, k, tok(t)], w_q[:, k, :, 64:96]) for k in range(2)])],
                                   dsts=[(0, P, qpe[:, t, :])]))
            schedule.append(Pieces(groups))

            tmp_q = at("rope_tmp_latent", [P, 256], F32, ht_at)

            def dve(eng):
                for t in range(XT):
                    x = qpe[:, t, :]
                    dve_s.chain(rotate(eng, dve_s, x, x, *tables(32, t), 8, 2, 8, tmp_q))

            schedule.append(Work(dve=dve))
            for four in range(2):
                groups = []
                for i in range(4):
                    h = 4 * four + i
                    for c0, n in ((0, S), (S, CTX)):
                        groups.append(dict(ops=[("product", (0, 64), 0, n, [(w_kv[:, h, 0:64], ckvT[:, c0:c0 + n])])], dsts=[(0, 64, kbT[0:64, i, c0:c0 + n])]))
                        groups.append(dict(ops=[("product", (0, 64), 0, n, [(w_q[:, k, h, 0:64], cqT[:, k, c0:c0 + n]) for k in range(2)])],
                                           dsts=[(0, 64, qbT[0:64, i, c0:c0 + n])]))
                groups += both(lambda t: PE_[:, t, 1152:1184], [(0, 32, lambda c, i=i: kbT[64:96, i, c]) for i in range(4)])
                groups += both(lambda t: qpe[:, t, four * P:(four + 1) * P], [(32 * i, 32 * i + 32, lambda c, i=i: qbT[64:96, i, c]) for i in range(4)])
                schedule.append(Pieces(groups))
                units = []
                for t in allt:
                    for i in range(4):
                        h = 4 * four + i
                        blocks = list(range(XT + CT)) if t < XT else [XT, XT + 1]
                        spans = ((0, S), (S, CTX)) if t < XT else ((S, CTX),)
                        keys = [(kbT[:, i, c0:c0 + n], c0 if t < XT else 0) for c0, n in spans]
                        units.append(dict(q=qbT[:, i, tok(t)], keys=keys, mask=[], values=[vb[:, b, h * 64:h * 64 + 64] for b in blocks],
                                          scale=96 ** -0.5, sink=None, finish=("plain", PE_[:, t, HALF + h * 64:HALF + h * 64 + 64], None)))
                schedule.append(Attention(units, probsb, probsb_t, stats))
            schedule.append(MixTransposed(lambda t, kt: PE_[:, t, kt * P:(kt + 1) * P], XT + CT))
            schedule.append(Linear(a["ev_w_out_2"][0], [(n * HALF, HALF, allt) for n in range(2)], lambda t, c0, n: Y[:, t, c0:c0 + n]))
            schedule.append(Residual([0] * XT + [1] * CT))
            schedule.append(NormTransposed(True, 2, 3))
            schedule.append(FeedForward(a["ffn_w_in_2"][0], a["ffn_w_out_2"][0], XT + CT))
            schedule.append(Residual([2] * XT + [3] * CT))

        def layer_odd():
            barrier = len(schedule)
            small_loads = [
                (qk_gain[:, :, :], a["od_qk_norm_2"][0].partition_broadcast(P)),
                (lam_in[:, :, :], a["od_lambda_2"][0].partition_broadcast(P)),
                (sub_gain[:, :], a["od_subln_2"][0].partition_broadcast(P)),
            ]
            loaded = load_in.plan(16 * len(small_loads)) + 16 * len(small_loads)

            def sp(eng):
                for dst, src in small_loads:
                    eng.dma_start(dst, src, allow_slow_non_contiguous=True).then_inc(load_in.sem, 16)

            def dve(eng):
                eng.wait_ge(load_in.sem, loaded)
                eng.tensor_scalar(sub_gain[:, :], sub_gain[:, :], 1.0 - LAM_INIT, None, ALU.mult)
                pairs = lam_in[:, :, :].rearrange("p (a b) d -> p a b d", b=2)
                dve_s.chain(eng.tensor_tensor(lam_prod[:, :, :], pairs[:, :, 0, :], pairs[:, :, 1, :], ALU.mult))
                eng.tensor_reduce(lam_sum[:, :], lam_prod[:, :, :], AX, ALU.add)

            schedule.append(Work(sp=sp, dve=dve))
            schedule.append(Work(act=lambda eng: eng.activation(lam_prod[:, 0, 0:2], lam_sum[:, :], ACT.Exp)))

            def dve(eng):
                dve_s.chain(eng.tensor_tensor(neg_lam[:, :], lam_prod[:, 0, 1:2], lam_prod[:, 0, 0:1], ALU.subtract))
                eng.tensor_scalar(neg_lam[:, :], neg_lam[:, :], -LAM_INIT, None, ALU.add)

            schedule.append(Work(dve=dve))
            g = lambda i: a["norm_g_2"][1, i]
            schedule.append(Modulation(a["ada_w_2"][1], a["ada_b_2"][1], [
                ("shift", None, 0), ("scale", g(0), 1), ("gate", g(1), [0]),
                ("shift", None, 2), ("scale", g(2), 3), ("gate", g(3), [2])], 1))
            tables_phase()
            schedule.append(NormTransposed(True, 0, 1))
            allt, xt = range(XT + CT), range(XT)
            schedule.append(Linear(a["od_w_in_2"][0], [(0, 512, xt), (512, 256, allt), (768, 512, xt), (1280, 512, allt), (1792, 512, allt)],
                                   lambda t, c0, n: PO[:, t, c0:c0 + n]))
            sq = at("odd_squares", [P, XT + CT, 640], F32, ht_at)
            tmp = at("odd_rope_tmp", [P, 1024], F32, ht_at + 6 * 640 * 4)
            parts = [(t, 0, 10) if t < XT else (t, 8, 10) for t in allt]

            def dve(eng):
                for t, h0, h1 in parts:
                    z = PO[:, t, h0 * 64:h1 * 64]
                    ins = eng.tensor_tensor(sq[:, t, h0 * 64:h1 * 64], z, z, ALU.mult)
                dve_s.chain(ins)
                for t, h0, h1 in parts:
                    ins = eng.tensor_reduce(headsq[:, t * 10 + h0:t * 10 + h1], heads_view(sq[:, t, h0 * 64:h1 * 64], h1 - h0), AX, ALU.add)
                dve_s.chain(ins)
                eng.tensor_scalar(headms[:, 0:60], headsq[:, 0:60], 1.0 / 64, EPS, ALU.mult, ALU.add)

            def pool(eng):
                for t in xt:
                    x = PO[:, t, 768:1792]
                    pool_s.chain(rotate(eng, pool_s, x, x, *tables(64, t), 16, 2, 16, tmp))

            schedule.append(Work(dve=dve, pool=pool))
            schedule.append(Work(pool=lambda eng: eng.tensor_tensor(headr[:, 0:60], headms[:, 0:60], half64[:, 0:60], ALU.pow)))

            def dve(eng):
                for t, h0, h1 in parts:
                    z = heads_view(PO[:, t, h0 * 64:h1 * 64], h1 - h0)
                    dve_s.chain(eng.tensor_tensor(z, z, headr[:, t * 10 + h0:t * 10 + h1].unsqueeze(2).to_broadcast([P, h1 - h0, 64]), ALU.mult))
                    for which, lo, hi in ((0, h0, 8), (1, 8, 10)):
                        if lo < hi:
                            z = heads_view(PO[:, t, lo * 64:hi * 64], hi - lo)
                            ins = eng.tensor_tensor(z, z, qk_gain[:, which, :].unsqueeze(1).to_broadcast([P, hi - lo, 64]), ALU.mult)
                    dve_s.chain(ins)
                    if t < XT:
                        x = PO[:, t, 0:640]
                        dve_s.chain(rotate(eng, dve_s, x, x, *tables(64, t), 10, 2, 16, sq[:, t, :]))

            schedule.append(Work(dve=dve))
            groups = []
            for pair in range(4):
                groups.append(dict(ops=turn([PO[:, t, pair * P:(pair + 1) * P] for t in xt]), dsts=[(0, P, qcT[:, pair, :])]))
                groups.append(dict(ops=turn([PO[:, t, 768 + pair * P:768 + (pair + 1) * P] for t in xt]), dsts=[(0, P, qfT[:, pair, :])]))
                groups += both(lambda t: PO[:, t, 1280 + pair * P:1280 + (pair + 1) * P], [(0, P, lambda c, pair=pair: kfT[:, pair, c])])
            for kv in range(2):
                groups += both(lambda t: PO[:, t, 512 + 64 * kv:576 + 64 * kv],
                               [(0, 64, lambda c, kv=kv: kcT[0:64, kv, c]), (0, 64, lambda c, kv=kv: kcT[64:P, kv, c])])
            schedule.append(Pieces(groups))
            units = []
            for t in xt:
                for h in range(8):
                    r = slice(64 * (h % 2), 64 * (h % 2) + 64)
                    units.append(dict(q=qcT[r, h // 2, tok(t)], keys=[(kcT[r, h // 4, c0:c0 + n], c0) for c0, n in ((0, S), (S, CTX))], mask=[],
                                      values=[PO[:, b, 640 + 64 * (h // 4):704 + 64 * (h // 4)] for b in allt], scale=0.125, sink=None,
                                      finish=("plain", PO[:, t, h * 64:h * 64 + 64], None)))
                for h in range(4):
                    dst = PO[:, t, 768 + h * P:768 + (h + 1) * P]
                    for i in range(2):
                        r = slice(64 * i, 64 * i + 64)
                        units.append(dict(q=qfT[r, h, tok(t)], keys=[(kfT[r, h, c0:c0 + n], c0) for c0, n in ((0, S), (S, CTX))], mask=[],
                                          values=[PO[:, b, 1792 + h * P:1792 + (h + 1) * P] for b in allt], scale=0.125, sink=None,
                                          finish=("minus_lambda", dst, dst) if i else ("plain", dst, None)))
            schedule.append(Attention(units, probs3, probs3_t, stats, neg_lambda=neg_lam[:, 0:1]))

            dsq = at("diff_squares", [P, XT, HALF], F32, ht_at)

            def dve(eng):
                dve_s.chain(eng.tensor_tensor(dsq[:], PO[:, 0:XT, 768:1280], PO[:, 0:XT, 768:1280], ALU.mult))
                dve_s.chain(eng.tensor_reduce(headsq[:, 0:16], dsq[:].rearrange("p t (h d) -> p (t h) d", d=P), AX, ALU.add))
                eng.tensor_scalar(headms[:, 0:16], headsq[:, 0:16], 1.0 / P, EPS, ALU.mult, ALU.add)

            schedule.append(Work(dve=dve))
            schedule.append(Work(pool=lambda eng: eng.tensor_tensor(headr[:, 0:16], headms[:, 0:16], half64[:, 0:16], ALU.pow)))

            def dve(eng):
                for t in xt:
                    for h in range(4):
                        z = PO[:, t, 768 + h * P:768 + (h + 1) * P]
                        eng.scalar_tensor_tensor(out=z, in0=z, scalar=headr[:, 4 * t + h:4 * t + h + 1], in1=sub_gain[:, :], op0=ALU.mult, op1=ALU.mult)

            schedule.append(Work(dve=dve))
            schedule.append(MixTransposed(lambda t, kt: PO[:, t, (kt * P if kt < 4 else 256 + kt * P):(kt * P if kt < 4 else 256 + kt * P) + P], XT))
            schedule.append(Linear(a["od_w_out_2"][0], [(n * HALF, HALF, xt) for n in range(2)], lambda t, c0, n: Y[:, t, c0:c0 + n]))
            schedule.append(Residual([0] * XT))
            schedule.append(NormTransposed(False, 2, 3))
            schedule.append(FeedForward(a["ffn_w_in_2"][1], a["ffn_w_out_2"][1], XT))
            schedule.append(Residual([2] * XT))

        setup_phases()
        marks = []
        for l in range(DEPTH):
            layer_one(l)
            marks.append(len(schedule))
        layer_even()
        marks.append(len(schedule))
        layer_odd()
        marks.append(len(schedule))
        if stop is not None:
            schedule = schedule[:stop if stop >= 0 else marks[-stop - 1]]

        block = ctx.enter_context(nc.Block())

        @block.sync
        def _(sp):
            for i, phase in enumerate(schedule):
                if isinstance(phase, Modulation) and i:
                    sp_waits_phase(sp, i)
                phase.sync(sp)
            sp_waits_phase(sp, len(schedule))
            sp.dma_start(out[0].rearrange("(t p) d -> p t d", p=P), X[:, 0:XT, :]).then_inc(out_landed.sem, 16)
            sp.wait_ge(out_landed.sem, 16)

        @block.tensor
        def _(pe):
            for phase in schedule:
                phase.tensor(pe)
                phase_end(pe, "pe")

        @block.scalar
        def _(act):
            nonlocal act_s
            act_s = Steps(act, act_step.sem)
            for phase in schedule:
                phase.scalar(act)
                phase_end(act, "act")

        @block.vector
        def _(dve):
            nonlocal dve_s
            dve_s = Steps(dve, dve_step.sem)
            for phase in schedule:
                phase.vector(dve)
                phase_end(dve, "dve")

        @block.gpsimd
        def _(pool):
            nonlocal pool_s
            pool_s = Steps(pool, pool_step.sem)
            for phase in schedule:
                phase.gpsimd(pool)
                phase_end(pool, "pool")


_INS = ["x", "c", "positions", "w_mod", "b_mod", "pre_norm_gain", "post_norm_gain", "w_in", "attn_sinks", "gla_gate_w",
        "gla_gate_b", "gla_norm_gain", "w_out", "c_2", "ctx_2", "c_ctx_2", "ada_w_2", "ada_b_2", "norm_g_2", "ffn_w_in_2",
        "ffn_w_out_2", "ev_w_in_2", "ev_sink_2", "ev_q_norm_2", "ev_w_uq_2", "ev_kv_norm_2", "ev_w_ukv_2", "ev_w_out_2",
        "od_w_in_2", "od_qk_norm_2", "od_lambda_2", "od_subln_2", "od_w_out_2"]


def lay_out(nc, inputs):
    arrays, args = {}, {}
    tables = {"static": static_constants(), "one": block_one_constants(), "two": block_two_constants()}
    for name in _INS + list(tables):
        v = np.ascontiguousarray(tables[name] if name in tables else inputs[name])
        arrays[f"in_{name}_dram"] = v
        args[name] = nc.dram_tensor(f"in_{name}_dram", v.shape, mybir.dt.from_np(v.dtype), kind="ExternalInput").ap()
    return arrays, args


def kernel(**inputs):
    import concourse.bacc as bacc
    from concourse.bass_utils import run_bass_kernel_spmd

    nc = bacc.Bacc("TRN2", target_bir_lowering=False, num_devices=1)
    arrays, args = lay_out(nc, inputs)
    out = nc.dram_tensor("out_0_dram", (1, S, D), F32, kind="ExternalOutput").ap()
    build(nc, args, out)
    r = run_bass_kernel_spmd(nc, [arrays], core_ids=[0])
    return r.results[0]["out_0_dram"]
```

```python
from contextlib import ExitStack
import math

import numpy as np

import concourse.bass as bass
from concourse import mybir

F32 = mybir.dt.float32
F32R = mybir.dt.float32r
BF16 = mybir.dt.bfloat16
I32 = mybir.dt.int32
U32 = mybir.dt.uint32
ALU = mybir.AluOpType
ACT = mybir.ActivationFunctionType
AX = mybir.AxisListType.X

P = 128
D = 1024
KT = D // P
S = 512
CTX = 256
XT = S // P
CT = CTX // P
TOK = S + CTX
DEPTH = 2
EPS = 1e-6
NEG = -1e30
HALF = 512

AQ, AK, AV, AG = 0, 512, 640, 768
RQ, RK, RV, RG = 1280, 1536, 1792, 2048
GQ, GK, GV, GG, GA = 2304, 2432, 2560, 2816, 3072
IN1 = 3088
GLA_C = 64
GATE_NORM = 16.0
LEVELS = (32, 16, 8, 4, 2, 1)

EV_IN, OD_IN = 1184, 2304
FFN = 2816
LAM_INIT = 0.8 - 0.6 * math.exp(-0.3)

def _layout(widths):
    at, cols = 0, {}
    for name, n in widths:
        cols[name] = (at, at + n)
        at += n
    return cols, at


STATIC_COLS, STATIC_W = _layout([("ident", P), ("ones", P)])
ONE_COLS, ONE_W = _layout([
    ("window", 2 * P), ("tri", P), ("levels", 7 * P), ("rdecay", 4 * P), ("rqdecay", 2 * P),
    ("rkdecay", 4), ("rchunk", 2), ("rblock", P), ("gblock", 2 * P), ("freqs", 2 * 64)])
TWO_COLS, TWO_W = _layout([("window", 2 * P), ("cos64", 4 * 64), ("sin64", 4 * 64), ("cos32", 4 * 32),
                           ("sin32", 4 * 32)])


def static_constants():
    t = np.zeros((P, STATIC_W), np.float32)
    t[:, slice(*STATIC_COLS["ident"])] = np.eye(P)
    t[:, slice(*STATIC_COLS["ones"])] = 1.0
    return t


def block_one_constants():
    t = np.zeros((P, ONE_W), np.float32)
    put = lambda name, v: t.__setitem__((slice(None), slice(*ONE_COLS[name])), np.asarray(v).reshape(P, -1))
    i, j = np.arange(P)[:, None], np.arange(P)[None, :]
    put("window", np.concatenate([np.where(j > i, 0, NEG), np.where(j <= i, 0, NEG)], 1))
    src, dst = np.arange(P)[:, None], np.arange(P)[None, :]
    put("tri", (src <= dst) & (src // GLA_C == dst // GLA_C))
    lv = [(src // (2 * s) == dst // (2 * s)) & (src % (2 * s) < s) & (dst % (2 * s) >= s) for s in LEVELS]
    put("levels", np.stack(lv + [src == dst], 1).astype(np.float32))
    log_g = np.log(1.0 - 2.0 ** (-5.0 - np.arange(4)))
    diff = dst - src
    dm = np.where(diff >= 0, np.exp(log_g[:, None, None] * np.maximum(diff, 0)), 0.0) * 64 ** -0.5
    put("rdecay", np.stack([dm[0], dm[2], dm[1], dm[3]], 1))
    part = np.arange(P)[:, None] // 64
    qd = [np.exp(log_g[2 * pair + part] * (np.arange(P)[None, :] + 1.0)) for pair in range(2)]
    put("rqdecay", np.stack(qd, 1))
    put("rkdecay", np.exp(log_g[None, :] * (P - 1.0 - np.arange(P)[:, None])) * 64 ** -0.5)
    put("rchunk", np.concatenate([np.exp(log_g[2 * pair + part] * P) for pair in range(2)], 1))
    put("rblock", src // 64 == dst // 64)
    put("gblock", src // 32 == np.arange(2 * P)[None, :] // 64)
    rope = (np.float32(10000.0) ** (-np.arange(0, 64, 2, dtype=np.float32) / np.float32(64))).astype(np.float32)
    ret = (1.0 / (np.float32(10000.0) ** np.linspace(0.0, 1.0, 32, dtype=np.float32))).astype(np.float32)
    put("freqs", np.tile(np.concatenate([rope, rope, ret, ret])[None], (P, 1)))
    return t


def block_two_constants():
    t = np.zeros((P, TWO_W), np.float32)
    put = lambda name, v: t.__setitem__((slice(None), slice(*TWO_COLS[name])), np.asarray(v).reshape(P, -1))
    i, j = np.arange(P)[:, None], np.arange(P)[None, :]
    put("window", np.concatenate([np.where(j >= i, 0, NEG), np.where(j <= i, 0, NEG)], 1))
    tok = np.arange(S)
    for width in (64, 32):
        half = width // 4
        fr = (np.float32(10000.0) ** (-np.arange(half, dtype=np.float32) / np.float32(half))).astype(np.float32)
        cos, sin = [], []
        for pos in (tok // 64, tok % 64):
            a = pos.astype(np.float32)[:, None] * fr[None]
            cos += [np.cos(a), np.cos(a)]
            sin += [-np.sin(a), np.sin(a)]
        for name, parts in (("cos", cos), ("sin", sin)):
            full = np.concatenate(parts, 1).reshape(XT, P, width).transpose(1, 0, 2)
            put(f"{name}{width}", full)
    return t


class Signal:

    def __init__(self, sem):
        self.sem, self.planned = sem, 0

    def plan(self, n):
        before = self.planned
        self.planned += n
        return before


class Steps:

    def __init__(self, eng, sem):
        self.eng, self.sem, self.n = eng, sem, 0

    def mark(self, ins):
        self.n += 1
        ins.then_inc(self.sem, 1)
        return self.n

    def chain(self, ins):
        self.eng.wait_ge(self.sem, self.mark(ins))


def build(nc, a, out, stop=None):
    with ExitStack() as ctx:
        base = (nc.sbuf_base + 31) // 32 * 32
        room = nc.sbuf_usable_end - base
        place = [0]

        def at(name, shape, dt, offset):
            assert offset + int(np.prod(shape[1:])) * mybir.dt.size(dt) <= room, (name, offset)
            return nc.alloc_sbuf_tensor_at(name, shape, dt, offset=base + offset)

        def static(name, shape, dt=F32):
            t = at(name, shape, dt, place[0])
            place[0] += (int(np.prod(shape[1:])) * mybir.dt.size(dt) + 31) // 32 * 32
            return t

        def region(start):
            where = [start]

            def take(name, shape, dt=F32):
                t = at(name, shape, dt, where[0])
                where[0] += (int(np.prod(shape[1:])) * mybir.dt.size(dt) + 31) // 32 * 32
                return t
            take.where = where
            return take

        def signal(name):
            return Signal(ctx.enter_context(nc.semaphore(name)))

        ps = ctx.enter_context(nc.psum_tensor("ps", [P, 8, HALF], F32))

        X = static("x_tokens", [P, XT + CT, D])
        ht_at = place[0]
        HT = static("h_transposed", [P, 2, KT, TOK], F32R)
        ht_end = place[0]
        w_raw = static("w_raw", [P, 4, 1024])
        w_hi = static("w_hi", [P, 2, 1024], F32R)
        w_lo = static("w_lo", [P, 2, 1024], F32R)
        aux_at = place[0]
        static("aux_room", [P, 3 * 2 * HALF])
        con = static("static_constants", [P, STATIC_W])
        gate_rows_at = place[0]
        gate_rows = static("gate_rows", [P, 4, D])
        mod_cols = static("mod_columns", [P, 8, KT, 2])
        c_raw = static("c_raw", [P, 3, KT])
        c_act = static("c_act", [P, 2, KT, 2])
        mod_bias = static("mod_bias", [P, 2, HALF])
        mod_gain = static("mod_gain", [P, HALF])
        sumsq = static("sumsq", [P, 8])
        meansq = static("meansq", [P, 8])
        rstd = static("rstd", [P, 32])
        minus_half = static("minus_half", [P, 32])
        identb = static("ident_bf16", [P, P], BF16)
        window = static("window_bf16", [P, 2 * P], BF16)
        small_at, SMALL = place[0], 5440
        arena = small_at + SMALL
        ident = con[:, slice(*STATIC_COLS["ident"])]
        ones = con[:, slice(*STATIC_COLS["ones"])]
        mod_acc_aux = at("mod_acc_aux", [P, 2, 2, HALF], F32, aux_at + 2 * D * 2)
        mod_acc_gates = at("mod_acc_gates", [P, 2, 2, HALF], F32, gate_rows_at)

        take = region(arena)
        xn = take("x_normed", [P, XT + CT, D])
        junk = take("square_junk", [P, D])
        h_full = take("h_full", [P, 2, HALF])
        take = region(arena)
        Y = take("y_tokens", [P, XT + CT, D])
        act_t = take("ffn_hidden", [P, 2, 6, TOK], F32R)
        res_junk = at("residual_junk", [P, D], F32, arena + (XT + CT) * D * 4)

        dve_s = act_s = pool_s = None

        load_in = signal("inputs_landed")
        w_landed = [signal(f"w_landed{i}") for i in range(4)]
        w_hi_ready, w_lo_ready, w_used = signal("w_hi_ready"), signal("w_lo_ready"), signal("w_used")
        phase_done = signal("phase_done")
        out_landed = signal("out_landed")
        dve_step, act_step, pool_step = signal("dve_step"), signal("act_step"), signal("pool_step")
        units_done = {"act": 0, "pool": 0, "pe": 0}
        phases_done = {"pe": 0, "act": 0, "dve": 0, "pool": 0}

        def phase_end(eng, name):
            phases_done[name] += 1
            eng.drain().then_inc(phase_done.sem, 1)
            eng.wait_ge(phase_done.sem, 4 * phases_done[name])

        def flows(phase):
            return isinstance(phase, (NormTransposed, MixTransposed))

        def sp_waits_phase(sp, n):
            assert not flows(schedule[n - 1])
            sp.wait_ge(phase_done.sem, 4 * sum(not flows(p) for p in schedule[:n]))

        stream = []
        ring = {"weight": [], "mod": []}

        def ring_slot(sp, kind):
            u = len(stream)
            if u >= 4:
                before, n = stream[u - 4]
                sp.wait_ge((w_lo_ready if before == "weight" else mod_unit).sem, n + 1)
            stream.append((kind, len(ring[kind])))
            ring[kind].append(u)
            return u

        def weights_load(sp, src, k, n):
            u = ring_slot(sp, "weight")
            dst = w_raw[:, u % 4, 0:k * n].rearrange("p (k n) -> p k n", k=k)
            sp.dma_start(dst, src.rearrange("(k p) n -> p k n", p=P)).then_inc(w_landed[u % 4].sem, 16)

        def weights_high(act, k, n):
            i = units_done["act"]
            units_done["act"] += 1
            u = ring["weight"][i]
            act.wait_ge(w_landed[u % 4].sem, 16 * (u // 4 + 1))
            if i >= 2:
                act.wait_ge(w_used.sem, i - 1)
            act.activation(w_hi[:, i % 2, 0:k * n], w_raw[:, u % 4, 0:k * n], ACT.Copy).then_inc(w_hi_ready.sem, 1)

        def weights_low(pool, k, n):
            i = units_done["pool"]
            units_done["pool"] += 1
            u = ring["weight"][i]
            pool.wait_ge(w_hi_ready.sem, i + 1)
            pool.tensor_tensor(w_lo[:, i % 2, 0:k * n], w_raw[:, u % 4, 0:k * n],
                               w_hi[:, i % 2, 0:k * n].bitcast(F32), ALU.subtract).then_inc(w_lo_ready.sem, 1)

        def weights_use(pe, k, n):
            u = units_done["pe"]
            units_done["pe"] += 1
            pe.wait_ge(w_lo_ready.sem, u + 1)
            return [w[:, u % 2, 0:k * n].rearrange("p (k n) -> p k n", k=k) for w in (w_hi, w_lo)]

        def matmul3(pe, acc, left, right, start, stop):
            pe.matmul(acc, left[0], right[0], start=start, stop=False)
            pe.matmul(acc, left[0], right[1], start=False, stop=False)
            return pe.matmul(acc, left[1], right[0], start=False, stop=stop)

        mod_side = [signal("mod_bias_landed0"), signal("mod_bias_landed1"), signal("mod_gain_landed")]
        mod_unit, mod_summed, mod_turned, mod_kept = (signal(n) for n in ("mod_unit", "mod_summed", "mod_turned", "mod_kept"))
        mod_ready = signal("mod_bias_cleared")
        turns_before = []

        class ModJob:
            jobs = turns = 0

            def __init__(self, w, bias, kind, gain, conds, targets, half, col, acc):
                self.k, ModJob.jobs = ModJob.jobs, ModJob.jobs + 1
                self.w, self.bias = w[:, col:col + HALF], bias[col:col + HALF]
                self.kind, self.conds, self.targets, self.half = kind, conds, targets, half
                self.gain = None if gain is None else gain[half * HALF:(half + 1) * HALF]
                self.acc = acc[:, self.k % 2]
                self.turn0 = ModJob.turns
                self.turns = len(conds) if kind == "gate" else 1
                ModJob.turns += self.turns
                turns_before.append(self.turn0)
                self.side_bias = mod_side[self.k % 2].plan(16) + 16
                if gain is not None:
                    self.side_gain = mod_side[2].plan(16) + 16

            def load(self, sp, q):
                if q == 0:
                    if self.k == 0:
                        sp.wait_ge(mod_ready.sem, 1)
                    if self.k >= 2:
                        sp.wait_ge(mod_summed.sem, self.k - 1)
                    sp.dma_start(mod_bias[0:1, self.k % 2, :], self.bias.rearrange("(o n) -> o n", o=1)).then_inc(mod_side[self.k % 2].sem, 16)
                if q == 2 and self.gain is not None:
                    if self.k >= 1:
                        sp.wait_ge(mod_summed.sem, self.k)
                    sp.dma_start(mod_gain[:, :], self.gain.partition_broadcast(P)).then_inc(mod_side[2].sem, 16)
                u = ring_slot(sp, "mod")
                sp.dma_start(w_raw[:, u % 4, :].rearrange("p (k n) -> p k n", k=2),
                             self.w[q * 256:(q + 1) * 256].rearrange("(k p) n -> p k n", p=P)).then_inc(w_landed[u % 4].sem, 16)

            def sum(self, dve, q):
                first = mod_bias[:, self.k % 2, :]
                if q == 0:
                    dve.wait_ge(mod_side[self.k % 2].sem, self.side_bias)
                    if self.k >= 2:
                        dve.wait_ge(mod_turned.sem, turns_before[self.k - 1])
                    if self.kind == "scale":
                        dve_s.chain(dve.tensor_scalar(first[0:1, :], first[0:1, :], 1.0, None, ALU.add))
                i = 4 * self.k + q
                u = ring["mod"][i]
                dve.wait_ge(w_landed[u % 4].sem, 16 * (u // 4 + 1))
                for j in range(2):
                    for r, (cond, c) in enumerate(self.conds):
                        ins = dve.scalar_tensor_tensor(out=self.acc[:, r], in0=w_raw[:, u % 4, j * HALF:(j + 1) * HALF],
                                                       scalar=c_act[:, cond, 2 * q + j, c:c + 1],
                                                       in1=first if q == 0 and j == 0 else self.acc[:, r], op0=ALU.mult, op1=ALU.add)
                        if j == 0 and r == len(self.conds) - 1:
                            dve_s.chain(ins)
                ins.then_inc(mod_unit.sem, 1)
                dve.wait_ge(mod_unit.sem, i + 1)
                if q == 3:
                    n = len(self.conds)
                    if self.gain is not None:
                        dve.wait_ge(mod_side[2].sem, self.side_gain)
                        dve.tensor_tensor(self.acc[:, 0:n], self.acc[:, 0:n], mod_gain[:, :].unsqueeze(1).to_broadcast([P, n, HALF]), ALU.mult)\
                           .then_inc(mod_summed.sem, 1)
                    else:
                        dve.drain().then_inc(mod_summed.sem, 1)

            def turn(self, pe):
                pe.wait_ge(mod_summed.sem, self.k + 1)
                for r in range(self.turns):
                    m = self.turn0 + r
                    if m >= 2:
                        pe.wait_ge(mod_kept.sem, m - 1)
                    if self.kind == "gate":
                        ins = pe.matmul(ps[:, 6 + m % 2, :], ones, self.acc[:, r], start=True, stop=True)
                    else:
                        for i in range(len(self.conds)):
                            for j in range(4):
                                ins = pe.matmul(ps[:, 6 + m % 2, 4 * i + j:4 * i + j + 1], self.acc[:, i, j * P:(j + 1) * P], ones[:, 0:1],
                                                start=True, stop=True)
                    ins.then_inc(mod_turned.sem, 1)

            def keep(self, act):
                for r in range(self.turns):
                    m = self.turn0 + r
                    act.wait_ge(mod_turned.sem, m + 1)
                    if self.kind == "gate":
                        ins = act.activation(gate_rows[:, self.targets[r], self.half * HALF:(self.half + 1) * HALF], ps[:, 6 + m % 2, :], ACT.Copy)
                    else:
                        n = len(self.conds)
                        ins = act.activation(mod_cols[:, self.targets[0], 4 * self.half:4 * self.half + 4, 0:n].rearrange("p j r -> p r j"),
                                             ps[:, 6 + m % 2, 0:4 * n].rearrange("p (r j) -> p r j", j=4), ACT.Copy)
                    ins.then_inc(mod_kept.sem, 1)

        def mod_jobs(w, bias, vectors, conds, acc):
            return [ModJob(w, bias, kind, gain, conds, targets, half, n * D + half * HALF, acc)
                    for n, kind, gain, targets in vectors for half in range(2)]

        class Modulation:

            def __init__(self, jobs):
                self.jobs = jobs

            def sync(self, sp):
                for job in self.jobs:
                    for q in range(4):
                        job.load(sp, q)

            def vector(self, dve):
                for job in self.jobs:
                    for q in range(4):
                        job.sum(dve, q)

            def tensor(self, pe):
                for job in self.jobs:
                    job.turn(pe)

            def scalar(self, act):
                for job in self.jobs:
                    job.keep(act)

            def gpsimd(self, pool):
                pass

        sq_ready, ms_ready, rstd_ready, xn_ready = (signal(n) for n in ("squares_ready", "meansq_ready", "rstd_ready", "xn_ready"))
        ht_turned, ht_high, ht_full, ht_low = (signal(n) for n in ("ht_turned", "ht_high", "ht_full", "ht_low"))

        def wait_features(pe, source, kt):
            pe.wait_ge(ht_low.sem, source.g0 + (kt + 1) * len(source.groups) // KT)

        def wait_bank(pe, source, bank):
            pe.wait_ge(source.bank_signal.sem, source.bank0 + len(source.groups) - 8 + bank + 1)

        class NormTransposed:
            def __init__(self, with_ctx, shift, scale, prime):
                self.prime = prime
                self.T = XT + (CT if with_ctx else 0)
                self.shift, self.scale = shift, scale
                self.q0, self.m0, self.r0 = sq_ready.plan(self.T), ms_ready.plan(1), rstd_ready.plan(1)
                self.x0 = xn_ready.plan(self.T)
                kinds = [(0, range(0, XT)), (1, range(XT, XT + CT))][:1 + with_ctx]
                self.groups = [(kt, r, tiles) for kt in range(KT) for r, tiles in kinds]
                self.g0 = ht_turned.plan(len(self.groups))
                for s in (ht_high, ht_low):
                    s.plan(len(self.groups))
                self.f0 = ht_full.plan(len(self.groups))
                self.bank_signal, self.bank0 = ht_full, self.f0

            def scalar(self, act):
                for t in range(self.T):
                    if t:
                        act.wait_ge(sq_ready.sem, self.q0 + t)
                    act.activation(junk[:, :], X[:, t, :], ACT.Square, accum_out=sumsq[:, t:t + 1]).then_inc(sq_ready.sem, 1)
                for _ in range(2):
                    weights_high(act, *self.prime)
                for g, (kt, r, tiles) in enumerate(self.groups):
                    n = len(tiles) * P
                    act.wait_ge(ht_full.sem, self.f0 + g + 1)
                    act.activation(HT[:, 0, kt, tiles[0] * P:tiles[0] * P + n], h_full[:, g % 2, 0:n], ACT.Copy).then_inc(ht_high.sem, 1)

            def vector(self, dve):
                dve.wait_ge(sq_ready.sem, self.q0 + self.T)
                dve.tensor_scalar(meansq[:, 0:self.T], sumsq[:, 0:self.T], 1.0 / D, EPS, ALU.mult, ALU.add).then_inc(ms_ready.sem, 1)
                dve.wait_ge(rstd_ready.sem, self.r0 + 1)
                for t in range(self.T):
                    dve.tensor_scalar(xn[:, t, :], X[:, t, :], rstd[:, t:t + 1], None, ALU.mult).then_inc(xn_ready.sem, 1)
                for g, (kt, r, tiles) in enumerate(self.groups):
                    n = len(tiles) * P
                    dve.wait_ge(ht_turned.sem, self.g0 + g + 1)
                    if g >= 2:
                        dve.wait_ge(ht_low.sem, self.g0 + g - 1)
                    dve.tensor_scalar(h_full[:, g % 2, 0:n], ps[:, g % 8, 0:n], mod_cols[:, self.scale, kt, r:r + 1],
                                      mod_cols[:, self.shift, kt, r:r + 1], ALU.mult, ALU.add).then_inc(ht_full.sem, 1)

            def gpsimd(self, pool):
                pool.wait_ge(ms_ready.sem, self.m0 + 1)
                pool.tensor_tensor(rstd[:, 0:self.T], meansq[:, 0:self.T], minus_half[:, 0:self.T], ALU.pow).then_inc(rstd_ready.sem, 1)
                for _ in range(2):
                    weights_low(pool, *self.prime)
                for g, (kt, r, tiles) in enumerate(self.groups):
                    n = len(tiles) * P
                    hi = HT[:, 0, kt, tiles[0] * P:tiles[0] * P + n]
                    pool.wait_ge(ht_full.sem, self.f0 + g + 1)
                    pool.wait_ge(ht_high.sem, self.g0 + g + 1)
                    pool.tensor_tensor(HT[:, 1, kt, tiles[0] * P:tiles[0] * P + n], h_full[:, g % 2, 0:n], hi.bitcast(F32),
                                       ALU.subtract).then_inc(ht_low.sem, 1)

            def tensor(self, pe):
                for g, (kt, r, tiles) in enumerate(self.groups):
                    if g >= 8:
                        pe.wait_ge(ht_full.sem, self.f0 + g - 7)
                    for i, t in enumerate(tiles):
                        if kt == 0:
                            pe.wait_ge(xn_ready.sem, self.x0 + t + 1)
                        ins = pe.transpose(ps[:, g % 8, i * P:(i + 1) * P], xn[:, t, kt * P:(kt + 1) * P], ident)
                    ins.then_inc(ht_turned.sem, 1)

            def sync(self, sp):
                pass

        class MixTransposed:
            prime = (2, HALF)

            def __init__(self, src, tiles):
                self.src = src
                kinds = [range(0, XT), range(XT, tiles)][:1 + (tiles > XT)]
                self.groups = [(kt, kind) for kt in range(KT) for kind in kinds]
                self.g0 = ht_turned.plan(len(self.groups))
                for s in (ht_high, ht_low):
                    s.plan(len(self.groups))
                self.bank_signal, self.bank0 = ht_low, self.g0

            def tensor(self, pe):
                for g, (kt, tiles) in enumerate(self.groups):
                    if g >= 8:
                        pe.wait_ge(ht_low.sem, self.g0 + g - 7)
                    for i, t in enumerate(tiles):
                        ins = pe.transpose(ps[:, g % 8, i * P:(i + 1) * P], self.src(t, kt), ident)
                    ins.then_inc(ht_turned.sem, 1)

            def scalar(self, act):
                for _ in range(2):
                    weights_high(act, *self.prime)
                for g, (kt, tiles) in enumerate(self.groups):
                    n = len(tiles) * P
                    act.wait_ge(ht_turned.sem, self.g0 + g + 1)
                    act.activation(HT[:, 0, kt, tiles[0] * P:tiles[0] * P + n], ps[:, g % 8, 0:n], ACT.Copy).then_inc(ht_high.sem, 1)

            def vector(self, dve):
                for g, (kt, tiles) in enumerate(self.groups):
                    n = len(tiles) * P
                    dve.wait_ge(ht_high.sem, self.g0 + g + 1)
                    dve.tensor_tensor(HT[:, 1, kt, tiles[0] * P:tiles[0] * P + n], ps[:, g % 8, 0:n],
                                      HT[:, 0, kt, tiles[0] * P:tiles[0] * P + n].bitcast(F32), ALU.subtract).then_inc(ht_low.sem, 1)

            def gpsimd(self, pool):
                for _ in range(2):
                    weights_low(pool, *self.prime)

            def sync(self, sp):
                pass

        acc_ready, acc_free = signal("acc_ready"), signal("acc_free")

        class Linear:

            def __init__(self, w, chunks, dst, mods=()):
                self.w, self.chunks, self.dst = w, chunks, dst
                self.mods = list(mods) + [[]] * (len(chunks) - len(mods))
                self.a0 = acc_ready.plan(sum(len(t) - 1 for _, _, t in chunks))
                self.f0 = acc_free.plan(sum(len(t) for _, _, t in chunks))
                self.w0 = w_used.plan(4 * len(chunks))
                self.source = schedule[-1]
                self.beside = {"dve": {}, "act": {}, "pool": {}}

            def wait_copied(self, eng, c):
                eng.wait_ge(acc_free.sem, self.f0 + sum(len(t) for _, _, t in self.chunks[:c + 1]))

            def sync(self, sp):
                for (c0, n, tiles), jobs in zip(self.chunks, self.mods):
                    for q in range(4):
                        weights_load(sp, self.w[q * 256:(q + 1) * 256, c0:c0 + n], 2, n)
                        if len(jobs) == 1:
                            jobs[0].load(sp, q)
                        if len(jobs) == 2:
                            jobs[q // 2].load(sp, 2 * (q % 2))
                            jobs[q // 2].load(sp, 2 * (q % 2) + 1)

            def scalar(self, act):
                before = []
                for c, ((c0, n, tiles), jobs) in enumerate(zip(self.chunks, self.mods)):
                    steps = self.beside["act"].get(c, [])
                    for q in range(4):
                        if c or q >= 2:
                            weights_high(act, 2, n)
                        if q < len(steps):
                            steps[q](act)
                        if q == 1:
                            for job in before:
                                job.keep(act)
                    before = jobs
                for job in before:
                    job.keep(act)
                for step in self.beside["act"].get(len(self.chunks), []):
                    step(act)

            def gpsimd(self, pool):
                for c, (c0, n, tiles) in enumerate(self.chunks):
                    steps = self.beside["pool"].get(c, [])
                    for q in range(4):
                        if c or q >= 2:
                            weights_low(pool, 2, n)
                        if q < len(steps):
                            steps[q](pool)

            def tensor(self, pe):
                first = 0
                for (c0, n, tiles), jobs in zip(self.chunks, self.mods):
                    for q in range(4):
                        w = weights_use(pe, 2, n)
                        for i, t in enumerate(tiles, first):
                            if q == 0 and i >= 6:
                                pe.wait_ge(acc_free.sem, self.f0 + i - 5)
                            elif q == 0:
                                wait_bank(pe, self.source, i)
                            for j in range(2):
                                kt = 2 * q + j
                                if first == 0 and i == 0:
                                    wait_features(pe, self.source, kt)
                                ins = matmul3(pe, ps[:, i % 6, 0:n], [HT[:, s, kt, t * P:(t + 1) * P] for s in range(2)],
                                              [w[s][:, j, :] for s in range(2)], start=(kt == 0), stop=(kt == KT - 1))
                            if q == 3 and t != tiles[-1]:
                                ins.then_inc(acc_ready.sem, 1)
                        ins.then_inc(w_used.sem, 1)
                    if first == 0 and jobs:
                        wait_bank(pe, self.source, 6)
                        wait_bank(pe, self.source, 7)
                    first += len(tiles)
                    for job in jobs:
                        job.turn(pe)

            def vector(self, dve):
                i = ready = 0
                for c, ((c0, n, tiles), jobs) in enumerate(zip(self.chunks, self.mods)):
                    for job in jobs:
                        for q in range(4):
                            job.sum(dve, q)
                    for step in self.beside["dve"].get(c, []):
                        step(dve)
                    for t in tiles:
                        if t != tiles[-1]:
                            ready += 1
                            dve.wait_ge(acc_ready.sem, self.a0 + ready)
                        else:
                            dve.wait_ge(w_used.sem, self.w0 + 4 * (c + 1))
                        dve.tensor_copy(self.dst(t, c0, n), ps[:, i % 6, 0:n]).then_inc(acc_free.sem, 1)
                        i += 1

        y_gated = signal("y_gated")

        class Residual:
            def __init__(self, gates):
                self.gates, self.T = gates, len(gates)
                self.q0, self.m0, self.r0 = sq_ready.plan(self.T), ms_ready.plan(1), rstd_ready.plan(1)
                self.y0 = y_gated.plan(self.T)

            def scalar(self, act):
                for t in range(self.T):
                    if t:
                        act.wait_ge(sq_ready.sem, self.q0 + t)
                    act.activation(res_junk[:, :], Y[:, t, :], ACT.Square, accum_out=sumsq[:, t:t + 1]).then_inc(sq_ready.sem, 1)

            def gpsimd(self, pool):
                pool.wait_ge(ms_ready.sem, self.m0 + 1)
                pool.tensor_tensor(rstd[:, 0:self.T], meansq[:, 0:self.T], minus_half[:, 0:self.T], ALU.pow).then_inc(rstd_ready.sem, 1)
                for t in range(1, self.T, 3):
                    pool.wait_ge(y_gated.sem, self.y0 + t + 1)
                    pool.tensor_tensor(X[:, t, :], X[:, t, :], Y[:, t, :], ALU.add)

            def vector(self, dve):
                dve.wait_ge(sq_ready.sem, self.q0 + self.T)
                dve.tensor_scalar(meansq[:, 0:self.T], sumsq[:, 0:self.T], 1.0 / D, EPS, ALU.mult, ALU.add).then_inc(ms_ready.sem, 1)
                dve.wait_ge(rstd_ready.sem, self.r0 + 1)
                for t, g in enumerate(self.gates):
                    dve.scalar_tensor_tensor(out=Y[:, t, :], in0=Y[:, t, :], scalar=rstd[:, t:t + 1], in1=gate_rows[:, g, :],
                                             op0=ALU.mult, op1=ALU.mult).then_inc(y_gated.sem, 1)
                for t in range(self.T):
                    if t % 3 != 1:
                        dve.wait_ge(y_gated.sem, self.y0 + t + 1)
                        dve.tensor_tensor(X[:, t, :], X[:, t, :], Y[:, t, :], ALU.add)

            def tensor(self, pe):
                pass

            def sync(self, sp):
                pass

        s_scored, s_max, s_exp, s_turned, s_kept_a, s_kept_v, s_summed, s_out = (signal("att_" + n) for n in (
            "scored", "max", "exp", "turned", "kept_act", "kept_dve", "summed", "out"))

        class Attention:

            def __init__(self, units, probs, probs_t, stats, neg_sinks=None, sinks=None, neg_lambda=None):
                self.units, self.probs, self.probs_t, self.stats = units, probs, probs_t, stats
                self.neg_sinks, self.sinks, self.neg_lambda = neg_sinks, sinks, neg_lambda
                n = len(units)
                self.b = {s: s.plan(n) for s in (s_scored, s_max, s_exp, s_turned, s_summed, s_out)}
                self.ka = s_kept_a.plan((n + 1) // 2)
                self.kv = s_kept_v.plan(n // 2)

            def wait(self, eng, s, count):
                if count > 0:
                    eng.wait_ge(s.sem, self.b[s] + count)

            def wait_kept(self, eng, u):
                if u >= 0:
                    s, before = ((s_kept_a, self.ka), (s_kept_v, self.kv))[u % 2]
                    eng.wait_ge(s.sem, before + u // 2 + 1)

            def scores(self, u):
                return ps[:, 2 * (u % 2):2 * (u % 2) + 2, :].rearrange("p b n -> p (b n)")

            def tensor(self, pe):
                n = len(self.units)
                for step in range(n + 3):
                    u = step
                    if u < n:
                        un, sc = self.units[u], self.scores(u)
                        self.wait(pe, s_exp, u - 1)
                        for bank in range(2):
                            for k, c in [(k, c) for k, c in un["keys"] if c // HALF == bank]:
                                masks = [(m, mc) for m, mc in un["mask"] if c <= mc < c + k.shape[1]]
                                ins = pe.matmul(sc[:, c:c + k.shape[1]], un["q"], k, start=True, stop=not masks)
                                for m, mc in masks:
                                    ins = pe.matmul(sc[:, mc:mc + P], identb[:, :], m, start=False, stop=(mc == masks[-1][1]))
                        ins.then_inc(s_scored.sem, 1)
                    u = step - 2
                    if 0 <= u < n:
                        blocks = len(self.units[u]["values"])
                        self.wait(pe, s_exp, u + 1)
                        self.wait_kept(pe, u - 1)
                        for b in range(blocks):
                            ins = pe.transpose(ps[:, 4 + b // 4, (b % 4) * P:(b % 4 + 1) * P],
                                               self.probs[:, u % 2, b * P:(b + 1) * P], ident)
                        ins.then_inc(s_turned.sem, 1)
                    u = step - 3
                    if 0 <= u < n:
                        vals = self.units[u]["values"]
                        self.wait_kept(pe, u)
                        self.wait(pe, s_out, u - 1)
                        for b, v in enumerate(vals):
                            ins = pe.matmul(ps[:, 6 + u % 2, 0:v.shape[1]], self.probs_t[:, u % 2, b * P:(b + 1) * P], v,
                                            start=(b == 0), stop=(b == len(vals) - 1))
                        ins.then_inc(s_summed.sem, 1)

            def copy_probs(self, eng, act, u, sig):
                w = len(self.units[u]["values"]) * P
                eng.wait_ge(s_turned.sem, self.b[s_turned] + u + 1)
                self.wait(eng, s_summed, u - 1)
                src = ps[:, 4:6, :].rearrange("p b n -> p (b n)")[:, 0:w]
                dst = self.probs_t[:, u % 2, 0:w]
                (eng.activation(dst, src, ACT.Copy) if act else eng.tensor_copy(dst, src)).then_inc(sig.sem, 1)

            def scalar(self, act):
                n, st = len(self.units), self.stats
                for step in range(n + 2):
                    u = step
                    if u < n:
                        un = self.units[u]
                        w, r = len(un["values"]) * P, u % 4
                        act.wait_ge(s_max.sem, self.b[s_max] + u + 1)
                        self.wait(act, s_turned, u - 1)
                        if u >= 4:
                            self.wait(act, s_out, u - 3)
                        ins = act.activation(self.probs[:, u % 2, 0:w], self.scores(u)[:, 0:w], ACT.Exp, bias=st[:, 1, r:r + 1],
                                             scale=un["scale"], accum_out=st[:, 2, r:r + 1])
                        if un["sink"] is not None:
                            h = un["sink"]
                            ins = act.activation(st[:, 3, r:r + 1], st[:, 1, r:r + 1], ACT.Exp, bias=self.sinks[:, h:h + 1])
                        ins.then_inc(s_exp.sem, 1)
                    u = step - 2
                    if 0 <= u < n and u % 2 == 0:
                        self.copy_probs(act, True, u, s_kept_a)

            def vector(self, dve):
                n, st = len(self.units), self.stats
                for step in range(n + 3):
                    u = step
                    if u < n:
                        un = self.units[u]
                        w, r = len(un["values"]) * P, u % 4
                        dve.wait_ge(s_scored.sem, self.b[s_scored] + u + 1)
                        dve_s.chain(dve.tensor_reduce(st[:, 0, r:r + 1], self.scores(u)[:, 0:w], AX, ALU.max))
                        if un["sink"] is not None:
                            h = un["sink"]
                            ins = dve.tensor_scalar(st[:, 1, r:r + 1], st[:, 0, r:r + 1], -un["scale"], self.neg_sinks[:, h:h + 1],
                                                    ALU.mult, ALU.min)
                        else:
                            ins = dve.tensor_scalar(st[:, 1, r:r + 1], st[:, 0, r:r + 1], -un["scale"], None, ALU.mult)
                        ins.then_inc(s_max.sem, 1)
                    u = step - 2
                    if 0 <= u < n and u % 2 == 1:
                        self.copy_probs(dve, False, u, s_kept_v)
                    u = step - 3
                    if 0 <= u < n:
                        un = self.units[u]
                        r, dv = u % 4, un["values"][0].shape[1]
                        total, inv = st[:, 2, r:r + 1], st[:, 5, r:r + 1]
                        dve.wait_ge(s_exp.sem, self.b[s_exp] + u + 1)
                        if un["sink"] is not None:
                            dve_s.chain(dve.tensor_tensor(st[:, 4, r:r + 1], total, st[:, 3, r:r + 1], ALU.add))
                            total = st[:, 4, r:r + 1]
                        dve_s.chain(dve.reciprocal(inv, total))
                        kind, dst, other = un["finish"]
                        if kind == "minus_lambda":
                            dve_s.chain(dve.tensor_tensor(st[:, 6, r:r + 1], inv, self.neg_lambda, ALU.mult))
                            inv = st[:, 6, r:r + 1]
                        dve.wait_ge(s_summed.sem, self.b[s_summed] + u + 1)
                        o = ps[:, 6 + u % 2, 0:dv]
                        if kind == "plain":
                            ins = dve.tensor_scalar(dst, o, inv, None, ALU.mult)
                        else:
                            op = ALU.mult if kind == "gated" else ALU.add
                            if kind == "minus_lambda":
                                dve.wait_ge(s_out.sem, self.b[s_out] + u)
                            ins = dve.scalar_tensor_tensor(out=dst, in0=o, scalar=inv, in1=other, op0=ALU.mult, op1=op)
                        ins.then_inc(s_out.sem, 1)

            def gpsimd(self, pool):
                pass

            def sync(self, sp):
                pass

        def rotate(eng, steps, dst, src, cos, sin, heads, groups, half, tmp):
            w = groups * 2 * half
            v = lambda z: z.rearrange("p (h w) -> p h w", w=w)
            cb = cos.unsqueeze(1).to_broadcast([P, heads, w])
            full = lambda z: z.rearrange("p (h g s d) -> p h g s d", g=groups, s=2, d=half)
            sb_ = sin.rearrange("p (g s d) -> p g s d", s=2, d=half)
            n = heads * w
            for s in range(2):
                sc = sb_[:, :, s, :].unsqueeze(1).to_broadcast([P, heads, groups, half])
                a_, b_ = full(tmp[:, 0:n])[:, :, :, s, :], full(src)[:, :, :, 1 - s, :]
                ins = eng.tensor_tensor(a_, b_, sc, ALU.mult)
            steps.chain(ins)
            steps.chain(eng.tensor_tensor(v(dst), v(src), cb, ALU.mult))
            return eng.tensor_tensor(dst, dst, tmp[:, 0:n], ALU.add)

        made, kept_a, kept_v = signal("piece_made"), signal("piece_kept_act"), signal("piece_kept_dve")

        def turn(srcs):
            return [("turn", s.shape[1], i * P, s) for i, s in enumerate(srcs)]

        class Pieces:

            def __init__(self, groups, pool=None):
                self.groups, self.pool = groups, pool
                self.t0 = made.plan(len(groups))
                self.kept = []
                free = 0
                for g in groups:
                    if "mask" in g or free % 2:
                        s = kept_v
                    else:
                        s = kept_a
                    free += "mask" not in g
                    self.kept.append((s, s.plan(1) + 1))

            def tensor(self, pe):
                for g, group in enumerate(self.groups):
                    if g >= 8:
                        sig, count = self.kept[g - 8]
                        pe.wait_ge(sig.sem, count)
                    b = g % 8
                    for op in group["ops"]:
                        if op[0] == "turn":
                            _, m, col, src = op
                            ins = pe.transpose(ps[0:m, b, col:col + P], src, ident)
                        else:
                            _, (p0, p1), col, n, pairs = op[:5]
                            first, last = op[5] if len(op) > 5 else (True, True)
                            for i, (l, r) in enumerate(pairs):
                                ins = pe.matmul(ps[p0:p1, b, col:col + n], l, r, start=(i == 0 and first),
                                                stop=(i == len(pairs) - 1 and last), skip_group_check=len(op) > 5)
                    ins.then_inc(made.sem, 1)

            def keep(self, eng, sig):
                for g, group in enumerate(self.groups):
                    if self.kept[g][0] is not sig:
                        continue
                    eng.wait_ge(made.sem, self.t0 + g + 1)
                    for p0, p1, dst in group["dsts"]:
                        n = int(np.prod(dst.shape[1:]))
                        src = ps[p0:p1, g % 8, 0:n]
                        if len(dst.shape) == 3:
                            src = src.rearrange("p (a b) -> p a b", b=dst.shape[2])
                        if "mask" in group:
                            ins = eng.tensor_tensor(dst, src, group["mask"], ALU.mult)
                        elif sig is kept_a:
                            ins = eng.activation(dst, src, ACT.Copy, scale=group.get("scale", 1.0))
                        elif "scale" in group:
                            ins = eng.tensor_scalar(dst, src, group["scale"], None, ALU.mult)
                        else:
                            ins = eng.tensor_copy(dst, src)
                    ins.then_inc(sig.sem, 1)

            def scalar(self, act):
                self.keep(act, kept_a)

            def vector(self, dve):
                self.keep(dve, kept_v)

            def gpsimd(self, pool):
                if self.pool:
                    self.pool(pool)

            def sync(self, sp):
                pass

        class Work:

            def __init__(self, act=None, dve=None, pool=None, sp=None):
                none = lambda eng: None
                self.scalar, self.vector, self.gpsimd, self.sync = act or none, dve or none, pool or none, sp or none

            def tensor(self, pe):
                pass

        f_silu, f_full, f_high, f_low = (signal("ffn_" + n) for n in ("silu", "full", "high", "low"))
        f_out, f_added = signal("ffn_out_ready"), signal("ffn_out_added")
        GROUP = 256
        GROUPS = FFN // GROUP
        silu_t = at("ffn_silu", [P, 2, TOK], F32, aux_at)
        full_t = at("ffn_full", [P, 2, TOK], F32, aux_at + 2 * TOK * 4)

        class FeedForward:

            def __init__(self, w_in, w_out, tiles, mods=((), (), (), ())):
                self.w_in, self.w_out, self.T = w_in, w_out, tiles
                self.mods = mods
                self.source = schedule[-1]
                self.segs = [(0, HALF)] if tiles == XT else [(0, 384), (384, 384)]
                self.parts = [range(i, min(i + 3, GROUPS)) for i in range(0, GROUPS, 3)]
                self.b = {s: s.plan(n) for s, n in ((f_silu, GROUPS), (f_full, 2 * GROUPS), (f_high, 2 * GROUPS), (f_low, 2 * GROUPS),
                                                    (f_out, len(self.parts) * 2 * (tiles - 1)), (f_added, len(self.parts) * 2 * tiles))}
                self.w0 = w_used.plan(6 * GROUPS)
                self.gate_unit, self.up_unit, self.out_unit, u = {}, {}, {}, 0
                for p, part in enumerate(self.parts):
                    for g in part:
                        self.gate_unit[g], self.up_unit[g] = self.w0 + u + 2, self.w0 + u + 4
                        u += 4
                    for h in range(2):
                        u += len(part)
                        self.out_unit[p, h] = self.w0 + u

            def wait(self, eng, s, n):
                if n > 0:
                    eng.wait_ge(s.sem, self.b[s] + n)

            def mod_units(self, p):
                return [(job, q) for job in self.mods[p] for q in range(4)]

            def sync(self, sp):
                for p, part in enumerate(self.parts):
                    units = self.mod_units(p)
                    for g in part:
                        for off in (0, FFN):
                            for half in range(2):
                                weights_load(sp, self.w_in[half * HALF:(half + 1) * HALF, off + g * GROUP:off + (g + 1) * GROUP], 4, GROUP)
                                for _ in range(0 if off and half else 2 if len(part) == 2 and not (off or half) else 1):
                                    if units:
                                        job, q = units.pop(0)
                                        job.load(sp, q)
                    for n in range(2):
                        for g in part:
                            weights_load(sp, self.w_out[g * GROUP:(g + 1) * GROUP, n * HALF:(n + 1) * HALF], 2, HALF)

            def split_hidden(self, eng, g, act):
                n, lane = self.T * P, g % 3
                for a in range(2):
                    full = full_t[:, a, 0:n]
                    high, low = (act_t[:, s, 2 * lane + a, 0:n] for s in range(2))
                    self.wait(eng, f_full, 2 * g + a + 1)
                    if act:
                        eng.activation(high, full, ACT.Copy).then_inc(f_high.sem, 1)
                    else:
                        self.wait(eng, f_high, 2 * g + a + 1)
                        eng.tensor_tensor(low, full, high.bitcast(F32), ALU.subtract).then_inc(f_low.sem, 1)

            def scalar(self, act):
                n, before = self.T * P, None
                w, k = self.segs[0][1], len(self.segs)
                for p, part in enumerate(self.parts):
                    for g in part:
                        if g:
                            weights_high(act, 4, GROUP)
                            weights_high(act, 4, GROUP)
                        if before is not None:
                            self.split_hidden(act, before, True)
                        weights_high(act, 4, GROUP)
                        weights_high(act, 4, GROUP)
                        act.wait_ge(w_used.sem, self.gate_unit[g])
                        self.wait(act, f_full, 2 * g)
                        for a in range(2):
                            ins = act.activation(silu_t[:, a, 0:n].rearrange("p (s w) -> p s w", w=w), ps[:, a * k:(a + 1) * k, 0:w], ACT.Silu)
                        ins.then_inc(f_silu.sem, 1)
                        before = g
                    for i in range(2 * len(part)):
                        weights_high(act, 2, HALF)
                        if i == 1:
                            self.split_hidden(act, before, True)
                            before = None
                        if i == len(part) + 1:
                            for job in self.mods[p]:
                                job.keep(act)

            def gpsimd(self, pool):
                before = None
                for part in self.parts:
                    for g in part:
                        if g:
                            weights_low(pool, 4, GROUP)
                            weights_low(pool, 4, GROUP)
                        if before is not None:
                            self.split_hidden(pool, before, False)
                        weights_low(pool, 4, GROUP)
                        weights_low(pool, 4, GROUP)
                        before = g
                    for i in range(2 * len(part)):
                        weights_low(pool, 2, HALF)
                        if i == 1:
                            self.split_hidden(pool, before, False)
                            before = None

            def vector(self, dve):
                w, k, i = self.segs[0][1], len(self.segs), 0
                n = self.T * P
                for p, part in enumerate(self.parts):
                    units = self.mod_units(p)
                    for g in part:
                        for _ in range(3 if len(part) == 3 else 4):
                            if units:
                                job, q = units.pop(0)
                                job.sum(dve, q)
                        self.wait(dve, f_silu, g + 1)
                        dve.wait_ge(w_used.sem, self.up_unit[g])
                        self.wait(dve, f_low, 2 * g)
                        for a in range(2):
                            view = lambda z: z[:, a, 0:n].rearrange("p (s w) -> p s w", w=w)
                            dve.tensor_tensor(view(full_t), ps[:, 4 + a * k:4 + (a + 1) * k, 0:w], view(silu_t), ALU.mult)\
                               .then_inc(f_full.sem, 1)
                    for h in range(2):
                        for t in range(self.T):
                            i += 1
                            y = Y[:, t, h * HALF:(h + 1) * HALF]
                            if t < self.T - 1:
                                self.wait(dve, f_out, i - (2 * p + h))
                            else:
                                dve.wait_ge(w_used.sem, self.out_unit[p, h])
                            if p == 0:
                                ins = dve.tensor_copy(y, ps[:, t, :])
                            else:
                                self.wait(dve, f_added, i - 2 * self.T)
                                ins = dve.tensor_tensor(y, y, ps[:, t, :], ALU.add)
                            ins.then_inc(f_added.sem, 1)

            def tensor(self, pe):
                k, i = len(self.segs), 0
                for p, part in enumerate(self.parts):
                    for g in part:
                        for what, free in ((0, f_silu), (4, f_full)):
                            for half in range(2):
                                w = weights_use(pe, 4, GROUP)
                                if half == 0:
                                    self.wait(pe, free, g if free is f_silu else 2 * g)
                                    if what and p and g == part[0] and self.mods[p - 1]:
                                        job = self.mods[p - 1][-1]
                                        pe.wait_ge(mod_kept.sem, job.turn0 + job.turns)
                                for a in range(2):
                                    for s, (c0, n) in enumerate(self.segs):
                                        bank = what + a * k + s
                                        if half == 0 and p and g == part[0] and bank < self.T:
                                            self.wait(pe, f_added, i - self.T + bank + 1)
                                        if g == 0 and half == 0:
                                            wait_bank(pe, self.source, bank)
                                        for j in range(4):
                                            kt = 4 * half + j
                                            if g == 0 and what == 0 and a == 0 and s == 0:
                                                wait_features(pe, self.source, kt)
                                            ins = matmul3(pe, ps[:, bank, 0:n], [z[:, j, a * P:(a + 1) * P] for z in w],
                                                          [HT[:, z, kt, c0:c0 + n] for z in range(2)], kt == 0, kt == KT - 1)
                                ins.then_inc(w_used.sem, 1)
                    for h in range(2):
                        for m, g in enumerate(part):
                            w = weights_use(pe, 2, HALF)
                            self.wait(pe, f_low, 2 * g + 2)
                            for t in range(self.T):
                                if m == 0 and h:
                                    self.wait(pe, f_added, i - self.T + t + 1)
                                elif m == 0 and t in (0, 4):
                                    self.wait(pe, f_silu, part[-1] + 1) if t == 0 else self.wait(pe, f_full, 2 * part[-1] + 2)
                                for j in range(2):
                                    lane = 2 * (g % 3) + j
                                    ins = matmul3(pe, ps[:, t, :], [act_t[:, z, lane, t * P:(t + 1) * P] for z in range(2)],
                                                  [z[:, j, :] for z in w], m == 0 and j == 0, m == len(part) - 1 and j == 1)
                                if m == len(part) - 1 and t < self.T - 1:
                                    ins.then_inc(f_out.sem, 1)
                            ins.then_inc(w_used.sem, 1)
                        i += self.T
                        if h == 0:
                            for job in self.mods[p]:
                                job.turn(pe)

        def heads_view(z, h):
            return z.rearrange("p (h d) -> p h d", h=h)

        c1 = np.float32(6.28125)
        c2 = np.float32(np.round((2 * math.pi - 6.28125) * 2 ** 19) / 2 ** 19)
        c3 = np.float32(np.round((2 * math.pi - float(c1) - float(c2)) * 2 ** 31) / 2 ** 31)
        c4 = np.float32(2 * math.pi - float(c1) - float(c2) - float(c3))
        MAGIC = 1.5 * 2.0 ** 23

        take = region(arena)
        P1 = take("proj_one", [P, XT, IN1])
        cos1 = take("cos_one", [P, XT, 2, 64])
        sin1 = take("sin_one", [P, XT, 2, 64])
        rope_tmp_one = take("rope_tmp_one", [P, 640])
        take = region(aux_at)
        gqT, gkT = take("gla_q_t", [P, S]), take("gla_k_t", [P, S])
        gaT = take("gla_a_t", [16, S])
        one_end = take.where[0]
        con1 = at("constants_one", [P, ONE_W], F32, gate_rows_at + 4 * D)
        assert ONE_W * 4 <= 3 * 4 * D
        c1t = lambda name: con1[:, slice(*ONE_COLS[name])]
        small = region(small_at)
        pos_i, pos_f = small("positions_int", [P, XT], I32), small("positions", [P, XT])
        sinks = small("sinks", [P, 8])
        neg_sinks = small("neg_sinks", [P, 8])
        stats = small("attention_stats", [P, 7, 4])
        gate_w = small("gla_gate_w", [16, P])
        gate_b = small("gla_gate_b", [P, 1])
        gla_gain = small("gla_gain", [P, 64])
        headsq = small("head_squares", [P, 64])
        headms = small("head_meansq", [P, 64])
        headr = small("head_rstd", [P, 64])
        half64 = small("minus_half64", [P, 64])
        gla_decay = small("gla_chunk_decay", [P, 8])
        qn_col = small("latent_q_gain", [P, 2])
        kvn_col = small("latent_kv_gain", [P, 1])
        qk_gain = small("qk_gain", [P, 2, 64])
        sub_gain = small("sub_gain", [P, P])
        lam_in = small("lambda_in", [P, 4, 64])
        lam_prod = small("lambda_products", [P, 2, 64])
        lam_sum = small("lambda_sums", [P, 2])
        neg_lam = small("neg_lambda", [P, 1])
        assert small.where[0] <= small_at + SMALL, small.where[0] - small_at
        take = region(ht_at)
        angle = take("angle", [P, XT, 2, 64])
        turns = take("turns", [P, XT, 2, 64])
        reduced = take("reduced", [P, 2, XT, 2, 64])
        take = region(ht_at)
        qT, kT = take("att_q_t", [P, 4, S]), take("att_k_t", [P, 2, 2, S])
        probs1, probs1_t = take("att_probs_one", [P, 2, 2 * P]), take("att_probs_t_one", [P, 2, 2 * P])
        qrT, krT, qdT = take("ret_q_t", [P, 2, S]), take("ret_k_t", [P, 2, S]), take("ret_qdecay_t", [P, 2, S])
        ret_k = take("ret_k_decayed", [P, XT, 256])
        ret_a = at("ret_scores_t", [P, XT, 2, 256], F32, ht_at)
        ret_u = take("ret_updates", [P, XT, 2, P])
        ret_s = take("ret_states", [P, XT, 2, P])
        assert take.where[0] <= ht_end
        rope_tmp_v = at("rope_tmp_dve", [P, 1024], F32, ht_at)
        rope_tmp_p = at("rope_tmp_pool", [P, 1024], F32, ht_at + 4096)
        take = region(ht_at)
        B = take("gla_log_decay_sums", [P, S])
        gla_a = take("gla_scores_t", [P, 4, S])
        g_dist, g_exp = take("gla_distance", [P, 2, S]), take("gla_factor", [P, 2, S])
        g_q, g_k = take("gla_q_level", [P, 2, S]), take("gla_k_level", [P, 2, S])
        g_kd, g_kdt, g_qe = take("gla_k_decayed_t", [P, S]), take("gla_k_decayed", [P, XT, P]), take("gla_q_decayed_t", [P, S])
        gla_u = take("gla_updates", [P, 8, 256])
        assert take.where[0] <= ht_end
        gla_s = at("gla_states", [P, 8, 256], F32, ht_at + 4 * (S + 4 * S))
        z_t, z_abs, z_min, z_exp = (g_q[:, 0], g_q[:, 1], g_k[:, 0], g_k[:, 1])
        log_a, log_a_tok = g_kd[:, :], g_kdt

        def tok(t):
            return slice(t * P, (t + 1) * P)

        schedule = []

        def setup_phases():
            n_loads = [0]
            loads = [
                (con[:, :], a["static"]), (con1[:, :], a["one"]),
                (X[:, 0:XT, :], a["x"][0].rearrange("(t p) d -> p t d", p=P)),
                (X[:, XT:, :], a["ctx_2"][0].rearrange("(t p) d -> p t d", p=P)),
                (c_raw[:, 0, :], a["c"][0].rearrange("(k p) -> p k", p=P)),
                (c_raw[:, 1, :], a["c_2"][0].rearrange("(k p) -> p k", p=P)),
                (c_raw[:, 2, :], a["c_ctx_2"].rearrange("(k p) -> p k", p=P)),
                (pos_i[:, :], a["positions"][0].rearrange("(t p) -> p t", p=P)),
            ]
            total = load_in.plan(16 * len(loads)) + 16 * len(loads)

            def sp(eng):
                for dst, src in loads:
                    eng.dma_start(dst, src, allow_slow_non_contiguous=True).then_inc(load_in.sem, 16)

            def act(eng):
                eng.wait_ge(load_in.sem, total)
                for cond, r, raw in ((0, 0, 0), (0, 1, 0), (1, 0, 1), (1, 1, 2)):
                    eng.activation(c_act[:, cond, :, r], c_raw[:, raw, :], ACT.Silu)

            def dve(eng):
                eng.memset(minus_half[:, :], -0.5)
                eng.memset(half64[:, :], -0.5)
                eng.memset(mod_bias[:, :, :].rearrange("p b n -> p (b n)"), 0.0).then_inc(mod_ready.sem, 1)
                eng.memset(headsq[:, :], 1.0)
                eng.memset(headms[:, :], 1.0)
                eng.wait_ge(load_in.sem, total)
                eng.tensor_copy(identb[:, :], ident)
                eng.tensor_copy(window[:, :], c1t("window"))
                dve_s.chain(eng.tensor_copy(pos_f[:, :], pos_i[:, :]))
                f = c1t("freqs").rearrange("p (k n) -> p k n", k=2)
                for t in range(XT):
                    ins = eng.tensor_scalar(angle[:, t], f, pos_f[:, t:t + 1], None, ALU.mult)
                dve_s.chain(ins)
                for which, quarter in ((0, 0.0), (1, 0.25)):
                    r = reduced[:, which]
                    dve_s.chain(eng.tensor_scalar(turns[:], angle[:], 1.0 / (2 * math.pi), quarter, ALU.mult, ALU.add))
                    dve_s.chain(eng.tensor_scalar(turns[:], turns[:], MAGIC, None, ALU.add))
                    dve_s.chain(eng.tensor_scalar(turns[:], turns[:], MAGIC, None, ALU.subtract))
                    flat = lambda z: z.rearrange("p t k n -> p (t k n)")
                    for i, part in enumerate((c1, c2, c3, c4)):
                        dve_s.chain(eng.scalar_tensor_tensor(out=flat(r), in0=flat(turns[:]), scalar=-float(part),
                                                             in1=flat(angle[:] if i == 0 else r), op0=ALU.mult, op1=ALU.add))
                    dve_s.chain(eng.tensor_scalar(r, r, math.pi / 2 * which, 3.1415925, ALU.add, ALU.min))
                    dve_s.chain(eng.tensor_scalar(r, r, -3.1415925, None, ALU.max))

            schedule.append(Work(act=act, dve=dve, sp=sp))

            def sines(eng):
                eng.activation(cos1[:], reduced[:, 1], ACT.Sin)
                for s, sign in ((0, -1.0), (1, 1.0)):
                    eng.activation(sin1[:, :, :, 32 * s:32 * s + 32], reduced[:, 0, :, :, 32 * s:32 * s + 32], ACT.Sin, scale=sign)

            schedule.append(Work(act=sines))
            schedule.append(Modulation(mods_one(0, [(0, "shift", None, [0]), (1, "scale", a["pre_norm_gain"][0], [1])])))

        def clear_other_head(eng, keys):
            eng.memset(keys[64:P, :, 0, :], 0.0)
            eng.memset(keys[0:64, :, 1, :], 0.0)

        def key_runs(blocks):
            runs = []
            for i, b in enumerate(blocks):
                if runs and runs[-1][0] + runs[-1][1] == b and i % 4:
                    runs[-1][1] += 1
                else:
                    runs.append([b, 1, i * P])
            return runs

        def mods_one(l, vectors):
            return mod_jobs(a["w_mod"][l], a["b_mod"][l], vectors, [(0, 0)], mod_acc_aux)

        def mods_two(l, vectors, conds, acc=mod_acc_aux):
            return mod_jobs(a["ada_w_2"][l], a["ada_b_2"][l], vectors, [(1, 0), (1, 1)][:conds], acc)

        def layer_one(l):
            small_loads = [
                (sinks[:, :], a["attn_sinks"][l].partition_broadcast(P)), (gate_w[:, :], a["gla_gate_w"][l]),
                (gate_b[:, :], a["gla_gate_b"][l].rearrange("(p o) -> p o", o=1)),
                (gla_gain[:, :], a["gla_norm_gain"][l].partition_broadcast(P)),
            ]
            loaded = load_in.plan(16 * len(small_loads)) + 16 * len(small_loads)
            barrier = len(schedule)

            def sp(eng):
                if barrier:
                    sp_waits_phase(eng, barrier)
                for dst, src in small_loads:
                    eng.dma_start(dst, src, allow_slow_non_contiguous=True).then_inc(load_in.sem, 16)

            def dve(eng):
                eng.wait_ge(load_in.sem, loaded)
                eng.tensor_scalar(neg_sinks[:, :], sinks[:, :], -1.0, None, ALU.mult)

            schedule.append(Work(sp=sp, dve=dve))
            schedule.append(NormTransposed(False, 4 * l, 4 * l + 1, (2, HALF)))
            starts = [0, 512, 1024, 1536, 2048, 2560, IN1 - 256, IN1]
            chunks = [(c0, c1 - c0, range(XT)) for c0, c1 in zip(starts, starts[1:])]
            gates = mods_one(l, [(2, "gate", a["post_norm_gain"][l], [0])])
            if l == 0:
                ahead = mods_one(1, [(0, "shift", None, [4]), (1, "scale", a["pre_norm_gain"][1], [5])])
            else:
                ahead = mods_two(0, [(0, "shift", None, [0]), (1, "scale", a["norm_g_2"][0, 0], [1])], 2)
            schedule.append(Linear(a["w_in"][l], chunks, lambda t, c0, n: P1[:, t, c0:c0 + n], [[job] for job in gates + ahead]))

            linear = schedule[-1]

            def rotate_columns(which, c0, c1, chunk):
                def step(eng):
                    linear.wait_copied(eng, chunk)
                    for t in range(XT):
                        x = P1[:, t, c0:c1]
                        dve_s.chain(rotate(eng, dve_s, x, x, cos1[:, t, which], sin1[:, t, which], (c1 - c0) // 64, 1, 32, rope_tmp_one))
                return step

            def silu_columns(c0, n, chunk, t):
                def step(eng):
                    linear.wait_copied(eng, chunk)
                    x = P1[:, t, c0:c0 + n]
                    eng.activation(x, x, ACT.Silu)
                return step

            linear.beside["dve"] = {2: [rotate_columns(0, AQ, AV, 1)], 4: [rotate_columns(1, RQ, RV, 3)]}
            linear.beside["act"] = {c: [silu_columns(c0, n, chunk, t) for t in range(XT)]
                                    for c, c0, n, chunk in ((3, AG, 512, 2), (5, RG, 256, 4), (len(chunks), GG, 256, len(chunks) - 1))}

            def tiles_of(c0, m):
                return turn([P1[:, t, c0:c0 + m] for t in range(XT)])

            groups = [dict(ops=tiles_of(AQ + pair * P, P), dsts=[(0, P, qT[:, pair, :])]) for pair in range(4)]
            groups += [dict(ops=tiles_of(AK + g * 64, 64), dsts=[(0, 64, kT[0:64, g, 0, :]), (0, 64, kT[64:P, g, 1, :])]) for g in range(2)]
            groups += [dict(ops=tiles_of(c + pair * P, P), dsts=[(0, P, z[:, pair, :])]) for c, z in ((RQ, qrT), (RK, krT)) for pair in range(2)]
            groups += [dict(ops=tiles_of(GQ, P), dsts=[(0, P, gqT[:, :])], scale=32 ** -0.5), dict(ops=tiles_of(GK, P), dsts=[(0, P, gkT[:, :])]),
                       dict(ops=tiles_of(GA, 16), dsts=[(0, 16, gaT[:, :])])]
            schedule.append(Pieces(groups, lambda eng: clear_other_head(eng, kT)))

            units = []
            for t in range(XT):
                for h in range(8):
                    first = max(t - 1, 0)
                    blocks = list(range(first, t + 1))
                    keys = [(kT[:, h // 4, h % 2, b * P:(b + n) * P], c) for b, n, c in key_runs(blocks)]
                    mask = [(window[:, (0 if b < t else P):(P if b < t else 2 * P)], i * P) for i, b in enumerate(blocks)]
                    o = P1[:, t, AQ + h * 64:AQ + h * 64 + 64]
                    units.append(dict(q=qT[:, h // 2, tok(t)], keys=keys, mask=mask,
                                      values=[P1[:, b, AV + 64 * (h // 4):AV + 64 * (h // 4) + 64] for b in blocks], scale=0.125, sink=h,
                                      finish=("gated", o, P1[:, t, AG + h * 64:AG + h * 64 + 64])))
            schedule.append(Attention(units, probs1, probs1_t, stats, neg_sinks, sinks))

            def dve(eng):
                for pair in range(2):
                    v = lambda z: z[:, pair, :].rearrange("p (t n) -> p t n", n=P)
                    eng.tensor_tensor(v(qdT), v(qrT), c1t("rqdecay")[:, pair * P:(pair + 1) * P].unsqueeze(1).to_broadcast([P, XT, P]), ALU.mult)

            def pool(eng):
                eng.memset(ret_s[:, 0], 0.0)
                for t in range(XT):
                    eng.tensor_tensor(heads_view(ret_k[:, t], 4), heads_view(P1[:, t, RK:RV], 4),
                                      c1t("rkdecay").unsqueeze(2).to_broadcast([P, 4, 64]), ALU.mult)

            schedule.append(Work(dve=dve, pool=pool))
            groups = []
            for t in range(XT):
                for par in range(2):
                    rows = slice(64 * par, 64 * par + 64)
                    groups.append(dict(ops=[("product", (0, P), pair * P, P, [(krT[rows, pair, tok(t)], qrT[rows, pair, tok(t)])]) for pair in range(2)],
                                       dsts=[(0, P, ret_a[:, t, par])], mask=c1t("rdecay")[:, par * 256:(par + 1) * 256]))
                if t < XT - 1:
                    groups.append(dict(ops=[("product", (0, P), pair * P, P, [(ret_k[:, t, tok(pair)], P1[:, t, RV + pair * P:RV + (pair + 1) * P])])
                                            for pair in range(2)], dsts=[(0, P, ret_u[:, t])],
                                       mask=c1t("rblock").unsqueeze(1).to_broadcast([P, 2, P])))
            schedule.append(Pieces(groups))

            def dve(eng):
                for t in range(XT - 1):
                    for pair in range(2):
                        ins = eng.scalar_tensor_tensor(out=ret_s[:, t + 1, pair], in0=ret_s[:, t, pair], scalar=c1t("rchunk")[:, pair:pair + 1],
                                                       in1=ret_u[:, t, pair], op0=ALU.mult, op1=ALU.add)
                    dve_s.chain(ins)

            schedule.append(Work(dve=dve))
            groups = []
            for t in range(XT):
                ops = [("product", (0, P), pair * P, P, [(qdT[:, pair, tok(t)], ret_s[:, t, pair])],
                        (pair == 0, False)) for pair in range(2)]
                ops += [("product", (0, P), h * 64, 64, [(ret_a[:, t, h % 2, (h // 2) * P:(h // 2 + 1) * P], P1[:, t, RV + h * 64:RV + h * 64 + 64])],
                         (False, h == 3)) for h in range(4)]
                groups.append(dict(ops=ops, dsts=[(0, P, P1[:, t, RQ:RQ + 256])]))
            schedule.append(Pieces(groups))

            schedule.append(Pieces([dict(ops=[("product", (0, P), 0, S, [(gate_w[:, :], gaT[:, :])])], dsts=[(0, P, z_t)])]))

            def dve(eng):
                eng.tensor_scalar(z_min, z_t, gate_b[:, 0:1], 0.0, ALU.add, ALU.min)

            schedule.append(Work(dve=dve))

            def act(eng):
                act_s.chain(eng.activation(z_abs, z_t, ACT.Abs, bias=gate_b[:, 0:1]))
                act_s.chain(eng.activation(z_exp, z_abs, ACT.Exp, scale=-1.0))
                eng.activation(z_t, z_exp, ACT.Ln, bias=1.0)

            schedule.append(Work(act=act))
            schedule.append(Work(dve=lambda eng: eng.tensor_tensor(log_a, z_min, z_t, ALU.subtract)))
            schedule.append(Pieces([dict(ops=turn([log_a[:, tok(t)] for t in range(XT)]), dsts=[(0, P, log_a_tok[:, :, :])])]))
            schedule.append(Pieces([dict(ops=[("product", (0, P), t * P, P, [(log_a_tok[:, t], c1t("tri"))]) for t in range(XT)],
                                         dsts=[(0, P, B[:, :])])]))
            schedule.append(GlaLevels())

            chunk_view = lambda z: z.rearrange("p (c n) -> p c n", n=GLA_C)
            dist, fac, fac2 = g_q[:, 0], g_q[:, 1], g_k[:, 0]

            def dve(eng):
                b = chunk_view(B[:, :])
                eng.tensor_tensor(chunk_view(dist), b, b[:, :, GLA_C - 1:GLA_C].to_broadcast([P, 8, GLA_C]), ALU.subtract)

            def act(eng):
                eng.activation(fac2, B[:, :], ACT.Exp, scale=1.0 / GATE_NORM)
                eng.activation(gla_decay[:, :], B[:, GLA_C - 1::GLA_C], ACT.Exp, scale=1.0 / GATE_NORM)

            schedule.append(Work(dve=dve, act=act, pool=lambda eng: eng.memset(gla_s[:, 0], 0.0)))
            schedule.append(Work(act=lambda eng: eng.activation(fac, dist, ACT.Exp, scale=-1.0 / GATE_NORM),
                                 dve=lambda eng: eng.tensor_tensor(g_qe[:, :], gqT[:, :], fac2, ALU.mult)))
            schedule.append(Work(dve=lambda eng: eng.tensor_tensor(g_kd[:, :], gkT[:, :], fac, ALU.mult)))
            schedule.append(Pieces([dict(ops=turn([g_kd[:, tok(t)] for t in range(XT)]), dsts=[(0, P, g_kdt[:, :, :])])]))
            groups = []
            for par in range(2):
                for two in range(2):
                    cs = [2 * t + par for t in (2 * two, 2 * two + 1)]
                    rows = slice(GLA_C * par, GLA_C * par + GLA_C)
                    groups.append(dict(ops=[("product", (0, P), i * 256, 256, [(g_kdt[rows, c // 2, :], P1[rows, c // 2, GV:GV + 256])])
                                            for i, c in enumerate(cs)],
                                       dsts=[(0, P, gla_u[:, cs[0]:cs[1] + 1:2, :])], mask=c1t("gblock").unsqueeze(1).to_broadcast([P, 2, 256])))
            schedule.append(Pieces(groups))

            def dve(eng):
                for c in range(7):
                    dve_s.chain(eng.scalar_tensor_tensor(out=gla_s[:, c + 1], in0=gla_s[:, c], scalar=gla_decay[:, c:c + 1], in1=gla_u[:, c],
                                                         op0=ALU.mult, op1=ALU.add))

            schedule.append(Work(dve=dve))
            groups = []
            for t in range(XT):
                ops = []
                for par in range(2):
                    c = 2 * t + par
                    ops.append(("product", (64 * par, 64 * par + 64), 0, 256, [(g_qe[:, c * GLA_C:(c + 1) * GLA_C], gla_s[:, c])], (True, False)))
                ops += [("product", (0, P), h * 64, 64, [(gla_a[:, h, tok(t)], P1[:, t, GV + h * 64:GV + h * 64 + 64])], (False, h == 3)) for h in range(4)]
                groups.append(dict(ops=ops, dsts=[(0, P, P1[:, t, GQ:GQ + 256])]))
            schedule.append(Pieces(groups))

            sq = at(f"head_sq_{l}", [P, 2, XT, 256], F32, ht_at)

            def dve(eng):
                for i, c0 in enumerate((RQ, GQ)):
                    dve_s.chain(eng.tensor_tensor(sq[:, i], P1[:, :, c0:c0 + 256], P1[:, :, c0:c0 + 256], ALU.mult))
                    dve_s.chain(eng.tensor_reduce(headsq[:, 16 * i:16 * i + 16], sq[:, i].rearrange("p t (h d) -> p (t h) d", d=64), AX, ALU.add))
                eng.tensor_scalar(headms[:, 0:32], headsq[:, 0:32], 1.0 / 64, EPS, ALU.mult, ALU.add)

            def pool(eng):
                for t in range(XT):
                    g = heads_view(P1[:, t, GG:GG + 256], 4)
                    eng.tensor_tensor(g, g, gla_gain[:, :].unsqueeze(1).to_broadcast([P, 4, 64]), ALU.mult)

            schedule.append(Work(dve=dve, pool=pool))
            schedule.append(Work(pool=lambda eng: eng.tensor_tensor(headr[:, 0:32], headms[:, 0:32], half64[:, 0:32], ALU.pow)))

            def dve(eng):
                for t in range(XT):
                    for i, (c0, gc) in enumerate(((RQ, RG), (GQ, GG))):
                        z = P1[:, t, c0:c0 + 256]
                        r = headr[:, 16 * i + 4 * t:16 * i + 4 * t + 4].unsqueeze(2).to_broadcast([P, 4, 64])
                        dve_s.chain(eng.tensor_tensor(heads_view(z, 4), heads_view(z, 4), r, ALU.mult))
                        eng.tensor_tensor(z, z, P1[:, t, gc:gc + 256], ALU.mult)

            schedule.append(Work(dve=dve))
            cols = [0, 128, 256, 384, RQ, RQ + 128, GQ, GQ + 128]
            schedule.append(MixTransposed(lambda t, kt: P1[:, t, cols[kt]:cols[kt] + P], XT))
            schedule.append(Linear(a["w_out"][l], [(n * HALF, HALF, range(XT)) for n in range(2)], lambda t, c0, n: Y[:, t, c0:c0 + n]))
            schedule.append(Residual([0] * XT))

        g_ref, g_fac, g_ql, g_kl, g_mm, g_cp = (signal("gla_" + n) for n in ("distance", "factor", "q_level", "k_level", "scored", "placed"))

        class GlaLevels:

            def __init__(self):
                n = len(LEVELS)
                self.b = {s: s.plan(n) for s in (g_ref, g_fac, g_ql, g_kl)}
                self.b[g_mm], self.b[g_cp] = g_mm.plan(n + 1), g_cp.plan(n + 1)

            def wait(self, eng, s, n):
                if n > 0:
                    eng.wait_ge(s.sem, self.b[s] + n)

            def place(self, dve, l):
                mask = c1t("levels")[:, l * P:(l + 1) * P].bitcast(U32).unsqueeze(1).to_broadcast([P, XT, P])
                self.wait(dve, g_mm, l + 1)
                self.wait(dve, g_cp, l)
                for h in range(4):
                    v = lambda z: z.rearrange("p (t n) -> p t n", n=P)
                    ins = dve.copy_predicated(v(gla_a[:, h]), mask, v(ps[:, 4 * (l % 2) + h, :]))
                ins.then_inc(g_cp.sem, 1)

            def vector(self, dve):
                n = len(LEVELS)
                dve_s.mark(dve.memset(gla_a[:].rearrange("p h s -> p (h s)"), 0.0))
                dve.wait_ge(dve_s.sem, dve_s.n)
                for step in range(n + 2):
                    if step < n:
                        s = LEVELS[step]
                        v = lambda z: z.rearrange("p (b n) -> p b n", n=2 * s)
                        b = v(B[:, :])
                        dist = g_dist[:, step % 2]
                        self.wait(dve, g_fac, step - 1)
                        dve_s.chain(dve.tensor_tensor(v(dist), b, b[:, :, s - 1:s].to_broadcast([P, S // (2 * s), 2 * s]), ALU.subtract))
                        dve.scalar_tensor_tensor(out=dist, in0=dist, scalar=-1.0, in1=dist, op0=ALU.mult, op1=ALU.max).then_inc(g_ref.sem, 1)
                    l = step - 1
                    if 0 <= l < n:
                        self.wait(dve, g_fac, l + 1)
                        self.wait(dve, g_mm, l - 1)
                        dve.tensor_tensor(g_q[:, l % 2], gqT[:, :], g_exp[:, l % 2], ALU.mult).then_inc(g_ql.sem, 1)
                    if step - 2 >= 0:
                        self.place(dve, step - 2)
                self.place(dve, n)

            def scalar(self, act):
                for l in range(len(LEVELS)):
                    self.wait(act, g_ref, l + 1)
                    self.wait(act, g_ql, l - 1)
                    self.wait(act, g_kl, l - 1)
                    act.activation(g_exp[:, l % 2], g_dist[:, l % 2], ACT.Exp, scale=-1.0 / GATE_NORM).then_inc(g_fac.sem, 1)

            def gpsimd(self, pool):
                for l in range(len(LEVELS)):
                    self.wait(pool, g_fac, l + 1)
                    self.wait(pool, g_mm, l - 1)
                    pool.tensor_tensor(g_k[:, l % 2], gkT[:, :], g_exp[:, l % 2], ALU.mult).then_inc(g_kl.sem, 1)

            def tensor(self, pe):
                n = len(LEVELS)
                for l in range(n + 1):
                    if l < n:
                        self.wait(pe, g_ql, l + 1)
                        self.wait(pe, g_kl, l + 1)
                    self.wait(pe, g_cp, l - 1)
                    q, k = (g_q[:, l % 2], g_k[:, l % 2]) if l < n else (gqT[:, :], gkT[:, :])
                    for h in range(4):
                        rows = slice(32 * h, 32 * h + 32)
                        for t in range(XT):
                            ins = pe.matmul(ps[:, 4 * (l % 2) + h, tok(t)], k[rows, tok(t)], q[rows, tok(t)], start=True, stop=True)
                    ins.then_inc(g_mm.sem, 1)

            def sync(self, sp):
                pass

        con2 = at("constants_two", [P, TWO_W], F32, aux_at)
        c2t = lambda name: con2[:, slice(*TWO_COLS[name])]
        take = region(arena)
        PE_ = take("proj_even", [P, XT + CT, EV_IN])
        rope_tmp_even = at("rope_tmp_even", [P, 640], F32, take.where[0])
        cqT, ckvT = take("latent_q_t", [P, 2, TOK]), take("latent_kv_t", [P, TOK])
        w_uq, w_ukv = take("w_uq", [P, 2, D * 3 // 4]), take("w_ukv", [P, D])
        qpe = take("latent_q_rope", [P, XT + CT, 256])
        EV_END = take.where[0]
        take = region(ht_at)
        rope_p2 = take("rope_tmp_pool_two", [P, 1024])
        norm_junk = take("latent_squares", [P, XT + CT, 384])
        take = region(ht_at)
        qaT, kaT = take("even_q_t", [P, 4, TOK]), take("even_k_t", [P, 2, 2, TOK])
        probs2, probs2_t = take("att_probs_two", [P, 2, TOK]), take("att_probs_t_two", [P, 2, TOK])
        assert take.where[0] <= ht_end
        take = region(ht_at + 2 * 2 * TOK * 4)
        probsb, probsb_t = (at(n, [P, 2, TOK], F32, ht_at + i * 2 * TOK * 4) for i, n in enumerate(("att_probs_lat", "att_probs_t_lat")))
        vb = take("latent_values", [P, XT + CT, HALF])
        take = region(take.where[0])
        kbT, qbT = take("latent_k_t", [96, 4, TOK]), take("latent_q_heads_t", [96, 4, TOK])
        assert take.where[0] <= ht_end, (take.where[0], ht_end)
        take = region(arena)
        PO = take("proj_odd", [P, XT + CT, OD_IN])
        rope_tmp_odd = take("rope_tmp_odd", [P, 640])
        take = region(ht_at)
        probs3 = take("att_probs_three", [P, 2, TOK])
        probs3_t = take("att_probs_t_three", [P, 2, TOK])
        qcT, kcT = take("odd_q_t", [P, 4, S]), take("odd_k_t", [P, 2, TOK])
        qfT, kfT = take("diff_q_t", [P, 4, S]), take("diff_k_t", [P, 4, TOK])
        assert take.where[0] <= ht_end

        def rows_of(src, kt, tiles):
            return [src(t)[:, kt] for t in tiles]

        def both(src, dst, m=P, dsts=None, **more):
            out = []
            for tiles in (range(XT), range(XT, XT + CT)):
                cols = slice(tiles[0] * P, tiles[-1] * P + P)
                out.append(dict(ops=turn([src(t) for t in tiles]), dsts=[(p0, p1, d(cols)) for p0, p1, d in dst], **more))
            return out

        def tables(width, t):
            return (c2t(f"cos{width}")[:, t * width:(t + 1) * width], c2t(f"sin{width}")[:, t * width:(t + 1) * width])

        def tables_phase():
            barrier, loaded = len(schedule), load_in.plan(16) + 16

            def sp(eng):
                sp_waits_phase(eng, barrier)
                eng.dma_start(con2[:, :], a["two"]).then_inc(load_in.sem, 16)

            def dve(eng):
                eng.wait_ge(load_in.sem, loaded)
                eng.tensor_copy(window[:, :], c2t("window"))

            schedule.append(Work(sp=sp, dve=dve))

        def layer_even():
            barrier = len(schedule)
            small_loads = [
                (sinks[:, :], a["ev_sink_2"][0].partition_broadcast(P)),
                (qn_col[:, :], a["ev_q_norm_2"][0].rearrange("(k p) -> p k", p=P)),
                (kvn_col[:, :], a["ev_kv_norm_2"][0].rearrange("(p o) -> p o", o=1)),
            ]
            loaded = load_in.plan(16 * len(small_loads)) + 16 * len(small_loads)

            def sp(eng):
                sp_waits_phase(eng, barrier)
                for dst, src in small_loads:
                    eng.dma_start(dst, src, allow_slow_non_contiguous=True).then_inc(load_in.sem, 16)

            def dve(eng):
                eng.wait_ge(load_in.sem, loaded)
                eng.tensor_scalar(neg_sinks[:, :], sinks[:, :], -1.0, None, ALU.mult)

            schedule.append(Work(sp=sp, dve=dve))
            g = lambda i: a["norm_g_2"][0, i]
            tables_phase()
            schedule.append(NormTransposed(True, 0, 1, (2, HALF)))
            allt = range(XT + CT)
            jobs = mods_two(0, [(2, "gate", g(1), [0, 1]), (3, "shift", None, [2])], 2)
            schedule.append(Linear(a["ev_w_in_2"][0], [(0, 512, allt), (512, 416, allt), (928, 256, allt)],
                                   lambda t, c0, n: PE_[:, t, c0:c0 + n], [jobs[0:2], jobs[2:4]]))
            linear = schedule[-1]

            def rotate_qk(eng):
                linear.wait_copied(eng, 1)
                for t in range(XT):
                    x = PE_[:, t, 0:640]
                    dve_s.chain(rotate(eng, dve_s, x, x, *tables(64, t), 10, 2, 16, rope_tmp_even))

            linear.beside["dve"] = {2: [rotate_qk]}
            barrier2 = len(schedule)
            loaded2 = load_in.plan(32) + 32

            def sp(eng):
                sp_waits_phase(eng, barrier2)
                eng.dma_start(w_uq[:, :, :], a["ev_w_uq_2"][0].rearrange("(k p) n -> p k n", p=P)).then_inc(load_in.sem, 16)
                eng.dma_start(w_ukv[:, :], a["ev_w_ukv_2"][0]).then_inc(load_in.sem, 16)

            def act(eng):
                for t in allt:
                    eng.activation(norm_junk[:, t, 0:256], PE_[:, t, 768:1024], ACT.Square, accum_out=headsq[:, t:t + 1])
                    eng.activation(norm_junk[:, t, 256:384], PE_[:, t, 1024:1152], ACT.Square, accum_out=headsq[:, 8 + t:9 + t])

            def pool(eng):
                for t in range(XT):
                    x = PE_[:, t, 1152:1184]
                    pool_s.chain(rotate(eng, pool_s, x, x, *tables(32, t), 1, 2, 8, rope_p2))

            schedule.append(Work(act=act, pool=pool, sp=sp))

            def dve(eng):
                eng.tensor_scalar(headms[:, 0:6], headsq[:, 0:6], 1.0 / 256, EPS, ALU.mult, ALU.add)
                eng.tensor_scalar(headms[:, 8:14], headsq[:, 8:14], 1.0 / 128, EPS, ALU.mult, ALU.add)

            schedule.append(Work(dve=dve))
            schedule.append(Work(pool=lambda eng: eng.tensor_tensor(headr[:, 0:16], headms[:, 0:16], half64[:, 0:16], ALU.pow)))

            def dve(eng):
                eng.wait_ge(load_in.sem, loaded2)
                for t in allt:
                    for c0, c1_, s in ((768, 1024, 0), (1024, 1152, 8)):
                        z = PE_[:, t, c0:c1_]
                        eng.tensor_scalar(z, z, headr[:, s + t:s + t + 1], None, ALU.mult)

            schedule.append(Work(dve=dve))
            groups = []
            for pair in range(4):
                groups += both(lambda t: PE_[:, t, pair * P:(pair + 1) * P], [(0, P, lambda c, pair=pair: qaT[:, pair, c])])
            for kv in range(2):
                groups += both(lambda t: PE_[:, t, 512 + 64 * kv:576 + 64 * kv],
                               [(0, 64, lambda c, kv=kv: kaT[0:64, kv, 0, c]), (0, 64, lambda c, kv=kv: kaT[64:P, kv, 1, c])])
                groups += both(lambda t: PE_[:, t, 768 + P * kv:768 + P * (kv + 1)], [(0, P, lambda c, kv=kv: cqT[:, kv, c])],
                               scale=qn_col[:, kv:kv + 1])
            groups += both(lambda t: PE_[:, t, 1024:1152], [(0, P, lambda c: ckvT[:, c])], scale=kvn_col[:, 0:1])
            schedule.append(Pieces(groups, lambda eng: clear_other_head(eng, kaT)))

            units = []
            for t in allt:
                for h in range(8):
                    local = [b for b in (t - 1, t, t + 1) if 0 <= b < XT] if t < XT else []
                    blocks = local + [XT, XT + 1]
                    mask = [(window[:, (0 if b < t else P):(P if b < t else 2 * P)], i * P) for i, b in enumerate(local) if b != t]
                    units.append(dict(q=qaT[:, h // 2, tok(t)], keys=[(kaT[:, h // 4, h % 2, b * P:(b + n) * P], c) for b, n, c in key_runs(blocks)],
                                      mask=mask, values=[PE_[:, b, 640 + 64 * (h // 4):704 + 64 * (h // 4)] for b in blocks], scale=0.125, sink=h,
                                      finish=("plain", PE_[:, t, h * 64:h * 64 + 64], None)))
            schedule.append(Attention(units, probs2, probs2_t, stats, neg_sinks, sinks))

            w_kv = w_ukv[:, :].rearrange("p (h n) -> p h n", h=8)
            w_q = w_uq[:, :, :].rearrange("p k (h n) -> p k h n", h=8)
            groups = []
            for t in allt:
                groups.append(dict(ops=[("product", (0, P), 0, HALF, [(ckvT[:, tok(t)], w_kv[:, :, 64:128])])], dsts=[(0, P, vb[:, t, :])]))
                groups.append(dict(ops=[("product", (0, P), 0, 256, [(cqT[:, k, tok(t)], w_q[:, k, :, 64:96]) for k in range(2)])],
                                   dsts=[(0, P, qpe[:, t, :])]))
            schedule.append(Pieces(groups))

            tmp_q = at("rope_tmp_latent", [P, 256], F32, ht_at)

            def dve(eng):
                for t in range(XT):
                    x = qpe[:, t, :]
                    dve_s.chain(rotate(eng, dve_s, x, x, *tables(32, t), 8, 2, 8, tmp_q))

            schedule.append(Work(dve=dve))
            for four in range(2):
                groups = []
                for i in range(4):
                    h = 4 * four + i
                    for c0, n in ((0, S), (S, CTX)):
                        groups.append(dict(ops=[("product", (0, 64), 0, n, [(w_kv[:, h, 0:64], ckvT[:, c0:c0 + n])])], dsts=[(0, 64, kbT[0:64, i, c0:c0 + n])]))
                        groups.append(dict(ops=[("product", (0, 64), 0, n, [(w_q[:, k, h, 0:64], cqT[:, k, c0:c0 + n]) for k in range(2)])],
                                           dsts=[(0, 64, qbT[0:64, i, c0:c0 + n])]))
                groups += both(lambda t: PE_[:, t, 1152:1184], [(0, 32, lambda c, i=i: kbT[64:96, i, c]) for i in range(4)])
                groups += both(lambda t: qpe[:, t, four * P:(four + 1) * P], [(32 * i, 32 * i + 32, lambda c, i=i: qbT[64:96, i, c]) for i in range(4)])
                schedule.append(Pieces(groups))
                units = []
                for t in allt:
                    for i in range(4):
                        h = 4 * four + i
                        blocks = list(range(XT + CT)) if t < XT else [XT, XT + 1]
                        spans = ((0, S), (S, CTX)) if t < XT else ((S, CTX),)
                        keys = [(kbT[:, i, c0:c0 + n], c0 if t < XT else 0) for c0, n in spans]
                        units.append(dict(q=qbT[:, i, tok(t)], keys=keys, mask=[], values=[vb[:, b, h * 64:h * 64 + 64] for b in blocks],
                                          scale=96 ** -0.5, sink=None, finish=("plain", PE_[:, t, HALF + h * 64:HALF + h * 64 + 64], None)))
                schedule.append(Attention(units, probsb, probsb_t, stats))
            schedule.append(MixTransposed(lambda t, kt: PE_[:, t, kt * P:(kt + 1) * P], XT + CT))
            jobs = mods_two(0, [(4, "scale", g(2), [3]), (5, "gate", g(3), [2, 3])], 2)
            schedule.append(Linear(a["ev_w_out_2"][0], [(n * HALF, HALF, allt) for n in range(2)], lambda t, c0, n: Y[:, t, c0:c0 + n],
                                   [jobs[0:2], jobs[2:4]]))
            schedule.append(Residual([0] * XT + [1] * CT))
            schedule.append(NormTransposed(True, 2, 3, (4, GROUP)))
            g = lambda i: a["norm_g_2"][1, i]
            jobs = mods_two(1, [(0, "shift", None, [4]), (1, "scale", g(0), [5])], 2, mod_acc_gates)
            jobs += mods_two(1, [(3, "shift", None, [6]), (4, "scale", g(2), [7])], 1, mod_acc_gates)
            schedule.append(FeedForward(a["ffn_w_in_2"][0], a["ffn_w_out_2"][0], XT + CT, [jobs[2 * p:2 * p + 2] for p in range(4)]))
            schedule.append(Residual([2] * XT + [3] * CT))

        def layer_odd():
            barrier = len(schedule)
            small_loads = [
                (qk_gain[:, :, :], a["od_qk_norm_2"][0].partition_broadcast(P)),
                (lam_in[:, :, :], a["od_lambda_2"][0].partition_broadcast(P)),
                (sub_gain[:, :], a["od_subln_2"][0].partition_broadcast(P)),
            ]
            loaded = load_in.plan(16 * len(small_loads)) + 16 * len(small_loads)

            def sp(eng):
                for dst, src in small_loads:
                    eng.dma_start(dst, src, allow_slow_non_contiguous=True).then_inc(load_in.sem, 16)

            def dve(eng):
                eng.wait_ge(load_in.sem, loaded)
                eng.tensor_scalar(sub_gain[:, :], sub_gain[:, :], 1.0 - LAM_INIT, None, ALU.mult)
                pairs = lam_in[:, :, :].rearrange("p (a b) d -> p a b d", b=2)
                dve_s.chain(eng.tensor_tensor(lam_prod[:, :, :], pairs[:, :, 0, :], pairs[:, :, 1, :], ALU.mult))
                eng.tensor_reduce(lam_sum[:, :], lam_prod[:, :, :], AX, ALU.add)

            schedule.append(Work(sp=sp, dve=dve))
            schedule.append(Work(act=lambda eng: eng.activation(lam_prod[:, 0, 0:2], lam_sum[:, :], ACT.Exp)))

            def dve(eng):
                dve_s.chain(eng.tensor_tensor(neg_lam[:, :], lam_prod[:, 0, 1:2], lam_prod[:, 0, 0:1], ALU.subtract))
                eng.tensor_scalar(neg_lam[:, :], neg_lam[:, :], -LAM_INIT, None, ALU.add)

            schedule.append(Work(dve=dve))
            g = lambda i: a["norm_g_2"][1, i]
            tables_phase()
            schedule.append(NormTransposed(True, 4, 5, (2, HALF)))
            allt, xt = range(XT + CT), range(XT)
            jobs = mods_two(1, [(2, "gate", g(1), [0]), (5, "gate", g(3), [2])], 1)
            schedule.append(Linear(a["od_w_in_2"][0], [(0, 512, xt), (512, 256, allt), (768, 512, xt), (1280, 512, allt), (1792, 512, allt)],
                                   lambda t, c0, n: PO[:, t, c0:c0 + n], [[job] for job in jobs]))
            linear = schedule[-1]
            parts = [(t, 0, 10) if t < XT else (t, 8, 10) for t in allt]
            m0, r0 = ms_ready.plan(1), rstd_ready.plan(4)

            def head_squares(eng):
                linear.wait_copied(eng, 1)
                for i, (t, h0, h1) in enumerate(parts):
                    z, sq = PO[:, t, h0 * 64:h1 * 64], rope_tmp_odd[:, 0:(h1 - h0) * 64]
                    dve_s.chain(eng.tensor_tensor(sq, z, z, ALU.mult))
                    dve_s.chain(eng.tensor_reduce(headsq[:, t * 10 + h0:t * 10 + h1], heads_view(sq, h1 - h0), AX, ALU.add))
                eng.tensor_scalar(headms[:, 0:60], headsq[:, 0:60], 1.0 / 64, EPS, ALU.mult, ALU.add).then_inc(ms_ready.sem, 1)

            def head_rstd(i):
                def step(eng):
                    c = slice(15 * i, 15 * i + 15)
                    eng.wait_ge(ms_ready.sem, m0 + 1)
                    eng.tensor_tensor(headr[:, c], headms[:, c], half64[:, c], ALU.pow).then_inc(rstd_ready.sem, 1)
                return step

            def norm_heads(eng):
                eng.wait_ge(rstd_ready.sem, r0 + 4)
                for t, h0, h1 in parts:
                    z = heads_view(PO[:, t, h0 * 64:h1 * 64], h1 - h0)
                    dve_s.chain(eng.tensor_tensor(z, z, headr[:, t * 10 + h0:t * 10 + h1].unsqueeze(2).to_broadcast([P, h1 - h0, 64]), ALU.mult))
                    for which, lo, hi in ((0, h0, 8), (1, 8, 10)):
                        if lo < hi:
                            z = heads_view(PO[:, t, lo * 64:hi * 64], hi - lo)
                            ins = eng.tensor_tensor(z, z, qk_gain[:, which, :].unsqueeze(1).to_broadcast([P, hi - lo, 64]), ALU.mult)
                    dve_s.chain(ins)
                    if t < XT:
                        x = PO[:, t, 0:640]
                        dve_s.chain(rotate(eng, dve_s, x, x, *tables(64, t), 10, 2, 16, rope_tmp_odd))

            def rotate_diff(c0, chunk):
                def step(eng):
                    linear.wait_copied(eng, chunk)
                    for t in xt:
                        x = PO[:, t, c0:c0 + HALF]
                        dve_s.chain(rotate(eng, dve_s, x, x, *tables(64, t), 8, 2, 16, rope_tmp_odd))
                return step

            linear.beside["dve"] = {2: [head_squares], 3: [rotate_diff(768, 2)], 4: [norm_heads, rotate_diff(1280, 3)]}
            linear.beside["pool"] = {3: [head_rstd(i) for i in range(4)]}
            groups = []
            for pair in range(4):
                groups.append(dict(ops=turn([PO[:, t, pair * P:(pair + 1) * P] for t in xt]), dsts=[(0, P, qcT[:, pair, :])]))
                groups.append(dict(ops=turn([PO[:, t, 768 + pair * P:768 + (pair + 1) * P] for t in xt]), dsts=[(0, P, qfT[:, pair, :])]))
                groups += both(lambda t: PO[:, t, 1280 + pair * P:1280 + (pair + 1) * P], [(0, P, lambda c, pair=pair: kfT[:, pair, c])])
            for kv in range(2):
                groups += both(lambda t: PO[:, t, 512 + 64 * kv:576 + 64 * kv],
                               [(0, 64, lambda c, kv=kv: kcT[0:64, kv, c]), (0, 64, lambda c, kv=kv: kcT[64:P, kv, c])])
            schedule.append(Pieces(groups))
            units = []
            for t in xt:
                for h in range(8):
                    r = slice(64 * (h % 2), 64 * (h % 2) + 64)
                    units.append(dict(q=qcT[r, h // 2, tok(t)], keys=[(kcT[r, h // 4, c0:c0 + n], c0) for c0, n in ((0, S), (S, CTX))], mask=[],
                                      values=[PO[:, b, 640 + 64 * (h // 4):704 + 64 * (h // 4)] for b in allt], scale=0.125, sink=None,
                                      finish=("plain", PO[:, t, h * 64:h * 64 + 64], None)))
                for h in range(4):
                    dst = PO[:, t, 768 + h * P:768 + (h + 1) * P]
                    for i in range(2):
                        r = slice(64 * i, 64 * i + 64)
                        units.append(dict(q=qfT[r, h, tok(t)], keys=[(kfT[r, h, c0:c0 + n], c0) for c0, n in ((0, S), (S, CTX))], mask=[],
                                          values=[PO[:, b, 1792 + h * P:1792 + (h + 1) * P] for b in allt], scale=0.125, sink=None,
                                          finish=("minus_lambda", dst, dst) if i else ("plain", dst, None)))
            schedule.append(Attention(units, probs3, probs3_t, stats, neg_lambda=neg_lam[:, 0:1]))

            dsq = at("diff_squares", [P, XT, HALF], F32, ht_at)

            def dve(eng):
                dve_s.chain(eng.tensor_tensor(dsq[:], PO[:, 0:XT, 768:1280], PO[:, 0:XT, 768:1280], ALU.mult))
                dve_s.chain(eng.tensor_reduce(headsq[:, 0:16], dsq[:].rearrange("p t (h d) -> p (t h) d", d=P), AX, ALU.add))
                eng.tensor_scalar(headms[:, 0:16], headsq[:, 0:16], 1.0 / P, EPS, ALU.mult, ALU.add)

            schedule.append(Work(dve=dve))
            schedule.append(Work(pool=lambda eng: eng.tensor_tensor(headr[:, 0:16], headms[:, 0:16], half64[:, 0:16], ALU.pow)))

            def dve(eng):
                for t in xt:
                    for h in range(4):
                        z = PO[:, t, 768 + h * P:768 + (h + 1) * P]
                        eng.scalar_tensor_tensor(out=z, in0=z, scalar=headr[:, 4 * t + h:4 * t + h + 1], in1=sub_gain[:, :], op0=ALU.mult, op1=ALU.mult)

            schedule.append(Work(dve=dve))
            schedule.append(MixTransposed(lambda t, kt: PO[:, t, (kt * P if kt < 4 else 256 + kt * P):(kt * P if kt < 4 else 256 + kt * P) + P], XT))
            schedule.append(Linear(a["od_w_out_2"][0], [(n * HALF, HALF, xt) for n in range(2)], lambda t, c0, n: Y[:, t, c0:c0 + n]))
            schedule.append(Residual([0] * XT))
            schedule.append(NormTransposed(False, 6, 7, (4, GROUP)))
            schedule.append(FeedForward(a["ffn_w_in_2"][1], a["ffn_w_out_2"][1], XT))
            schedule.append(Residual([2] * XT))

        setup_phases()
        marks = []
        for l in range(DEPTH):
            layer_one(l)
            marks.append(len(schedule))
        layer_even()
        marks.append(len(schedule))
        layer_odd()
        marks.append(len(schedule))
        if stop is not None:
            schedule = schedule[:stop if stop >= 0 else marks[-stop - 1]]

        block = ctx.enter_context(nc.Block())

        @block.sync
        def _(sp):
            for i, phase in enumerate(schedule):
                phase.sync(sp)
            sp_waits_phase(sp, len(schedule))
            sp.dma_start(out[0].rearrange("(t p) d -> p t d", p=P), X[:, 0:XT, :]).then_inc(out_landed.sem, 16)
            sp.wait_ge(out_landed.sem, 16)

        @block.tensor
        def _(pe):
            for phase in schedule:
                phase.tensor(pe)
                if not flows(phase):
                    phase_end(pe, "pe")

        @block.scalar
        def _(act):
            nonlocal act_s
            act_s = Steps(act, act_step.sem)
            for phase in schedule:
                phase.scalar(act)
                if not flows(phase):
                    phase_end(act, "act")

        @block.vector
        def _(dve):
            nonlocal dve_s
            dve_s = Steps(dve, dve_step.sem)
            for phase in schedule:
                phase.vector(dve)
                if not flows(phase):
                    phase_end(dve, "dve")

        @block.gpsimd
        def _(pool):
            nonlocal pool_s
            pool_s = Steps(pool, pool_step.sem)
            for phase in schedule:
                phase.gpsimd(pool)
                if not flows(phase):
                    phase_end(pool, "pool")


_INS = ["x", "c", "positions", "w_mod", "b_mod", "pre_norm_gain", "post_norm_gain", "w_in", "attn_sinks", "gla_gate_w",
        "gla_gate_b", "gla_norm_gain", "w_out", "c_2", "ctx_2", "c_ctx_2", "ada_w_2", "ada_b_2", "norm_g_2", "ffn_w_in_2",
        "ffn_w_out_2", "ev_w_in_2", "ev_sink_2", "ev_q_norm_2", "ev_w_uq_2", "ev_kv_norm_2", "ev_w_ukv_2", "ev_w_out_2",
        "od_w_in_2", "od_qk_norm_2", "od_lambda_2", "od_subln_2", "od_w_out_2"]


def lay_out(nc, inputs):
    arrays, args = {}, {}
    tables = {"static": static_constants(), "one": block_one_constants(), "two": block_two_constants()}
    for name in _INS + list(tables):
        v = np.ascontiguousarray(tables[name] if name in tables else inputs[name])
        arrays[f"in_{name}_dram"] = v
        args[name] = nc.dram_tensor(f"in_{name}_dram", v.shape, mybir.dt.from_np(v.dtype), kind="ExternalInput").ap()
    return arrays, args


def kernel(**inputs):
    import concourse.bacc as bacc
    from concourse.bass_utils import run_bass_kernel_spmd

    nc = bacc.Bacc("TRN2", target_bir_lowering=False, num_devices=1)
    arrays, args = lay_out(nc, inputs)
    out = nc.dram_tensor("out_0_dram", (1, S, D), F32, kind="ExternalOutput").ap()
    build(nc, args, out)
    r = run_bass_kernel_spmd(nc, [arrays], core_ids=[0])
    return r.results[0]["out_0_dram"]
```

```python
from contextlib import ExitStack
import math

import numpy as np

import concourse.bass as bass
from concourse import mybir

F32 = mybir.dt.float32
F32R = mybir.dt.float32r
BF16 = mybir.dt.bfloat16
I32 = mybir.dt.int32
U32 = mybir.dt.uint32
ALU = mybir.AluOpType
ACT = mybir.ActivationFunctionType
AX = mybir.AxisListType.X

P = 128
D = 1024
KT = D // P
S = 512
CTX = 256
XT = S // P
CT = CTX // P
TOK = S + CTX
DEPTH = 2
EPS = 1e-6
NEG = -1e30
HALF = 512

AQ, AK, AV, AG = 0, 512, 640, 768
RQ, RK, RV, RG = 1280, 1536, 1792, 2048
GQ, GK, GV, GG, GA = 2304, 2432, 2560, 2816, 3072
IN1 = 3088
GLA_C = 64
GATE_NORM = 16.0
LEVELS = (32, 16, 8, 4, 2, 1)

EV_IN, OD_IN = 1184, 2304
FFN = 2816
LAM_INIT = 0.8 - 0.6 * math.exp(-0.3)

def _layout(widths):
    at, cols = 0, {}
    for name, n in widths:
        cols[name] = (at, at + n)
        at += n
    return cols, at


STATIC_COLS, STATIC_W = _layout([("ident", P), ("ones", P)])
ONE_COLS, ONE_W = _layout([
    ("window", 2 * P), ("tri", P), ("levels", 7 * P), ("rdecay", 4 * P), ("rqdecay", 2 * P),
    ("rkdecay", 4), ("rchunk", 2), ("rblock", P), ("gblock", 2 * P), ("gheads", 4), ("freqs", 2 * 64)])
TWO_COLS, TWO_W = _layout([("window", 2 * P), ("cos64", 4 * 64), ("sin64", 4 * 64), ("cos32", 4 * 32),
                           ("sin32", 4 * 32)])


def static_constants():
    t = np.zeros((P, STATIC_W), np.float32)
    t[:, slice(*STATIC_COLS["ident"])] = np.eye(P)
    t[:, slice(*STATIC_COLS["ones"])] = 1.0
    return t


def block_one_constants():
    t = np.zeros((P, ONE_W), np.float32)
    put = lambda name, v: t.__setitem__((slice(None), slice(*ONE_COLS[name])), np.asarray(v).reshape(P, -1))
    i, j = np.arange(P)[:, None], np.arange(P)[None, :]
    put("window", np.concatenate([np.where(j > i, 0, NEG), np.where(j <= i, 0, NEG)], 1))
    src, dst = np.arange(P)[:, None], np.arange(P)[None, :]
    put("tri", (src <= dst) & (src // GLA_C == dst // GLA_C))
    lv = [(src // (2 * s) == dst // (2 * s)) & (src % (2 * s) < s) & (dst % (2 * s) >= s) for s in LEVELS]
    put("levels", np.stack(lv + [src == dst], 1).astype(np.float32))
    log_g = np.log(1.0 - 2.0 ** (-5.0 - np.arange(4)))
    diff = dst - src
    dm = np.where(diff >= 0, np.exp(log_g[:, None, None] * np.maximum(diff, 0)), 0.0) * 64 ** -0.5
    put("rdecay", np.stack([dm[0], dm[2], dm[1], dm[3]], 1))
    part = np.arange(P)[:, None] // 64
    qd = [np.exp(log_g[2 * pair + part] * (np.arange(P)[None, :] + 1.0)) for pair in range(2)]
    put("rqdecay", np.stack(qd, 1))
    put("rkdecay", np.exp(log_g[None, :] * (P - 1.0 - np.arange(P)[:, None])) * 64 ** -0.5)
    put("rchunk", np.concatenate([np.exp(log_g[2 * pair + part] * P) for pair in range(2)], 1))
    put("rblock", src // 64 == dst // 64)
    put("gblock", src // 32 == np.arange(2 * P)[None, :] // 64)
    put("gheads", np.arange(P)[:, None] // 32 == np.arange(4)[None, :])
    rope = (np.float32(10000.0) ** (-np.arange(0, 64, 2, dtype=np.float32) / np.float32(64))).astype(np.float32)
    ret = (1.0 / (np.float32(10000.0) ** np.linspace(0.0, 1.0, 32, dtype=np.float32))).astype(np.float32)
    put("freqs", np.tile(np.concatenate([rope, rope, ret, ret])[None], (P, 1)))
    return t


def block_two_constants():
    t = np.zeros((P, TWO_W), np.float32)
    put = lambda name, v: t.__setitem__((slice(None), slice(*TWO_COLS[name])), np.asarray(v).reshape(P, -1))
    i, j = np.arange(P)[:, None], np.arange(P)[None, :]
    put("window", np.concatenate([np.where(j >= i, 0, NEG), np.where(j <= i, 0, NEG)], 1))
    tok = np.arange(S)
    for width in (64, 32):
        half = width // 4
        fr = (np.float32(10000.0) ** (-np.arange(half, dtype=np.float32) / np.float32(half))).astype(np.float32)
        cos, sin = [], []
        for pos in (tok // 64, tok % 64):
            a = pos.astype(np.float32)[:, None] * fr[None]
            cos += [np.cos(a), np.cos(a)]
            sin += [-np.sin(a), np.sin(a)]
        for name, parts in (("cos", cos), ("sin", sin)):
            full = np.concatenate(parts, 1).reshape(XT, P, width).transpose(1, 0, 2)
            put(f"{name}{width}", full)
    return t


class Signal:

    def __init__(self, sem):
        self.sem, self.planned = sem, 0

    def plan(self, n):
        before = self.planned
        self.planned += n
        return before


class Steps:

    def __init__(self, eng, sem):
        self.eng, self.sem, self.n = eng, sem, 0

    def mark(self, ins):
        self.n += 1
        ins.then_inc(self.sem, 1)
        return self.n

    def chain(self, ins):
        self.eng.wait_ge(self.sem, self.mark(ins))


def build(nc, a, out):
    with ExitStack() as ctx:
        base = (nc.sbuf_base + 31) // 32 * 32
        room = nc.sbuf_usable_end - base
        place = [0]

        def at(name, shape, dt, offset):
            assert offset + int(np.prod(shape[1:])) * mybir.dt.size(dt) <= room, (name, offset)
            return nc.alloc_sbuf_tensor_at(name, shape, dt, offset=base + offset)

        def static(name, shape, dt=F32):
            t = at(name, shape, dt, place[0])
            place[0] += (int(np.prod(shape[1:])) * mybir.dt.size(dt) + 31) // 32 * 32
            return t

        def region(start):
            where = [start]

            def take(name, shape, dt=F32):
                t = at(name, shape, dt, where[0])
                where[0] += (int(np.prod(shape[1:])) * mybir.dt.size(dt) + 31) // 32 * 32
                return t
            take.where = where
            return take

        def signal(name):
            return Signal(ctx.enter_context(nc.semaphore(name)))

        ps = ctx.enter_context(nc.psum_tensor("ps", [P, 8, HALF], F32))

        X = static("x_tokens", [P, XT + CT, D])
        ht_at = place[0]
        HT = static("h_transposed", [P, 2, KT, TOK], F32R)
        ht_end = place[0]
        w_raw = static("w_raw", [P, 4, 1024])
        w_hi = static("w_hi", [P, 2, 1024], F32R)
        w_lo = static("w_lo", [P, 2, 1024], F32R)
        aux_at = place[0]
        static("aux_room", [P, 3 * 2 * HALF])
        con = static("static_constants", [P, STATIC_W])
        gate_rows_at = place[0]
        gate_rows = static("gate_rows", [P, 4, D])
        mod_cols = static("mod_columns", [P, 8, KT, 2])
        c_raw = static("c_raw", [P, 3, KT])
        c_act = static("c_act", [P, 2, KT, 2])
        mod_bias = static("mod_bias", [P, 2, HALF])
        mod_gain = static("mod_gain", [P, HALF])
        sumsq = static("sumsq", [P, 2, 8])
        meansq = static("meansq", [P, 2, 8])
        rstd = static("rstd", [P, 32])
        minus_half = static("minus_half", [P, 32])
        identb = static("ident_bf16", [P, P], BF16)
        window = static("window_bf16", [P, 2 * P], BF16)
        small_at, SMALL = place[0], 5440
        arena = small_at + SMALL
        ident = con[:, slice(*STATIC_COLS["ident"])]
        ones = con[:, slice(*STATIC_COLS["ones"])]
        mod_acc_aux = at("mod_acc_aux", [P, 2, 2, HALF], F32, aux_at + 2 * D * 2)
        mod_acc_gates = at("mod_acc_gates", [P, 2, 2, HALF], F32, gate_rows_at)

        take = region(arena)
        xn = take("x_normed", [P, XT + CT, D])
        junk = take("square_junk", [P, D])
        h_full = take("h_full", [P, 2, HALF])
        take = region(arena)
        Y = take("y_tokens", [P, XT + CT, D])
        act_t = take("ffn_hidden", [P, 2, 6, TOK], F32R)
        res_junk = at("residual_junk", [P, D], F32, arena + (XT + CT) * D * 4)

        dve_s = act_s = pool_s = None

        load_in = signal("inputs_landed")
        w_landed = [signal(f"w_landed{i}") for i in range(4)]
        w_hi_ready, w_lo_ready, w_used = signal("w_hi_ready"), signal("w_lo_ready"), signal("w_used")
        phase_done = signal("phase_done")
        out_landed = signal("out_landed")
        dve_step, act_step, pool_step = signal("dve_step"), signal("act_step"), signal("pool_step")
        units_done = {"act": 0, "pool": 0, "pe": 0}
        phases_done = {"pe": 0, "act": 0, "dve": 0, "pool": 0}

        def phase_end(eng, name):
            phases_done[name] += 1
            eng.drain().then_inc(phase_done.sem, 1)
            eng.wait_ge(phase_done.sem, 4 * phases_done[name])

        def flows(phase):
            return isinstance(phase, (NormTransposed, MixTransposed)) or (isinstance(phase, Residual) and not phase.last)

        def sp_waits_phase(sp, n):
            assert not (n and flows(schedule[n - 1]))
            sp.wait_ge(phase_done.sem, 4 * sum(not flows(p) for p in schedule[:n]))

        stream = []
        ring = {"weight": [], "mod": []}

        def ring_slot(sp, kind):
            u = len(stream)
            if u >= 4:
                before, n = stream[u - 4]
                sp.wait_ge((w_lo_ready if before == "weight" else mod_unit).sem, n + 1)
            stream.append((kind, len(ring[kind])))
            ring[kind].append(u)
            return u

        def weights_load(sp, src, k, n):
            u = ring_slot(sp, "weight")
            dst = w_raw[:, u % 4, 0:k * n].rearrange("p (k n) -> p k n", k=k)
            sp.dma_start(dst, src.rearrange("(k p) n -> p k n", p=P)).then_inc(w_landed[u % 4].sem, 16)

        def weights_high(act, k, n):
            i = units_done["act"]
            units_done["act"] += 1
            u = ring["weight"][i]
            act.wait_ge(w_landed[u % 4].sem, 16 * (u // 4 + 1))
            if i >= 2:
                act.wait_ge(w_used.sem, i - 1)
            act.activation(w_hi[:, i % 2, 0:k * n], w_raw[:, u % 4, 0:k * n], ACT.Copy).then_inc(w_hi_ready.sem, 1)

        def weights_low(pool, k, n):
            i = units_done["pool"]
            units_done["pool"] += 1
            u = ring["weight"][i]
            pool.wait_ge(w_hi_ready.sem, i + 1)
            pool.tensor_tensor(w_lo[:, i % 2, 0:k * n], w_raw[:, u % 4, 0:k * n],
                               w_hi[:, i % 2, 0:k * n].bitcast(F32), ALU.subtract).then_inc(w_lo_ready.sem, 1)

        def weights_use(pe, k, n):
            u = units_done["pe"]
            units_done["pe"] += 1
            pe.wait_ge(w_lo_ready.sem, u + 1)
            return [w[:, u % 2, 0:k * n].rearrange("p (k n) -> p k n", k=k) for w in (w_hi, w_lo)]

        def matmul3(pe, acc, left, right, start, stop):
            pe.matmul(acc, left[0], right[0], start=start, stop=False)
            pe.matmul(acc, left[0], right[1], start=False, stop=False)
            return pe.matmul(acc, left[1], right[0], start=False, stop=stop)

        mod_side = [signal("mod_bias_landed0"), signal("mod_bias_landed1"), signal("mod_gain_landed")]
        mod_unit, mod_summed, mod_turned, mod_kept = (signal(n) for n in ("mod_unit", "mod_summed", "mod_turned", "mod_kept"))
        mod_ready = signal("mod_bias_cleared")
        turns_before = []

        class ModJob:
            jobs = turns = 0

            def __init__(self, w, bias, kind, gain, conds, targets, half, col, acc):
                self.k, ModJob.jobs = ModJob.jobs, ModJob.jobs + 1
                self.w, self.bias = w[:, col:col + HALF], bias[col:col + HALF]
                self.kind, self.conds, self.targets, self.half = kind, conds, targets, half
                self.gain = None if gain is None else gain[half * HALF:(half + 1) * HALF]
                self.acc = acc[:, self.k % 2]
                self.turn0 = ModJob.turns
                self.turns = len(conds) if kind == "gate" else 1
                ModJob.turns += self.turns
                turns_before.append(self.turn0)
                self.side_bias = mod_side[self.k % 2].plan(16) + 16
                if gain is not None:
                    self.side_gain = mod_side[2].plan(16) + 16

            def load(self, sp, q):
                if q == 0:
                    if self.k == 0:
                        sp.wait_ge(mod_ready.sem, 1)
                    if self.k >= 2:
                        sp.wait_ge(mod_summed.sem, self.k - 1)
                    sp.dma_start(mod_bias[0:1, self.k % 2, :], self.bias.rearrange("(o n) -> o n", o=1)).then_inc(mod_side[self.k % 2].sem, 16)
                if q == 2 and self.gain is not None:
                    if self.k >= 1:
                        sp.wait_ge(mod_summed.sem, self.k)
                    sp.dma_start(mod_gain[:, :], self.gain.partition_broadcast(P)).then_inc(mod_side[2].sem, 16)
                u = ring_slot(sp, "mod")
                sp.dma_start(w_raw[:, u % 4, :].rearrange("p (k n) -> p k n", k=2),
                             self.w[q * 256:(q + 1) * 256].rearrange("(k p) n -> p k n", p=P)).then_inc(w_landed[u % 4].sem, 16)

            def sum(self, dve, q):
                first = mod_bias[:, self.k % 2, :]
                if q == 0:
                    dve.wait_ge(mod_side[self.k % 2].sem, self.side_bias)
                    if self.k >= 2:
                        dve.wait_ge(mod_turned.sem, turns_before[self.k - 1])
                    if self.kind == "scale":
                        dve_s.chain(dve.tensor_scalar(first[0:1, :], first[0:1, :], 1.0, None, ALU.add))
                i = 4 * self.k + q
                u = ring["mod"][i]
                dve.wait_ge(w_landed[u % 4].sem, 16 * (u // 4 + 1))
                for j in range(2):
                    for r, (cond, c) in enumerate(self.conds):
                        ins = dve.scalar_tensor_tensor(out=self.acc[:, r], in0=w_raw[:, u % 4, j * HALF:(j + 1) * HALF],
                                                       scalar=c_act[:, cond, 2 * q + j, c:c + 1],
                                                       in1=first if q == 0 and j == 0 else self.acc[:, r], op0=ALU.mult, op1=ALU.add)
                        if j == 0 and r == len(self.conds) - 1:
                            dve_s.chain(ins)
                ins.then_inc(mod_unit.sem, 1)
                dve.wait_ge(mod_unit.sem, i + 1)
                if q == 3:
                    n = len(self.conds)
                    if self.gain is not None:
                        dve.wait_ge(mod_side[2].sem, self.side_gain)
                        dve.tensor_tensor(self.acc[:, 0:n], self.acc[:, 0:n], mod_gain[:, :].unsqueeze(1).to_broadcast([P, n, HALF]), ALU.mult)\
                           .then_inc(mod_summed.sem, 1)
                    else:
                        dve.drain().then_inc(mod_summed.sem, 1)

            def turn(self, pe):
                pe.wait_ge(mod_summed.sem, self.k + 1)
                for r in range(self.turns):
                    m = self.turn0 + r
                    if m >= 2:
                        pe.wait_ge(mod_kept.sem, m - 1)
                    if self.kind == "gate":
                        ins = pe.matmul(ps[:, 6 + m % 2, :], ones, self.acc[:, r], start=True, stop=True)
                    else:
                        for i in range(len(self.conds)):
                            for j in range(4):
                                ins = pe.matmul(ps[:, 6 + m % 2, 4 * i + j:4 * i + j + 1], self.acc[:, i, j * P:(j + 1) * P], ones[:, 0:1],
                                                start=True, stop=True)
                    ins.then_inc(mod_turned.sem, 1)

            def keep(self, act):
                for r in range(self.turns):
                    m = self.turn0 + r
                    act.wait_ge(mod_turned.sem, m + 1)
                    if self.kind == "gate":
                        ins = act.activation(gate_rows[:, self.targets[r], self.half * HALF:(self.half + 1) * HALF], ps[:, 6 + m % 2, :], ACT.Copy)
                    else:
                        n = len(self.conds)
                        ins = act.activation(mod_cols[:, self.targets[0], 4 * self.half:4 * self.half + 4, 0:n].rearrange("p j r -> p r j"),
                                             ps[:, 6 + m % 2, 0:4 * n].rearrange("p (r j) -> p r j", j=4), ACT.Copy)
                    ins.then_inc(mod_kept.sem, 1)

        def mod_jobs(w, bias, vectors, conds, acc):
            return [ModJob(w, bias, kind, gain, conds, targets, half, n * D + half * HALF, acc)
                    for n, kind, gain, targets in vectors for half in range(2)]

        class Modulation:

            def __init__(self, jobs, other_loads):
                self.jobs, self.other_loads = jobs, other_loads

            def sync(self, sp):
                for i, job in enumerate(self.jobs):
                    if i in self.other_loads:
                        self.other_loads[i](sp)
                    for q in range(4):
                        job.load(sp, q)
                self.other_loads[len(self.jobs)](sp)

            def vector(self, dve):
                for job in self.jobs:
                    for q in range(4):
                        job.sum(dve, q)

            def tensor(self, pe):
                for job in self.jobs:
                    job.turn(pe)

            def scalar(self, act):
                for job in self.jobs:
                    job.keep(act)

            def gpsimd(self, pool):
                pass

        sq_ready, ms_ready, rstd_ready, xn_ready = (signal(n) for n in ("squares_ready", "meansq_ready", "rstd_ready", "xn_ready"))
        ht_turned, ht_high, ht_full, ht_low = (signal(n) for n in ("ht_turned", "ht_high", "ht_full", "ht_low"))

        def wait_features(pe, source, kt):
            pe.wait_ge(ht_low.sem, source.g0 + (kt + 1) * len(source.groups) // KT)

        def wait_bank(pe, source, bank):
            pe.wait_ge(source.bank_signal.sem, source.bank0 + len(source.groups) - 8 + bank + 1)

        x_added = signal("x_added")

        def row_rstd(pool, which, t, squares):
            pool.wait_ge(sq_ready.sem, squares)
            ms = meansq[:, which, t:t + 1]
            pool_s.chain(pool.tensor_scalar(ms, sumsq[:, which, t:t + 1], 1.0 / D, EPS, ALU.mult, ALU.add))
            pool.tensor_tensor(rstd[:, 8 * which + t:8 * which + t + 1], ms, minus_half[:, 0:1], ALU.pow).then_inc(rstd_ready.sem, 1)

        class NormTransposed:
            def __init__(self, with_ctx, shift, scale, prime, sp=None):
                self.prime, self.sp = prime, sp
                self.before = schedule[-1]
                self.added = self.before.x0 if isinstance(self.before, Residual) else None
                self.T = XT + (CT if with_ctx else 0)
                self.shift, self.scale = shift, scale
                self.q0, self.r0 = sq_ready.plan(self.T), rstd_ready.plan(self.T)
                self.x0 = xn_ready.plan(self.T)
                kinds = [(0, range(0, XT)), (1, range(XT, XT + CT))][:1 + with_ctx]
                self.groups = [(kt, r, tiles) for kt in range(KT) for r, tiles in kinds]
                self.g0 = ht_turned.plan(len(self.groups))
                for s in (ht_high, ht_low):
                    s.plan(len(self.groups))
                self.f0 = ht_full.plan(len(self.groups))
                self.bank_signal, self.bank0 = ht_full, self.f0

            def scalar(self, act):
                for _ in range(2):
                    weights_high(act, *self.prime)
                for step in range(self.T + 1):
                    t = step
                    if t < self.T:
                        if self.added is not None and t < self.before.T:
                            act.wait_ge(x_added.sem, self.added + t + 1)
                        act.wait_ge(sq_ready.sem, self.q0 + t)
                        act.activation(junk[:, :], X[:, t, :], ACT.Square, accum_out=sumsq[:, 1, t:t + 1]).then_inc(sq_ready.sem, 1)
                    t = step - 1
                    if t >= 0:
                        act.wait_ge(rstd_ready.sem, self.r0 + t + 1)
                        act.activation(xn[:, t, :], X[:, t, :], ACT.Copy, scale=rstd[:, 8 + t:9 + t]).then_inc(xn_ready.sem, 1)
                for g, (kt, r, tiles) in enumerate(self.groups):
                    n = len(tiles) * P
                    act.wait_ge(ht_full.sem, self.f0 + g + 1)
                    act.activation(HT[:, 0, kt, tiles[0] * P:tiles[0] * P + n], h_full[:, g % 2, 0:n], ACT.Copy).then_inc(ht_high.sem, 1)

            def vector(self, dve):
                for g, (kt, r, tiles) in enumerate(self.groups):
                    n = len(tiles) * P
                    dve.wait_ge(ht_turned.sem, self.g0 + g + 1)
                    if g >= 2:
                        dve.wait_ge(ht_low.sem, self.g0 + g - 1)
                    dve.tensor_scalar(h_full[:, g % 2, 0:n], ps[:, g % 8, 0:n], mod_cols[:, self.scale, kt, r:r + 1],
                                      mod_cols[:, self.shift, kt, r:r + 1], ALU.mult, ALU.add).then_inc(ht_full.sem, 1)

            def gpsimd(self, pool):
                weights_low(pool, *self.prime)
                for t in range(self.T):
                    row_rstd(pool, 1, t, self.q0 + t + 1)
                weights_low(pool, *self.prime)
                for g, (kt, r, tiles) in enumerate(self.groups):
                    n = len(tiles) * P
                    hi = HT[:, 0, kt, tiles[0] * P:tiles[0] * P + n]
                    pool.wait_ge(ht_full.sem, self.f0 + g + 1)
                    pool.wait_ge(ht_high.sem, self.g0 + g + 1)
                    pool.tensor_tensor(HT[:, 1, kt, tiles[0] * P:tiles[0] * P + n], h_full[:, g % 2, 0:n], hi.bitcast(F32),
                                       ALU.subtract).then_inc(ht_low.sem, 1)

            def tensor(self, pe):
                for g, (kt, r, tiles) in enumerate(self.groups):
                    if g >= 8:
                        pe.wait_ge(ht_full.sem, self.f0 + g - 7)
                    for i, t in enumerate(tiles):
                        if kt == 0:
                            pe.wait_ge(xn_ready.sem, self.x0 + t + 1)
                        ins = pe.transpose(ps[:, g % 8, i * P:(i + 1) * P], xn[:, t, kt * P:(kt + 1) * P], ident)
                    ins.then_inc(ht_turned.sem, 1)

            def sync(self, sp):
                if self.sp:
                    self.sp(sp)

        class MixTransposed:
            prime = (2, HALF)

            def __init__(self, src, tiles):
                self.src = src
                kinds = [range(0, XT), range(XT, tiles)][:1 + (tiles > XT)]
                self.groups = [(kt, kind) for kt in range(KT) for kind in kinds]
                self.g0 = ht_turned.plan(len(self.groups))
                for s in (ht_high, ht_low):
                    s.plan(len(self.groups))
                self.bank_signal, self.bank0 = ht_low, self.g0

            def tensor(self, pe):
                for g, (kt, tiles) in enumerate(self.groups):
                    if g >= 8:
                        pe.wait_ge(ht_low.sem, self.g0 + g - 7)
                    for i, t in enumerate(tiles):
                        ins = pe.transpose(ps[:, g % 8, i * P:(i + 1) * P], self.src(t, kt), ident)
                    ins.then_inc(ht_turned.sem, 1)

            def scalar(self, act):
                for _ in range(2):
                    weights_high(act, *self.prime)
                for g, (kt, tiles) in enumerate(self.groups):
                    n = len(tiles) * P
                    act.wait_ge(ht_turned.sem, self.g0 + g + 1)
                    act.activation(HT[:, 0, kt, tiles[0] * P:tiles[0] * P + n], ps[:, g % 8, 0:n], ACT.Copy).then_inc(ht_high.sem, 1)

            def vector(self, dve):
                for g, (kt, tiles) in enumerate(self.groups):
                    n = len(tiles) * P
                    dve.wait_ge(ht_high.sem, self.g0 + g + 1)
                    dve.tensor_tensor(HT[:, 1, kt, tiles[0] * P:tiles[0] * P + n], ps[:, g % 8, 0:n],
                                      HT[:, 0, kt, tiles[0] * P:tiles[0] * P + n].bitcast(F32), ALU.subtract).then_inc(ht_low.sem, 1)

            def gpsimd(self, pool):
                for _ in range(2):
                    weights_low(pool, *self.prime)

            def sync(self, sp):
                pass

        acc_ready, acc_free = signal("acc_ready"), signal("acc_free")

        class Linear:

            def __init__(self, w, chunks, dst, mods=()):
                self.w, self.chunks, self.dst = w, chunks, dst
                self.mods = list(mods) + [[]] * (len(chunks) - len(mods))
                self.a0 = acc_ready.plan(sum(len(t) - 1 for _, _, t in chunks))
                self.f0 = acc_free.plan(sum(len(t) for _, _, t in chunks))
                self.w0 = w_used.plan(4 * len(chunks))
                self.residual = None
                self.source = schedule[-1]
                self.beside = {"dve": {}, "act": {}, "pool": {}}

            def wait_copied(self, eng, c):
                eng.wait_ge(acc_free.sem, self.f0 + sum(len(t) for _, _, t in self.chunks[:c + 1]))

            def sync(self, sp):
                for (c0, n, tiles), jobs in zip(self.chunks, self.mods):
                    for q in range(4):
                        weights_load(sp, self.w[q * 256:(q + 1) * 256, c0:c0 + n], 2, n)
                        if len(jobs) == 1:
                            jobs[0].load(sp, q)
                        if len(jobs) == 2:
                            jobs[q // 2].load(sp, 2 * (q % 2))
                            jobs[q // 2].load(sp, 2 * (q % 2) + 1)

            def scalar(self, act):
                before = []
                for c, ((c0, n, tiles), jobs) in enumerate(zip(self.chunks, self.mods)):
                    steps = self.beside["act"].get(c, [])
                    for q in range(4):
                        if c or q >= 2:
                            weights_high(act, 2, n)
                        if q < len(steps):
                            steps[q](act)
                        if q == 1:
                            for job in before:
                                job.keep(act)
                    before = jobs
                for job in before:
                    job.keep(act)
                for step in self.beside["act"].get(len(self.chunks), []):
                    step(act)
                if self.residual:
                    T = self.residual.T
                    for t in range(T):
                        act.wait_ge(acc_free.sem, self.f0 + T + t + 1)
                        self.residual.square(act, t, res_junk[:, :])

            def gpsimd(self, pool):
                for c, (c0, n, tiles) in enumerate(self.chunks):
                    steps = self.beside["pool"].get(c, [])
                    for q in range(4):
                        if c or q >= 2:
                            weights_low(pool, 2, n)
                        if q < len(steps):
                            steps[q](pool)

            def tensor(self, pe):
                first = 0
                for (c0, n, tiles), jobs in zip(self.chunks, self.mods):
                    for q in range(4):
                        w = weights_use(pe, 2, n)
                        for i, t in enumerate(tiles, first):
                            if q == 0 and i >= 6:
                                pe.wait_ge(acc_free.sem, self.f0 + i - 5)
                            elif q == 0:
                                wait_bank(pe, self.source, i)
                            for j in range(2):
                                kt = 2 * q + j
                                if first == 0 and i == 0:
                                    wait_features(pe, self.source, kt)
                                ins = matmul3(pe, ps[:, i % 6, 0:n], [HT[:, s, kt, t * P:(t + 1) * P] for s in range(2)],
                                              [w[s][:, j, :] for s in range(2)], start=(kt == 0), stop=(kt == KT - 1))
                            if q == 3 and t != tiles[-1]:
                                ins.then_inc(acc_ready.sem, 1)
                        ins.then_inc(w_used.sem, 1)
                    if first == 0 and jobs:
                        wait_bank(pe, self.source, 6)
                        wait_bank(pe, self.source, 7)
                    first += len(tiles)
                    for job in jobs:
                        job.turn(pe)

            def vector(self, dve):
                i = ready = 0
                for c, ((c0, n, tiles), jobs) in enumerate(zip(self.chunks, self.mods)):
                    for job in jobs:
                        for q in range(4):
                            job.sum(dve, q)
                    for step in self.beside["dve"].get(c, []):
                        step(dve)
                    for t in tiles:
                        if t != tiles[-1]:
                            ready += 1
                            dve.wait_ge(acc_ready.sem, self.a0 + ready)
                        else:
                            dve.wait_ge(w_used.sem, self.w0 + 4 * (c + 1))
                        dve.tensor_copy(self.dst(t, c0, n), ps[:, i % 6, 0:n]).then_inc(acc_free.sem, 1)
                        i += 1

        y_gated = signal("y_gated")

        class Residual:

            def __init__(self, gates, last=False):
                self.gates, self.T, self.last = gates, len(gates), last
                self.q0, self.r0, self.x0 = sq_ready.plan(self.T), rstd_ready.plan(self.T), x_added.plan(self.T)
                self.y0 = y_gated.plan(self.T)
                schedule[-1].residual = self

            def square(self, act, t, junk):
                if t:
                    act.wait_ge(sq_ready.sem, self.q0 + t)
                act.activation(junk, Y[:, t, :], ACT.Square, accum_out=sumsq[:, 0, t:t + 1]).then_inc(sq_ready.sem, 1)

            def gpsimd(self, pool):
                for t in range(self.T):
                    row_rstd(pool, 0, t, self.q0 + t + 1)

            def vector(self, dve):
                for step in range(self.T + 1):
                    t = step
                    if t < self.T:
                        dve.tensor_tensor(Y[:, t, :], Y[:, t, :], gate_rows[:, self.gates[t], :], ALU.mult).then_inc(y_gated.sem, 1)
                    t = step - 1
                    if t >= 0:
                        dve.wait_ge(y_gated.sem, self.y0 + t + 1)
                        dve.wait_ge(rstd_ready.sem, self.r0 + t + 1)
                        dve.scalar_tensor_tensor(out=X[:, t, :], in0=Y[:, t, :], scalar=rstd[:, t:t + 1], in1=X[:, t, :],
                                                 op0=ALU.mult, op1=ALU.add).then_inc(x_added.sem, 1)

            def tensor(self, pe):
                pass

            def scalar(self, act):
                pass

            def sync(self, sp):
                pass

        s_scored, s_max, s_exp, s_turned, s_kept_a, s_kept_v, s_summed, s_out, s_joined = (signal("att_" + n) for n in (
            "scored", "max", "exp", "turned", "kept_act", "kept_dve", "summed", "out", "joined"))

        class Attention:

            def __init__(self, units, probs, probs_t, stats, neg_sinks=None, sinks=None, neg_lambda=None):
                self.units, self.probs, self.probs_t, self.stats = units, probs, probs_t, stats
                self.neg_sinks, self.sinks, self.neg_lambda = neg_sinks, sinks, neg_lambda
                self.buffers = probs.shape[1]
                n = len(units)
                self.held, self.lag = (4, 4) if max(len(un["values"]) for un in units) <= 4 else (2, 2)
                self.order = {u: i for i, u in enumerate(u for u in range(n) if "second" not in units[u])}
                self.joined = {u: i for i, u in enumerate(u for u in range(n) if "first" in units[u])}
                m = len(self.order)
                self.b = {s: s.plan(n) for s in (s_scored, s_max, s_exp)}
                self.b.update({s: s.plan(m) for s in (s_turned, s_summed, s_out)})
                self.b[s_joined] = s_joined.plan(len(self.joined))
                by_vector = lambda u, i: u in self.joined if self.joined else i % 3 == 1 and self.held == 2
                self.kept = [(s, s.plan(1) + 1) for s in (s_kept_v if by_vector(u, i) else s_kept_a for u, i in self.order.items())]

            def wait_probs_ready(self, eng, u):
                if u in self.joined:
                    self.wait(eng, s_joined, self.joined[u] + 1)
                else:
                    self.wait(eng, s_exp, u + 1)

            def wait_probs_read(self, eng, u):
                if u in self.order:
                    self.wait(eng, s_turned, self.order[u] + 1)
                else:
                    self.wait(eng, s_joined, self.joined[self.units[u]["second"]] + 1)

            def wait(self, eng, s, count):
                if count > 0:
                    eng.wait_ge(s.sem, self.b[s] + count)

            def wait_kept(self, eng, u):
                if u >= 0:
                    s, count = self.kept[u]
                    eng.wait_ge(s.sem, count)

            def scores(self, u):
                if self.held == 4:
                    return ps[:, u % 4, :]
                return ps[:, 2 * (u % 2):2 * (u % 2) + 2, :].rearrange("p b n -> p (b n)")

            def tensor(self, pe):
                n = len(self.units)
                for step in range(n + self.lag + 1):
                    u = step
                    if u < n:
                        un, sc = self.units[u], self.scores(u)
                        self.wait(pe, s_exp, u - self.held + 1)
                        for bank in range(2):
                            for k, c in [(k, c) for k, c in un["keys"] if c // HALF == bank]:
                                masks = [(m, mc) for m, mc in un["mask"] if c <= mc < c + k.shape[1]]
                                ins = pe.matmul(sc[:, c:c + k.shape[1]], un["q"], k, start=True, stop=not masks)
                                for m, mc in masks:
                                    ins = pe.matmul(sc[:, mc:mc + P], identb[:, :], m, start=False, stop=(mc == masks[-1][1]))
                        ins.then_inc(s_scored.sem, 1)
                    u = step - self.lag
                    if u in self.order:
                        blocks = len(self.units[u]["values"])
                        self.wait_probs_ready(pe, u)
                        self.wait_kept(pe, self.order[u] - 1)
                        for b in range(blocks):
                            ins = pe.transpose(ps[:, 4 + b // 4, (b % 4) * P:(b % 4 + 1) * P],
                                               self.probs[:, u % self.buffers, b * P:(b + 1) * P], ident)
                        ins.then_inc(s_turned.sem, 1)
                    u = step - self.lag - 1
                    if u in self.order:
                        vals, o = self.units[u]["values"], self.order[u]
                        self.wait_kept(pe, o)
                        self.wait(pe, s_out, o - 1)
                        for b, v in enumerate(vals):
                            ins = pe.matmul(ps[:, 6 + o % 2, 0:v.shape[1]], self.probs_t[:, o % 2, b * P:(b + 1) * P], v,
                                            start=(b == 0), stop=(b == len(vals) - 1))
                        ins.then_inc(s_summed.sem, 1)

            def copy_probs(self, eng, act, u, sig):
                w, o = len(self.units[u]["values"]) * P, self.order[u]
                eng.wait_ge(s_turned.sem, self.b[s_turned] + o + 1)
                self.wait(eng, s_summed, o - 1)
                src = ps[:, 4:6, :].rearrange("p b n -> p (b n)")[:, 0:w]
                dst = self.probs_t[:, o % 2, 0:w]
                (eng.activation(dst, src, ACT.Copy) if act else eng.tensor_copy(dst, src)).then_inc(sig.sem, 1)

            def copy_by(self, eng, sig, u):
                if u in self.order and self.kept[self.order[u]][0] is sig:
                    self.copy_probs(eng, sig is s_kept_a, u, sig)

            def scalar(self, act):
                n, st = len(self.units), self.stats
                for step in range(n + self.lag):
                    self.copy_by(act, s_kept_a, step - self.lag)
                    u = step
                    if u < n:
                        un = self.units[u]
                        w, r = len(un["values"]) * P, u % 8
                        act.wait_ge(s_max.sem, self.b[s_max] + u + 1)
                        if u >= self.buffers:
                            self.wait_probs_read(act, u - self.buffers)
                        if u >= 8:
                            self.wait(act, s_out, self.order[self.units[u - 8].get("second", u - 8)] + 1)
                        ins = act.activation(self.probs[:, u % self.buffers, 0:w], self.scores(u)[:, 0:w], ACT.Exp, bias=st[:, 1, r:r + 1],
                                             scale=un["scale"], accum_out=st[:, 2, r:r + 1])
                        if un["sink"] is not None:
                            h = un["sink"]
                            ins = act.activation(st[:, 3, r:r + 1], st[:, 1, r:r + 1], ACT.Exp, bias=self.sinks[:, h:h + 1])
                        ins.then_inc(s_exp.sem, 1)

            def vector(self, dve):
                n, st = len(self.units), self.stats
                for step in range(n + self.lag + 1):
                    u = step
                    if u < n:
                        un = self.units[u]
                        w, r = len(un["values"]) * P, u % 8
                        dve.wait_ge(s_scored.sem, self.b[s_scored] + u + 1)
                        dve_s.chain(dve.tensor_reduce(st[:, 0, r:r + 1], self.scores(u)[:, 0:w], AX, ALU.max))
                        if un["sink"] is not None:
                            h = un["sink"]
                            ins = dve.tensor_scalar(st[:, 1, r:r + 1], st[:, 0, r:r + 1], -un["scale"], self.neg_sinks[:, h:h + 1],
                                                    ALU.mult, ALU.min)
                        else:
                            ins = dve.tensor_scalar(st[:, 1, r:r + 1], st[:, 0, r:r + 1], -un["scale"], None, ALU.mult)
                        ins.then_inc(s_max.sem, 1)
                    u = step - 1
                    if u in self.joined:
                        r, v = u % 8, self.units[u]["first"]
                        w = len(self.units[u]["values"]) * P
                        dve.wait_ge(s_exp.sem, self.b[s_exp] + u + 1)
                        dve_s.chain(dve.reciprocal(st[:, 5, r:r + 1], st[:, 2, r:r + 1]))
                        dve_s.chain(dve.scalar_tensor_tensor(out=st[:, 6, r:r + 1], in0=st[:, 5, r:r + 1], scalar=self.neg_lambda,
                                                             in1=st[:, 2, v % 8:v % 8 + 1], op0=ALU.mult, op1=ALU.mult))
                        p_u, p_v = (self.probs[:, z % self.buffers, 0:w] for z in (u, v))
                        dve.scalar_tensor_tensor(out=p_u, in0=p_u, scalar=st[:, 6, r:r + 1], in1=p_v, op0=ALU.mult, op1=ALU.add)\
                           .then_inc(s_joined.sem, 1)
                    u = step - self.lag
                    self.copy_by(dve, s_kept_v, u)
                    u = step - self.lag - 1
                    if u in self.order:
                        un, o = self.units[u], self.order[u]
                        r, dv = un.get("first", u) % 8, un["values"][0].shape[1]
                        total, inv = st[:, 2, r:r + 1], st[:, 5, r:r + 1]
                        dve.wait_ge(s_exp.sem, self.b[s_exp] + u + 1)
                        if un["sink"] is not None:
                            dve_s.chain(dve.tensor_tensor(st[:, 4, r:r + 1], total, st[:, 3, r:r + 1], ALU.add))
                            total = st[:, 4, r:r + 1]
                        dve_s.chain(dve.reciprocal(inv, total))
                        kind, dst, other = un["finish"]
                        dve.wait_ge(s_summed.sem, self.b[s_summed] + o + 1)
                        sums = ps[:, 6 + o % 2, 0:dv]
                        if kind == "plain":
                            ins = dve.tensor_scalar(dst, sums, inv, None, ALU.mult)
                        else:
                            ins = dve.scalar_tensor_tensor(out=dst, in0=sums, scalar=inv, in1=other, op0=ALU.mult, op1=ALU.mult)
                        ins.then_inc(s_out.sem, 1)

            def gpsimd(self, pool):
                pass

            def sync(self, sp):
                pass

        def rotate(eng, steps, dst, src, cos, sin, heads, groups, half, tmp):
            w = groups * 2 * half
            v = lambda z: z.rearrange("p (h w) -> p h w", w=w)
            cb = cos.unsqueeze(1).to_broadcast([P, heads, w])
            full = lambda z: z.rearrange("p (h g s d) -> p h g s d", g=groups, s=2, d=half)
            sb_ = sin.rearrange("p (g s d) -> p g s d", s=2, d=half)
            n = heads * w
            for s in range(2):
                sc = sb_[:, :, s, :].unsqueeze(1).to_broadcast([P, heads, groups, half])
                a_, b_ = full(tmp[:, 0:n])[:, :, :, s, :], full(src)[:, :, :, 1 - s, :]
                ins = eng.tensor_tensor(a_, b_, sc, ALU.mult)
            steps.chain(ins)
            steps.chain(eng.tensor_tensor(v(dst), v(src), cb, ALU.mult))
            return eng.tensor_tensor(dst, dst, tmp[:, 0:n], ALU.add)

        made, kept_a, kept_v = signal("piece_made"), signal("piece_kept_act"), signal("piece_kept_dve")

        def turn(srcs):
            return [("turn", s.shape[1], i * P, s) for i, s in enumerate(srcs)]

        class Pieces:

            def __init__(self, groups, pool=None):
                self.groups, self.pool = groups, pool
                self.t0 = made.plan(len(groups))
                self.kept = []
                free = 0
                for g in groups:
                    if "mask" in g or free % 2:
                        s = kept_v
                    else:
                        s = kept_a
                    free += "mask" not in g
                    self.kept.append((s, s.plan(1) + 1))

            def tensor(self, pe):
                for g, group in enumerate(self.groups):
                    if g >= 8:
                        sig, count = self.kept[g - 8]
                        pe.wait_ge(sig.sem, count)
                    b = g % 8
                    for op in group["ops"]:
                        if op[0] == "turn":
                            _, m, col, src = op
                            ins = pe.transpose(ps[0:m, b, col:col + P], src, ident)
                        else:
                            _, (p0, p1), col, n, pairs = op[:5]
                            first, last = op[5] if len(op) > 5 else (True, True)
                            for i, (l, r) in enumerate(pairs):
                                ins = pe.matmul(ps[p0:p1, b, col:col + n], l, r, start=(i == 0 and first),
                                                stop=(i == len(pairs) - 1 and last), skip_group_check=len(op) > 5)
                    ins.then_inc(made.sem, 1)

            def keep(self, eng, sig):
                for g, group in enumerate(self.groups):
                    if self.kept[g][0] is not sig:
                        continue
                    eng.wait_ge(made.sem, self.t0 + g + 1)
                    for p0, p1, dst in group["dsts"]:
                        n = int(np.prod(dst.shape[1:]))
                        src = ps[p0:p1, g % 8, 0:n]
                        if len(dst.shape) == 3:
                            src = src.rearrange("p (a b) -> p a b", b=dst.shape[2])
                        if "mask" in group:
                            ins = eng.tensor_tensor(dst, src, group["mask"], ALU.mult)
                        elif sig is kept_a:
                            ins = eng.activation(dst, src, ACT.Copy, scale=group.get("scale", 1.0))
                        elif "scale" in group:
                            ins = eng.tensor_scalar(dst, src, group["scale"], None, ALU.mult)
                        else:
                            ins = eng.tensor_copy(dst, src)
                    ins.then_inc(sig.sem, 1)

            def scalar(self, act):
                self.keep(act, kept_a)

            def vector(self, dve):
                self.keep(dve, kept_v)

            def gpsimd(self, pool):
                if self.pool:
                    self.pool(pool)

            def sync(self, sp):
                pass

        class Work:

            def __init__(self, act=None, dve=None, pool=None, sp=None):
                none = lambda eng: None
                self.scalar, self.vector, self.gpsimd, self.sync = act or none, dve or none, pool or none, sp or none

            def tensor(self, pe):
                pass

        f_silu, f_full, f_high, f_low = (signal("ffn_" + n) for n in ("silu", "full", "high", "low"))
        f_out, f_added = signal("ffn_out_ready"), signal("ffn_out_added")
        GROUP = 256
        GROUPS = FFN // GROUP
        silu_t = at("ffn_silu", [P, 2, TOK], F32, aux_at)
        ffn_junk = at("ffn_square_junk", [P, D], F32, aux_at + D * 4)
        full_t = at("ffn_full", [P, 2, TOK], F32, aux_at + 2 * TOK * 4)

        class FeedForward:

            def __init__(self, w_in, w_out, tiles, mods=((), (), (), ())):
                self.w_in, self.w_out, self.T = w_in, w_out, tiles
                self.mods = mods
                self.residual = None
                self.source = schedule[-1]
                self.segs = [(0, HALF)] if tiles == XT else [(0, 384), (384, 384)]
                self.parts = [range(i, min(i + 3, GROUPS)) for i in range(0, GROUPS, 3)]
                self.b = {s: s.plan(n) for s, n in ((f_silu, GROUPS), (f_full, 2 * GROUPS), (f_high, 2 * GROUPS), (f_low, 2 * GROUPS),
                                                    (f_out, len(self.parts) * 2 * (tiles - 1)), (f_added, len(self.parts) * 2 * tiles))}
                self.w0 = w_used.plan(6 * GROUPS)
                self.gate_unit, self.up_unit, self.out_unit, u = {}, {}, {}, 0
                for p, part in enumerate(self.parts):
                    for g in part:
                        self.gate_unit[g], self.up_unit[g] = self.w0 + u + 2, self.w0 + u + 4
                        u += 4
                    for h in range(2):
                        u += len(part)
                        self.out_unit[p, h] = self.w0 + u

            def wait(self, eng, s, n):
                if n > 0:
                    eng.wait_ge(s.sem, self.b[s] + n)

            def mod_units(self, p):
                return [(job, q) for job in self.mods[p] for q in range(4)]

            def sync(self, sp):
                for p, part in enumerate(self.parts):
                    units = self.mod_units(p)
                    for g in part:
                        for off in (0, FFN):
                            for half in range(2):
                                weights_load(sp, self.w_in[half * HALF:(half + 1) * HALF, off + g * GROUP:off + (g + 1) * GROUP], 4, GROUP)
                                for _ in range(0 if off and half else 2 if len(part) == 2 and not (off or half) else 1):
                                    if units:
                                        job, q = units.pop(0)
                                        job.load(sp, q)
                    for n in range(2):
                        for g in part:
                            weights_load(sp, self.w_out[g * GROUP:(g + 1) * GROUP, n * HALF:(n + 1) * HALF], 2, HALF)

            def split_hidden(self, eng, g, act):
                n, lane = self.T * P, g % 3
                for a in range(2):
                    full = full_t[:, a, 0:n]
                    high, low = (act_t[:, s, 2 * lane + a, 0:n] for s in range(2))
                    self.wait(eng, f_full, 2 * g + a + 1)
                    if act:
                        eng.activation(high, full, ACT.Copy).then_inc(f_high.sem, 1)
                    else:
                        self.wait(eng, f_high, 2 * g + a + 1)
                        eng.tensor_tensor(low, full, high.bitcast(F32), ALU.subtract).then_inc(f_low.sem, 1)

            def scalar(self, act):
                n, before = self.T * P, None
                w, k = self.segs[0][1], len(self.segs)
                for p, part in enumerate(self.parts):
                    for g in part:
                        if g:
                            weights_high(act, 4, GROUP)
                            weights_high(act, 4, GROUP)
                        if before is not None:
                            self.split_hidden(act, before, True)
                        weights_high(act, 4, GROUP)
                        weights_high(act, 4, GROUP)
                        act.wait_ge(w_used.sem, self.gate_unit[g])
                        self.wait(act, f_full, 2 * g)
                        for a in range(2):
                            ins = act.activation(silu_t[:, a, 0:n].rearrange("p (s w) -> p s w", w=w), ps[:, a * k:(a + 1) * k, 0:w], ACT.Silu)
                        ins.then_inc(f_silu.sem, 1)
                        before = g
                    for i in range(2 * len(part)):
                        weights_high(act, 2, HALF)
                        if i == 1:
                            self.split_hidden(act, before, True)
                            before = None
                        if i == len(part) + 1:
                            for job in self.mods[p]:
                                job.keep(act)
                for t in range(self.T):
                    self.wait(act, f_added, (2 * len(self.parts) - 1) * self.T + t + 1)
                    self.residual.square(act, t, ffn_junk[:, :])

            def gpsimd(self, pool):
                before = None
                for part in self.parts:
                    for g in part:
                        if g:
                            weights_low(pool, 4, GROUP)
                            weights_low(pool, 4, GROUP)
                        if before is not None:
                            self.split_hidden(pool, before, False)
                        weights_low(pool, 4, GROUP)
                        weights_low(pool, 4, GROUP)
                        before = g
                    for i in range(2 * len(part)):
                        weights_low(pool, 2, HALF)
                        if i == 1:
                            self.split_hidden(pool, before, False)
                            before = None

            def vector(self, dve):
                w, k, i = self.segs[0][1], len(self.segs), 0
                n = self.T * P
                for p, part in enumerate(self.parts):
                    units = self.mod_units(p)
                    for g in part:
                        for _ in range(3 if len(part) == 3 else 4):
                            if units:
                                job, q = units.pop(0)
                                job.sum(dve, q)
                        self.wait(dve, f_silu, g + 1)
                        dve.wait_ge(w_used.sem, self.up_unit[g])
                        self.wait(dve, f_low, 2 * g)
                        for a in range(2):
                            view = lambda z: z[:, a, 0:n].rearrange("p (s w) -> p s w", w=w)
                            dve.tensor_tensor(view(full_t), ps[:, 4 + a * k:4 + (a + 1) * k, 0:w], view(silu_t), ALU.mult)\
                               .then_inc(f_full.sem, 1)
                    for h in range(2):
                        for t in range(self.T):
                            i += 1
                            y = Y[:, t, h * HALF:(h + 1) * HALF]
                            if t < self.T - 1:
                                self.wait(dve, f_out, i - (2 * p + h))
                            else:
                                dve.wait_ge(w_used.sem, self.out_unit[p, h])
                            if p == 0:
                                ins = dve.tensor_copy(y, ps[:, t, :])
                            else:
                                self.wait(dve, f_added, i - 2 * self.T)
                                ins = dve.tensor_tensor(y, y, ps[:, t, :], ALU.add)
                            ins.then_inc(f_added.sem, 1)

            def tensor(self, pe):
                k, i = len(self.segs), 0
                for p, part in enumerate(self.parts):
                    for g in part:
                        for what, free in ((0, f_silu), (4, f_full)):
                            for half in range(2):
                                w = weights_use(pe, 4, GROUP)
                                if half == 0:
                                    self.wait(pe, free, g if free is f_silu else 2 * g)
                                    if what and p and g == part[0] and self.mods[p - 1]:
                                        job = self.mods[p - 1][-1]
                                        pe.wait_ge(mod_kept.sem, job.turn0 + job.turns)
                                for a in range(2):
                                    for s, (c0, n) in enumerate(self.segs):
                                        bank = what + a * k + s
                                        if half == 0 and p and g == part[0] and bank < self.T:
                                            self.wait(pe, f_added, i - self.T + bank + 1)
                                        if g == 0 and half == 0:
                                            wait_bank(pe, self.source, bank)
                                        for j in range(4):
                                            kt = 4 * half + j
                                            if g == 0 and what == 0 and a == 0 and s == 0:
                                                wait_features(pe, self.source, kt)
                                            ins = matmul3(pe, ps[:, bank, 0:n], [z[:, j, a * P:(a + 1) * P] for z in w],
                                                          [HT[:, z, kt, c0:c0 + n] for z in range(2)], kt == 0, kt == KT - 1)
                                ins.then_inc(w_used.sem, 1)
                    for h in range(2):
                        for m, g in enumerate(part):
                            w = weights_use(pe, 2, HALF)
                            self.wait(pe, f_low, 2 * g + 2)
                            for t in range(self.T):
                                if m == 0 and h:
                                    self.wait(pe, f_added, i - self.T + t + 1)
                                elif m == 0 and t in (0, 4):
                                    self.wait(pe, f_silu, part[-1] + 1) if t == 0 else self.wait(pe, f_full, 2 * part[-1] + 2)
                                for j in range(2):
                                    lane = 2 * (g % 3) + j
                                    ins = matmul3(pe, ps[:, t, :], [act_t[:, z, lane, t * P:(t + 1) * P] for z in range(2)],
                                                  [z[:, j, :] for z in w], m == 0 and j == 0, m == len(part) - 1 and j == 1)
                                if m == len(part) - 1 and t < self.T - 1:
                                    ins.then_inc(f_out.sem, 1)
                            ins.then_inc(w_used.sem, 1)
                        i += self.T
                        if h == 0:
                            for job in self.mods[p]:
                                job.turn(pe)

        def heads_view(z, h):
            return z.rearrange("p (h d) -> p h d", h=h)

        c1 = np.float32(6.28125)
        c2 = np.float32(np.round((2 * math.pi - 6.28125) * 2 ** 19) / 2 ** 19)
        c3 = np.float32(np.round((2 * math.pi - float(c1) - float(c2)) * 2 ** 31) / 2 ** 31)
        c4 = np.float32(2 * math.pi - float(c1) - float(c2) - float(c3))
        MAGIC = 1.5 * 2.0 ** 23

        take = region(arena)
        P1 = take("proj_one", [P, XT, IN1])
        cos1 = take("cos_one", [P, XT, 2, 64])
        sin1 = take("sin_one", [P, XT, 2, 64])
        rope_tmp_one = take("rope_tmp_one", [P, 640])
        angles_at = take.where[0]
        reduced = take("reduced_angles", [P, 2, XT, 2, 64])
        turns = at("turns", [P, XT, 2, 64], F32, take.where[0] - 2 * XT * 2 * 64 * 4 - 640 * 4)
        angle = at("angle", [P, XT, 2, 64], F32, aux_at)
        take = region(aux_at)
        gqT, gkT = take("gla_q_t", [P, S]), take("gla_k_t", [P, S])
        gaT = take("gla_a_t", [16, S])
        one_end = take.where[0]
        con1 = at("constants_one", [P, ONE_W], F32, gate_rows_at + 4 * D)
        assert ONE_W * 4 <= 3 * 4 * D
        c1t = lambda name: con1[:, slice(*ONE_COLS[name])]
        small = region(small_at)
        pos_i, pos_f = small("positions_int", [P, XT], I32), small("positions", [P, XT])
        sinks = small("sinks", [P, 8])
        neg_sinks = small("neg_sinks", [P, 8])
        stats = small("attention_stats", [P, 7, 8])
        gate_w = small("gla_gate_w", [16, P])
        gate_b = small("gla_gate_b", [P, 1])
        gla_gains = small("gla_gains", [P, 2, 64])
        headsq = small("head_squares", [P, 64])
        headms = small("head_meansq", [P, 64])
        headr = small("head_rstd", [P, 64])
        half64 = small("minus_half64", [P, 64])
        gla_decay = small("gla_chunk_decay", [P, 8])
        qn_col = small("latent_q_gain", [P, 2])
        kvn_col = small("latent_kv_gain", [P, 1])
        qk_gain = small("qk_gain", [P, 2, 64])
        sub_gain = small("sub_gain", [P, P])
        lam_in = small("lambda_in", [P, 4, 64])
        lam_prod = small("lambda_products", [P, 2, 64])
        lam_sum = small("lambda_sums", [P, 2])
        neg_lam = small("neg_lambda", [P, 1])
        lam_exp = small("lambda_exps", [P, 2])
        lambda_summed, lambda_exped = signal("lambda_summed"), signal("lambda_exped")
        assert small.where[0] <= small_at + SMALL, small.where[0] - small_at
        take = region(ht_at)
        qT, kT = take("att_q_t", [P, 4, S]), take("att_k_t", [P, 2, 2, S])
        probs1 = at("att_probs_one", [P, 4, 2 * P], F32, angles_at)
        probs1_t = take("att_probs_t_one", [P, 2, 2 * P])
        qrT, krT, qdT = take("ret_q_t", [P, 2, S]), take("ret_k_t", [P, 2, 2, S]), take("ret_qdecay_t", [P, 2, S])
        ret_k = take("ret_k_decayed", [P, XT, 256])
        ret_a = at("ret_scores_t", [P, XT, 2, 256], F32, ht_at)
        ret_u = take("ret_updates", [P, XT, 2, P])
        ret_s = take("ret_states", [P, XT, 2, P])
        assert take.where[0] <= ht_end
        take = region(ht_at)
        B = take("gla_log_decay_sums", [P, S])
        gla_a = take("gla_scores_t", [P, 4, S])
        g_dist, g_exp = take("gla_distance", [P, 2, S]), take("gla_factor", [P, 2, S])
        g_k, g_qh = take("gla_k_level", [P, 2, S]), take("gla_q_by_head", [P, 4, S])
        levels_at = take.where[0]
        g_q = take("gla_q_level", [P, 2, 4, S])
        assert take.where[0] <= ht_end
        gla_s = at("gla_states", [P, 8, 256], F32, ht_at + 4 * (S + 4 * S))
        z_t, z_abs, z_min, z_exp = (g_q[:, 1, 2], g_q[:, 1, 3], g_k[:, 0], g_k[:, 1])
        take = region(levels_at)
        g_kd, g_kdt, g_qe = take("gla_k_decayed_t", [P, S]), take("gla_k_decayed", [P, XT, P]), take("gla_q_decayed_t", [P, S])
        gla_u = take("gla_updates", [P, 8, 256])
        log_a, log_a_tok = g_kd[:, :], g_kdt

        def tok(t):
            return slice(t * P, (t + 1) * P)

        schedule = []

        early_landed, angles_ready, sines_ready = signal("early_landed"), signal("angles_ready"), signal("sines_ready")

        def setup_phases():
            early = [
                (c_raw[:, 0, :], a["c"][0].rearrange("(k p) -> p k", p=P)),
                (c_raw[:, 1, :], a["c_2"][0].rearrange("(k p) -> p k", p=P)),
                (c_raw[:, 2, :], a["c_ctx_2"].rearrange("(k p) -> p k", p=P)),
                (con[:, :], a["static"]),
            ]

            def sp(eng):
                for dst, src in early:
                    eng.dma_start(dst, src, allow_slow_non_contiguous=True).then_inc(early_landed.sem, 16)

            def act(eng):
                eng.wait_ge(early_landed.sem, 16 * len(early))
                for cond, r, raw in ((0, 0, 0), (0, 1, 0), (1, 0, 1), (1, 1, 2)):
                    eng.activation(c_act[:, cond, :, r], c_raw[:, raw, :], ACT.Silu)

            def dve(eng):
                eng.memset(mod_bias[:, :, :].rearrange("p b n -> p (b n)"), 0.0).then_inc(mod_ready.sem, 1)
                eng.memset(minus_half[:, :], -0.5)
                eng.memset(half64[:, :], -0.5)
                eng.memset(headsq[:, :], 1.0)
                eng.memset(headms[:, :], 1.0)
                eng.wait_ge(early_landed.sem, 16 * len(early))
                eng.tensor_copy(identb[:, :], ident)

            schedule.append(Work(act=act, dve=dve, sp=sp))

        def angles(eng):
            dve_s.chain(eng.tensor_copy(pos_f[:, :], pos_i[:, :]))
            f = c1t("freqs").rearrange("p (k n) -> p k n", k=2)
            for t in range(XT):
                ins = eng.tensor_scalar(angle[:, t], f, pos_f[:, t:t + 1], None, ALU.mult)
            dve_s.chain(ins)
            for which, quarter in ((0, 0.0), (1, 0.25)):
                r = reduced[:, which]
                dve_s.chain(eng.tensor_scalar(turns[:], angle[:], 1.0 / (2 * math.pi), quarter, ALU.mult, ALU.add))
                dve_s.chain(eng.tensor_scalar(turns[:], turns[:], MAGIC, None, ALU.add))
                dve_s.chain(eng.tensor_scalar(turns[:], turns[:], MAGIC, None, ALU.subtract))
                flat = lambda z: z.rearrange("p t k n -> p (t k n)")
                for i, part in enumerate((c1, c2, c3, c4)):
                    dve_s.chain(eng.scalar_tensor_tensor(out=flat(r), in0=flat(turns[:]), scalar=-float(part),
                                                         in1=flat(angle[:] if i == 0 else r), op0=ALU.mult, op1=ALU.add))
                dve_s.chain(eng.tensor_scalar(r, r, math.pi / 2 * which, 3.1415925, ALU.add, ALU.min))
                eng.tensor_scalar(r, r, -3.1415925, None, ALU.max).then_inc(angles_ready.sem, 1)

        def sines(eng):
            eng.wait_ge(angles_ready.sem, 2)
            eng.activation(cos1[:], reduced[:, 1], ACT.Sin).then_inc(sines_ready.sem, 1)
            for s, sign in ((0, -1.0), (1, 1.0)):
                eng.activation(sin1[:, :, :, 32 * s:32 * s + 32], reduced[:, 0, :, :, 32 * s:32 * s + 32], ACT.Sin, scale=sign)\
                   .then_inc(sines_ready.sem, 1)


        def clear_other_head(eng, keys):
            eng.memset(keys[64:P, :, 0, :], 0.0)
            eng.memset(keys[0:64, :, 1, :], 0.0)

        def key_runs(blocks):
            runs = []
            for i, b in enumerate(blocks):
                if runs and runs[-1][0] + runs[-1][1] == b and i % 4:
                    runs[-1][1] += 1
                else:
                    runs.append([b, 1, i * P])
            return runs

        def mods_one(l, vectors):
            return mod_jobs(a["w_mod"][l], a["b_mod"][l], vectors, [(0, 0)], mod_acc_aux)

        def mods_two(l, vectors, conds, acc=mod_acc_aux):
            return mod_jobs(a["ada_w_2"][l], a["ada_b_2"][l], vectors, [(1, 0), (1, 1)][:conds], acc)

        def prelude_one(l):
            small_loads = [
                (sinks[:, :], a["attn_sinks"][l].partition_broadcast(P)), (gate_w[:, :], a["gla_gate_w"][l]),
                (gate_b[:, :], a["gla_gate_b"][l].rearrange("(p o) -> p o", o=1)),
                (gla_gains[:, l, :], a["gla_norm_gain"][l].partition_broadcast(P)),
            ]
            if l == 0:
                small_loads = [
                    (con1[:, :], a["one"]), (pos_i[:, :], a["positions"][0].rearrange("(t p) -> p t", p=P)),
                    (X[:, XT:, :], a["ctx_2"][0].rearrange("(t p) d -> p t d", p=P))] + small_loads
            loaded = load_in.plan(16 * len(small_loads)) + 16 * len(small_loads)
            barrier = len(schedule)

            def sp(eng):
                if l:
                    sp_waits_phase(eng, barrier)
                for dst, src in small_loads:
                    eng.dma_start(dst, src, allow_slow_non_contiguous=True).then_inc(load_in.sem, 16)

            def dve(eng):
                eng.wait_ge(load_in.sem, loaded)
                eng.tensor_scalar(neg_sinks[:, :], sinks[:, :], -1.0, None, ALU.mult)
                if l == 0:
                    eng.tensor_copy(window[:, :], c1t("window"))

            return sp, dve

        first_sp, first_dve = prelude_one(0)

        def layer_one(l):
            schedule.append(NormTransposed(False, 4 * l, 4 * l + 1, (2, HALF)))
            starts = [0, 512, 1024, 1536, 2048, 2560, IN1 - 256, IN1]
            chunks = [(c0, c1 - c0, range(XT)) for c0, c1 in zip(starts, starts[1:])]
            gates = mods_one(l, [(2, "gate", a["post_norm_gain"][l], [0])])
            if l == 0:
                ahead = mods_one(1, [(0, "shift", None, [4]), (1, "scale", a["pre_norm_gain"][1], [5])])
            else:
                ahead = mods_two(0, [(0, "shift", None, [0]), (1, "scale", a["norm_g_2"][0, 0], [1])], 2)
            schedule.append(Linear(a["w_in"][l], chunks, lambda t, c0, n: P1[:, t, c0:c0 + n], [[job] for job in gates + ahead]))

            linear = schedule[-1]

            def rotate_columns(which, c0, c1, chunk):
                def step(eng):
                    eng.wait_ge(sines_ready.sem, 3)
                    linear.wait_copied(eng, chunk)
                    for t in range(XT):
                        x = P1[:, t, c0:c1]
                        dve_s.chain(rotate(eng, dve_s, x, x, cos1[:, t, which], sin1[:, t, which], (c1 - c0) // 64, 1, 32, rope_tmp_one))
                return step

            def silu_columns(c0, n, chunk, t):
                def step(eng):
                    linear.wait_copied(eng, chunk)
                    x = P1[:, t, c0:c0 + n]
                    eng.activation(x, x, ACT.Silu)
                return step

            linear.beside["dve"] = {2: [rotate_columns(0, AQ, AV, 1)], 4: [rotate_columns(1, RQ, RV, 3)]}
            if l == 0:
                linear.beside["dve"][0] = [first_dve, angles]
            linear.beside["act"] = {c: [silu_columns(c0, n, chunk, t) for t in range(XT)]
                                    for c, c0, n, chunk in ((3, AG, 512, 2), (5, RG, 256, 4), (len(chunks), GG, 256, len(chunks) - 1))}
            if l == 0:
                linear.beside["act"][1] = [sines]

            def tiles_of(c0, m):
                return turn([P1[:, t, c0:c0 + m] for t in range(XT)])

            groups = [dict(ops=tiles_of(AQ + pair * P, P), dsts=[(0, P, qT[:, pair, :])]) for pair in range(4)]
            groups += [dict(ops=tiles_of(AK + g * 64, 64), dsts=[(0, 64, kT[0:64, g, 0, :]), (0, 64, kT[64:P, g, 1, :])]) for g in range(2)]
            groups += [dict(ops=tiles_of(RQ + pair * P, P), dsts=[(0, P, qrT[:, pair, :])]) for pair in range(2)]
            groups += [dict(ops=tiles_of(RK + pair * P, P), dsts=[(0, 64, krT[0:64, pair, 0, :]), (64, P, krT[64:P, pair, 1, :])]) for pair in range(2)]
            groups += [dict(ops=tiles_of(GQ, P), dsts=[(0, P, gqT[:, :])], scale=32 ** -0.5), dict(ops=tiles_of(GK, P), dsts=[(0, P, gkT[:, :])]),
                       dict(ops=tiles_of(GA, 16), dsts=[(0, 16, gaT[:, :])])]
            schedule.append(Pieces(groups, lambda eng: (clear_other_head(eng, kT), clear_other_head(eng, krT))))

            units = []
            for t in range(XT):
                for h in range(8):
                    first = max(t - 1, 0)
                    blocks = list(range(first, t + 1))
                    keys = [(kT[:, h // 4, h % 2, b * P:(b + n) * P], c) for b, n, c in key_runs(blocks)]
                    mask = [(window[:, (0 if b < t else P):(P if b < t else 2 * P)], i * P) for i, b in enumerate(blocks)]
                    o = P1[:, t, AQ + h * 64:AQ + h * 64 + 64]
                    units.append(dict(q=qT[:, h // 2, tok(t)], keys=keys, mask=mask,
                                      values=[P1[:, b, AV + 64 * (h // 4):AV + 64 * (h // 4) + 64] for b in blocks], scale=0.125, sink=h,
                                      finish=("gated", o, P1[:, t, AG + h * 64:AG + h * 64 + 64])))
            schedule.append(Attention(units, probs1, probs1_t, stats, neg_sinks, sinks))

            def dve(eng):
                for pair in range(2):
                    v = lambda z: z[:, pair, :].rearrange("p (t n) -> p t n", n=P)
                    eng.tensor_tensor(v(qdT), v(qrT), c1t("rqdecay")[:, pair * P:(pair + 1) * P].unsqueeze(1).to_broadcast([P, XT, P]), ALU.mult)

            def pool(eng):
                eng.memset(ret_s[:, 0], 0.0)
                for t in range(XT):
                    eng.tensor_tensor(heads_view(ret_k[:, t], 4), heads_view(P1[:, t, RK:RV], 4),
                                      c1t("rkdecay").unsqueeze(2).to_broadcast([P, 4, 64]), ALU.mult)

            schedule.append(Work(dve=dve, pool=pool))
            groups = []
            for t in range(XT):
                for par in range(2):
                    groups.append(dict(ops=[("product", (0, P), pair * P, P, [(krT[:, pair, par, tok(t)], qrT[:, pair, tok(t)])]) for pair in range(2)],
                                       dsts=[(0, P, ret_a[:, t, par])], mask=c1t("rdecay")[:, par * 256:(par + 1) * 256]))
                if t < XT - 1:
                    groups.append(dict(ops=[("product", (0, P), pair * P, P, [(ret_k[:, t, tok(pair)], P1[:, t, RV + pair * P:RV + (pair + 1) * P])])
                                            for pair in range(2)], dsts=[(0, P, ret_u[:, t])],
                                       mask=c1t("rblock").unsqueeze(1).to_broadcast([P, 2, P])))
            schedule.append(Pieces(groups))

            def dve(eng):
                for t in range(XT - 1):
                    for pair in range(2):
                        ins = eng.scalar_tensor_tensor(out=ret_s[:, t + 1, pair], in0=ret_s[:, t, pair], scalar=c1t("rchunk")[:, pair:pair + 1],
                                                       in1=ret_u[:, t, pair], op0=ALU.mult, op1=ALU.add)
                    dve_s.chain(ins)

            schedule.append(Work(dve=dve))
            groups = []
            for t in range(XT):
                ops = [("product", (0, P), pair * P, P, [(qdT[:, pair, tok(t)], ret_s[:, t, pair])],
                        (pair == 0, False)) for pair in range(2)]
                ops += [("product", (0, P), h * 64, 64, [(ret_a[:, t, h % 2, (h // 2) * P:(h // 2 + 1) * P], P1[:, t, RV + h * 64:RV + h * 64 + 64])],
                         (False, h == 3)) for h in range(4)]
                groups.append(dict(ops=ops, dsts=[(0, P, P1[:, t, RQ:RQ + 256])]))
            schedule.append(Pieces(groups))

            schedule.append(Pieces([dict(ops=[("product", (0, P), 0, S, [(gate_w[:, :], gaT[:, :])])], dsts=[(0, P, z_t)])]))

            def dve(eng):
                eng.tensor_scalar(z_min, z_t, gate_b[:, 0:1], 0.0, ALU.add, ALU.min)

            schedule.append(Work(dve=dve))

            def act(eng):
                act_s.chain(eng.activation(z_abs, z_t, ACT.Abs, bias=gate_b[:, 0:1]))
                act_s.chain(eng.activation(z_exp, z_abs, ACT.Exp, scale=-1.0))
                eng.activation(z_t, z_exp, ACT.Ln, bias=1.0)

            def dve(eng):
                for h in range(4):
                    eng.tensor_scalar(g_qh[:, h], gqT[:, :], c1t("gheads")[:, h:h + 1], None, ALU.mult)

            schedule.append(Work(act=act, dve=dve))
            schedule.append(Work(dve=lambda eng: eng.tensor_tensor(log_a, z_min, z_t, ALU.subtract)))
            schedule.append(Pieces([dict(ops=turn([log_a[:, tok(t)] for t in range(XT)]), dsts=[(0, P, log_a_tok[:, :, :])])]))
            schedule.append(Pieces([dict(ops=[("product", (0, P), t * P, P, [(log_a_tok[:, t], c1t("tri"))]) for t in range(XT)],
                                         dsts=[(0, P, B[:, :])])]))
            schedule.append(GlaLevels())

            chunk_view = lambda z: z.rearrange("p (c n) -> p c n", n=GLA_C)
            dist, fac, fac2 = g_qh[:, 0], g_qh[:, 1], g_k[:, 0]

            def dve(eng):
                b = chunk_view(B[:, :])
                eng.tensor_tensor(chunk_view(dist), b, b[:, :, GLA_C - 1:GLA_C].to_broadcast([P, 8, GLA_C]), ALU.subtract)

            def act(eng):
                eng.activation(fac2, B[:, :], ACT.Exp, scale=1.0 / GATE_NORM)
                eng.activation(gla_decay[:, :], B[:, GLA_C - 1::GLA_C], ACT.Exp, scale=1.0 / GATE_NORM)

            schedule.append(Work(dve=dve, act=act, pool=lambda eng: eng.memset(gla_s[:, 0], 0.0)))
            schedule.append(Work(act=lambda eng: eng.activation(fac, dist, ACT.Exp, scale=-1.0 / GATE_NORM),
                                 dve=lambda eng: eng.tensor_tensor(g_qe[:, :], gqT[:, :], fac2, ALU.mult)))
            schedule.append(Work(dve=lambda eng: eng.tensor_tensor(g_kd[:, :], gkT[:, :], fac, ALU.mult)))
            schedule.append(Pieces([dict(ops=turn([g_kd[:, tok(t)] for t in range(XT)]), dsts=[(0, P, g_kdt[:, :, :])])]))
            groups = []
            for par in range(2):
                for two in range(2):
                    cs = [2 * t + par for t in (2 * two, 2 * two + 1)]
                    rows = slice(GLA_C * par, GLA_C * par + GLA_C)
                    groups.append(dict(ops=[("product", (0, P), i * 256, 256, [(g_kdt[rows, c // 2, :], P1[rows, c // 2, GV:GV + 256])])
                                            for i, c in enumerate(cs)],
                                       dsts=[(0, P, gla_u[:, cs[0]:cs[1] + 1:2, :])], mask=c1t("gblock").unsqueeze(1).to_broadcast([P, 2, 256])))
            schedule.append(Pieces(groups))

            def dve(eng):
                for c in range(7):
                    dve_s.chain(eng.scalar_tensor_tensor(out=gla_s[:, c + 1], in0=gla_s[:, c], scalar=gla_decay[:, c:c + 1], in1=gla_u[:, c],
                                                         op0=ALU.mult, op1=ALU.add))

            schedule.append(Work(dve=dve))
            groups = []
            for t in range(XT):
                ops = []
                for par in range(2):
                    c = 2 * t + par
                    ops.append(("product", (64 * par, 64 * par + 64), 0, 256, [(g_qe[:, c * GLA_C:(c + 1) * GLA_C], gla_s[:, c])], (True, False)))
                ops += [("product", (0, P), h * 64, 64, [(gla_a[:, h, tok(t)], P1[:, t, GV + h * 64:GV + h * 64 + 64])], (False, h == 3)) for h in range(4)]
                groups.append(dict(ops=ops, dsts=[(0, P, P1[:, t, GQ:GQ + 256])]))
            schedule.append(Pieces(groups))

            sq = at(f"head_sq_{l}", [P, 2, XT, 256], F32, ht_at)

            prelude_sp, prelude_dve = prelude_one(1) if l == 0 else prelude_even()
            m0, r0 = ms_ready.plan(2), rstd_ready.plan(3)

            def dve(eng):
                for i, c0 in enumerate((RQ, GQ)):
                    dve_s.chain(eng.tensor_tensor(sq[:, i], P1[:, :, c0:c0 + 256], P1[:, :, c0:c0 + 256], ALU.mult))
                    c = slice(16 * i, 16 * i + 16)
                    dve_s.chain(eng.tensor_reduce(headsq[:, c], sq[:, i].rearrange("p t (h d) -> p (t h) d", d=64), AX, ALU.add))
                    eng.tensor_scalar(headms[:, c], headsq[:, c], 1.0 / 64, EPS, ALU.mult, ALU.add).then_inc(ms_ready.sem, 1)
                for i, (c0, gc) in enumerate(((RQ, RG), (GQ, GG))):
                    eng.wait_ge(rstd_ready.sem, r0 + (1, 3)[i])
                    for t in range(XT):
                        z = P1[:, t, c0:c0 + 256]
                        r = headr[:, 16 * i + 4 * t:16 * i + 4 * t + 4].unsqueeze(2).to_broadcast([P, 4, 64])
                        dve_s.chain(eng.tensor_tensor(heads_view(z, 4), heads_view(z, 4), r, ALU.mult))
                        eng.tensor_tensor(z, z, P1[:, t, gc:gc + 256], ALU.mult)
                prelude_dve(eng)

            def pool(eng):
                for i in range(2):
                    c = slice(16 * i, 16 * i + 16)
                    eng.wait_ge(ms_ready.sem, m0 + i + 1)
                    eng.tensor_tensor(headr[:, c], headms[:, c], half64[:, c], ALU.pow).then_inc(rstd_ready.sem, 1)
                for t in range(XT):
                    g = heads_view(P1[:, t, GG:GG + 256], 4)
                    ins = eng.tensor_tensor(g, g, gla_gains[:, l, :].unsqueeze(1).to_broadcast([P, 4, 64]), ALU.mult)
                ins.then_inc(rstd_ready.sem, 1)

            schedule.append(Work(dve=dve, pool=pool, sp=prelude_sp))
            cols = [0, 128, 256, 384, RQ, RQ + 128, GQ, GQ + 128]
            schedule.append(MixTransposed(lambda t, kt: P1[:, t, cols[kt]:cols[kt] + P], XT))
            schedule.append(Linear(a["w_out"][l], [(n * HALF, HALF, range(XT)) for n in range(2)], lambda t, c0, n: Y[:, t, c0:c0 + n]))
            schedule.append(Residual([0] * XT))

        g_sub, g_ref, g_fac, g_ql, g_kl, g_mm, g_cp = (signal("gla_" + n) for n in ("difference", "distance", "factor", "q_level", "k_level", "scored", "placed"))

        class GlaLevels:

            def __init__(self):
                n = len(LEVELS)
                self.b = {s: s.plan(n) for s in (g_sub, g_ref, g_fac, g_ql, g_kl)}
                self.b[g_mm], self.b[g_cp] = g_mm.plan(n + 1), g_cp.plan(n + 1)

            def wait(self, eng, s, n):
                if n > 0:
                    eng.wait_ge(s.sem, self.b[s] + n)

            def place(self, dve, l):
                mask = c1t("levels")[:, l * P:(l + 1) * P].bitcast(U32).unsqueeze(1).to_broadcast([P, 4, P])
                self.wait(dve, g_mm, l + 1)
                self.wait(dve, g_cp, l)
                for t in range(XT):
                    ins = dve.copy_predicated(gla_a[:, :, tok(t)], mask, ps[:, 4 * (l % 2) + t, :].rearrange("p (h n) -> p h n", n=P))
                ins.then_inc(g_cp.sem, 1)

            def vector(self, dve):
                n = len(LEVELS)
                dve_s.mark(dve.memset(gla_a[:].rearrange("p h s -> p (h s)"), 0.0))
                dve.wait_ge(dve_s.sem, dve_s.n)
                for step in range(n + 2):
                    if step < n:
                        dist = g_dist[:, step % 2]
                        self.wait(dve, g_sub, step + 1)
                        dve.scalar_tensor_tensor(out=dist, in0=dist, scalar=-1.0, in1=dist, op0=ALU.mult, op1=ALU.max).then_inc(g_ref.sem, 1)
                    l = step - 1
                    if 0 <= l < n:
                        self.wait(dve, g_fac, l + 1)
                        self.wait(dve, g_mm, l - 1)
                        dve.tensor_tensor(g_q[:, l % 2], g_qh[:], g_exp[:, l % 2].unsqueeze(1).to_broadcast([P, 4, S]), ALU.mult)\
                           .then_inc(g_ql.sem, 1)
                    if step - 2 >= 0:
                        self.place(dve, step - 2)
                self.place(dve, n)

            def scalar(self, act):
                for l in range(len(LEVELS)):
                    self.wait(act, g_ref, l + 1)
                    self.wait(act, g_ql, l - 1)
                    self.wait(act, g_kl, l - 1)
                    act.activation(g_exp[:, l % 2], g_dist[:, l % 2], ACT.Exp, scale=-1.0 / GATE_NORM).then_inc(g_fac.sem, 1)

            def gpsimd(self, pool):
                for step in range(len(LEVELS) + 1):
                    l = step
                    if l < len(LEVELS):
                        s = LEVELS[l]
                        v = lambda z: z.rearrange("p (b n) -> p b n", n=2 * s)
                        b = v(B[:, :])
                        self.wait(pool, g_fac, l - 1)
                        pool.tensor_tensor(v(g_dist[:, l % 2]), b, b[:, :, s - 1:s].to_broadcast([P, S // (2 * s), 2 * s]), ALU.subtract)\
                            .then_inc(g_sub.sem, 1)
                    l = step - 1
                    if l < 0:
                        continue
                    self.wait(pool, g_fac, l + 1)
                    self.wait(pool, g_mm, l - 1)
                    pool.tensor_tensor(g_k[:, l % 2], gkT[:, :], g_exp[:, l % 2], ALU.mult).then_inc(g_kl.sem, 1)

            def tensor(self, pe):
                n = len(LEVELS)
                for l in range(n + 1):
                    if l < n:
                        self.wait(pe, g_ql, l + 1)
                        self.wait(pe, g_kl, l + 1)
                    self.wait(pe, g_cp, l - 1)
                    q, k = (g_q[:, l % 2], g_k[:, l % 2]) if l < n else (g_qh, gkT[:, :])
                    for t in range(XT):
                        ins = pe.matmul(ps[:, 4 * (l % 2) + t, :], k[:, tok(t)], q[:, :, tok(t)], start=True, stop=True)
                    ins.then_inc(g_mm.sem, 1)

            def sync(self, sp):
                pass

        con2 = at("constants_two", [P, TWO_W], F32, aux_at)
        c2t = lambda name: con2[:, slice(*TWO_COLS[name])]
        take = region(arena)
        PE_ = take("proj_even", [P, XT + CT, EV_IN])
        rope_tmp_even = at("rope_tmp_even", [P, 640], F32, take.where[0])
        cqT, ckvT = take("latent_q_t", [P, 2, TOK]), take("latent_kv_t", [P, TOK])
        w_uq, w_ukv = take("w_uq", [P, 2, D * 3 // 4]), take("w_ukv", [P, D])
        qpe = take("latent_q_rope", [P, XT + CT, 256])
        EV_END = take.where[0]
        take = region(ht_at)
        rope_p2 = take("rope_tmp_pool_two", [P, 1024])
        norm_junk = take("latent_squares", [P, XT + CT, 384])
        take = region(ht_at)
        qaT, kaT = take("even_q_t", [P, 4, TOK]), take("even_k_t", [P, 2, 2, TOK])
        probs2, probs2_t = take("att_probs_two", [P, 2, TOK]), take("att_probs_t_two", [P, 2, TOK])
        assert take.where[0] <= ht_end
        take = region(ht_at + 2 * 2 * TOK * 4)
        probsb, probsb_t = (at(n, [P, 2, TOK], F32, ht_at + i * 2 * TOK * 4) for i, n in enumerate(("att_probs_lat", "att_probs_t_lat")))
        vb = take("latent_values", [P, XT + CT, HALF])
        take = region(take.where[0])
        kbT, qbT = take("latent_k_t", [96, 4, TOK]), take("latent_q_heads_t", [96, 4, TOK])
        assert take.where[0] <= ht_end, (take.where[0], ht_end)
        take = region(arena)
        PO = take("proj_odd", [P, XT + CT, OD_IN])
        rope_tmp_odd = take("rope_tmp_odd", [P, 640])
        take = region(ht_at)
        probs3 = at("att_probs_three", [P, 4, TOK], F32, aux_at)
        probs3_t = at("att_probs_t_three", [P, 2, TOK], F32, arena + (XT + CT) * OD_IN * 4)
        qcT, kcT = take("odd_q_t", [P, 4, S]), take("odd_k_t", [P, 2, 2, TOK])
        qfT, kfT = take("diff_q_t", [P, 4, 2, S]), take("diff_k_t", [P, 4, TOK])
        assert take.where[0] <= ht_end

        def both(src, dst, **more):
            out = []
            for tiles in (range(XT), range(XT, XT + CT)):
                cols = slice(tiles[0] * P, tiles[-1] * P + P)
                out.append(dict(ops=turn([src(t) for t in tiles]), dsts=[(p0, p1, d(cols)) for p0, p1, d in dst], **more))
            return out

        def tables(width, t):
            return (c2t(f"cos{width}")[:, t * width:(t + 1) * width], c2t(f"sin{width}")[:, t * width:(t + 1) * width])

        def prelude_even():
            barrier = len(schedule)
            small_loads = [
                (con2[:, :], a["two"]),
                (sinks[:, :], a["ev_sink_2"][0].partition_broadcast(P)),
                (qn_col[:, :], a["ev_q_norm_2"][0].rearrange("(k p) -> p k", p=P)),
                (kvn_col[:, :], a["ev_kv_norm_2"][0].rearrange("(p o) -> p o", o=1)),
            ]
            loaded = load_in.plan(16 * len(small_loads)) + 16 * len(small_loads)

            def sp(eng):
                sp_waits_phase(eng, barrier)
                for dst, src in small_loads:
                    eng.dma_start(dst, src, allow_slow_non_contiguous=True).then_inc(load_in.sem, 16)

            def dve(eng):
                eng.wait_ge(load_in.sem, loaded)
                eng.tensor_scalar(neg_sinks[:, :], sinks[:, :], -1.0, None, ALU.mult)
                eng.tensor_copy(window[:, :], c2t("window"))

            return sp, dve

        def layer_even():
            g = lambda i: a["norm_g_2"][0, i]
            schedule.append(NormTransposed(True, 0, 1, (2, HALF)))
            allt = range(XT + CT)
            jobs = mods_two(0, [(2, "gate", g(1), [0, 1]), (3, "shift", None, [2])], 2)
            schedule.append(Linear(a["ev_w_in_2"][0], [(0, 512, allt), (512, 416, allt), (928, 256, allt)],
                                   lambda t, c0, n: PE_[:, t, c0:c0 + n], [jobs[0:2], jobs[2:4]]))
            linear = schedule[-1]

            def rotate_qk(eng):
                linear.wait_copied(eng, 1)
                for t in range(XT):
                    x = PE_[:, t, 0:640]
                    dve_s.chain(rotate(eng, dve_s, x, x, *tables(64, t), 10, 2, 16, rope_tmp_even))

            linear.beside["dve"] = {2: [rotate_qk]}
            barrier2 = len(schedule)
            loaded2 = load_in.plan(32) + 32

            def sp(eng):
                sp_waits_phase(eng, barrier2)
                eng.dma_start(w_uq[:, :, :], a["ev_w_uq_2"][0].rearrange("(k p) n -> p k n", p=P)).then_inc(load_in.sem, 16)
                eng.dma_start(w_ukv[:, :], a["ev_w_ukv_2"][0]).then_inc(load_in.sem, 16)

            def act(eng):
                for t in allt:
                    eng.activation(norm_junk[:, t, 0:256], PE_[:, t, 768:1024], ACT.Square, accum_out=headsq[:, t:t + 1])
                    eng.activation(norm_junk[:, t, 256:384], PE_[:, t, 1024:1152], ACT.Square, accum_out=headsq[:, 8 + t:9 + t])

            def pool(eng):
                for t in range(XT):
                    x = PE_[:, t, 1152:1184]
                    pool_s.chain(rotate(eng, pool_s, x, x, *tables(32, t), 1, 2, 8, rope_p2))

            schedule.append(Work(act=act, pool=pool, sp=sp))

            def dve(eng):
                eng.tensor_scalar(headms[:, 0:6], headsq[:, 0:6], 1.0 / 256, EPS, ALU.mult, ALU.add)
                eng.tensor_scalar(headms[:, 8:14], headsq[:, 8:14], 1.0 / 128, EPS, ALU.mult, ALU.add)

            schedule.append(Work(dve=dve))
            schedule.append(Work(pool=lambda eng: eng.tensor_tensor(headr[:, 0:16], headms[:, 0:16], half64[:, 0:16], ALU.pow)))

            def dve(eng):
                eng.wait_ge(load_in.sem, loaded2)
                for t in allt:
                    for c0, c1_, s in ((768, 1024, 0), (1024, 1152, 8)):
                        z = PE_[:, t, c0:c1_]
                        eng.tensor_scalar(z, z, headr[:, s + t:s + t + 1], None, ALU.mult)

            schedule.append(Work(dve=dve))
            groups = []
            for pair in range(4):
                groups += both(lambda t: PE_[:, t, pair * P:(pair + 1) * P], [(0, P, lambda c, pair=pair: qaT[:, pair, c])])
            for kv in range(2):
                groups += both(lambda t: PE_[:, t, 512 + 64 * kv:576 + 64 * kv],
                               [(0, 64, lambda c, kv=kv: kaT[0:64, kv, 0, c]), (0, 64, lambda c, kv=kv: kaT[64:P, kv, 1, c])])
                groups += both(lambda t: PE_[:, t, 768 + P * kv:768 + P * (kv + 1)], [(0, P, lambda c, kv=kv: cqT[:, kv, c])],
                               scale=qn_col[:, kv:kv + 1])
            groups += both(lambda t: PE_[:, t, 1024:1152], [(0, P, lambda c: ckvT[:, c])], scale=kvn_col[:, 0:1])
            schedule.append(Pieces(groups, lambda eng: clear_other_head(eng, kaT)))

            units = []
            for t in allt:
                for h in range(8):
                    local = [b for b in (t - 1, t, t + 1) if 0 <= b < XT] if t < XT else []
                    blocks = local + [XT, XT + 1]
                    mask = [(window[:, (0 if b < t else P):(P if b < t else 2 * P)], i * P) for i, b in enumerate(local) if b != t]
                    units.append(dict(q=qaT[:, h // 2, tok(t)], keys=[(kaT[:, h // 4, h % 2, b * P:(b + n) * P], c) for b, n, c in key_runs(blocks)],
                                      mask=mask, values=[PE_[:, b, 640 + 64 * (h // 4):704 + 64 * (h // 4)] for b in blocks], scale=0.125, sink=h,
                                      finish=("plain", PE_[:, t, h * 64:h * 64 + 64], None)))
            schedule.append(Attention(units, probs2, probs2_t, stats, neg_sinks, sinks))

            w_kv = w_ukv[:, :].rearrange("p (h n) -> p h n", h=8)
            w_q = w_uq[:, :, :].rearrange("p k (h n) -> p k h n", h=8)
            groups = []
            for t in allt:
                groups.append(dict(ops=[("product", (0, P), 0, HALF, [(ckvT[:, tok(t)], w_kv[:, :, 64:128])])], dsts=[(0, P, vb[:, t, :])]))
                groups.append(dict(ops=[("product", (0, P), 0, 256, [(cqT[:, k, tok(t)], w_q[:, k, :, 64:96]) for k in range(2)])],
                                   dsts=[(0, P, qpe[:, t, :])]))
            schedule.append(Pieces(groups))

            tmp_q = at("rope_tmp_latent", [P, 256], F32, ht_at)

            def dve(eng):
                for t in range(XT):
                    x = qpe[:, t, :]
                    dve_s.chain(rotate(eng, dve_s, x, x, *tables(32, t), 8, 2, 8, tmp_q))

            schedule.append(Work(dve=dve))
            for four in range(2):
                groups = []
                for i in range(4):
                    h = 4 * four + i
                    for c0, n in ((0, S), (S, CTX)):
                        groups.append(dict(ops=[("product", (0, 64), 0, n, [(w_kv[:, h, 0:64], ckvT[:, c0:c0 + n])])], dsts=[(0, 64, kbT[0:64, i, c0:c0 + n])]))
                        groups.append(dict(ops=[("product", (0, 64), 0, n, [(w_q[:, k, h, 0:64], cqT[:, k, c0:c0 + n]) for k in range(2)])],
                                           dsts=[(0, 64, qbT[0:64, i, c0:c0 + n])]))
                groups += both(lambda t: PE_[:, t, 1152:1184], [(0, 32, lambda c, i=i: kbT[64:96, i, c]) for i in range(4)])
                groups += both(lambda t: qpe[:, t, four * P:(four + 1) * P], [(32 * i, 32 * i + 32, lambda c, i=i: qbT[64:96, i, c]) for i in range(4)])
                schedule.append(Pieces(groups))
                units = []
                for t in allt:
                    for i in range(4):
                        h = 4 * four + i
                        blocks = list(range(XT + CT)) if t < XT else [XT, XT + 1]
                        spans = ((0, S), (S, CTX)) if t < XT else ((S, CTX),)
                        keys = [(kbT[:, i, c0:c0 + n], c0 if t < XT else 0) for c0, n in spans]
                        units.append(dict(q=qbT[:, i, tok(t)], keys=keys, mask=[], values=[vb[:, b, h * 64:h * 64 + 64] for b in blocks],
                                          scale=96 ** -0.5, sink=None, finish=("plain", PE_[:, t, HALF + h * 64:HALF + h * 64 + 64], None)))
                schedule.append(Attention(units, probsb, probsb_t, stats))
            schedule.append(MixTransposed(lambda t, kt: PE_[:, t, kt * P:(kt + 1) * P], XT + CT))
            jobs = mods_two(0, [(4, "scale", g(2), [3]), (5, "gate", g(3), [2, 3])], 2)
            schedule.append(Linear(a["ev_w_out_2"][0], [(n * HALF, HALF, allt) for n in range(2)], lambda t, c0, n: Y[:, t, c0:c0 + n],
                                   [jobs[0:2], jobs[2:4]]))
            schedule.append(Residual([0] * XT + [1] * CT))
            schedule.append(NormTransposed(True, 2, 3, (4, GROUP)))
            g = lambda i: a["norm_g_2"][1, i]
            jobs = mods_two(1, [(0, "shift", None, [4]), (1, "scale", g(0), [5])], 2, mod_acc_gates)
            jobs += mods_two(1, [(3, "shift", None, [6]), (4, "scale", g(2), [7])], 1, mod_acc_gates)
            schedule.append(FeedForward(a["ffn_w_in_2"][0], a["ffn_w_out_2"][0], XT + CT, [jobs[2 * p:2 * p + 2] for p in range(4)]))
            schedule.append(Residual([2] * XT + [3] * CT))

        def layer_odd():
            g = lambda i: a["norm_g_2"][1, i]
            small_loads = [
                (con2[:, :], a["two"]),
                (qk_gain[:, :, :], a["od_qk_norm_2"][0].partition_broadcast(P)),
                (lam_in[:, :, :], a["od_lambda_2"][0].partition_broadcast(P)),
                (sub_gain[:, :], a["od_subln_2"][0].partition_broadcast(P)),
            ]
            barrier, loaded = len(schedule) - 1, load_in.plan(16 * len(small_loads)) + 16 * len(small_loads)

            def sp(eng):
                sp_waits_phase(eng, barrier)
                for dst, src in small_loads:
                    eng.dma_start(dst, src, allow_slow_non_contiguous=True).then_inc(load_in.sem, 16)

            schedule.append(NormTransposed(True, 4, 5, (2, HALF), sp))
            allt, xt = range(XT + CT), range(XT)
            jobs = mods_two(1, [(2, "gate", g(1), [0]), (5, "gate", g(3), [2])], 1)
            schedule.append(Linear(a["od_w_in_2"][0], [(0, 512, xt), (512, 256, allt), (768, 512, xt), (1280, 512, allt), (1792, 512, allt)],
                                   lambda t, c0, n: PO[:, t, c0:c0 + n], [[job] for job in jobs]))
            linear = schedule[-1]
            parts = [(t, 0, 10) if t < XT else (t, 8, 10) for t in allt]
            m0, r0 = ms_ready.plan(1), rstd_ready.plan(4)

            def lambda_sums(eng):
                eng.wait_ge(load_in.sem, loaded)
                eng.tensor_scalar(sub_gain[:, :], sub_gain[:, :], 1.0 - LAM_INIT, None, ALU.mult)
                pairs = lam_in[:, :, :].rearrange("p (a b) d -> p a b d", b=2)
                dve_s.chain(eng.tensor_tensor(lam_prod[:, :, :], pairs[:, :, 0, :], pairs[:, :, 1, :], ALU.mult))
                eng.tensor_reduce(lam_sum[:, :], lam_prod[:, :, :], AX, ALU.add).then_inc(lambda_summed.sem, 1)

            def lambda_exp(eng):
                eng.wait_ge(lambda_summed.sem, 1)
                eng.activation(lam_exp[:, :], lam_sum[:, :], ACT.Exp).then_inc(lambda_exped.sem, 1)

            def lambda_total(eng):
                eng.wait_ge(lambda_exped.sem, 1)
                dve_s.chain(eng.tensor_tensor(neg_lam[:, :], lam_exp[:, 1:2], lam_exp[:, 0:1], ALU.subtract))
                eng.tensor_scalar(neg_lam[:, :], neg_lam[:, :], -LAM_INIT, None, ALU.add)

            def head_squares(eng):
                linear.wait_copied(eng, 1)
                for i, (t, h0, h1) in enumerate(parts):
                    z, sq = PO[:, t, h0 * 64:h1 * 64], rope_tmp_odd[:, 0:(h1 - h0) * 64]
                    dve_s.chain(eng.tensor_tensor(sq, z, z, ALU.mult))
                    dve_s.chain(eng.tensor_reduce(headsq[:, t * 10 + h0:t * 10 + h1], heads_view(sq, h1 - h0), AX, ALU.add))
                eng.tensor_scalar(headms[:, 0:60], headsq[:, 0:60], 1.0 / 64, EPS, ALU.mult, ALU.add).then_inc(ms_ready.sem, 1)

            def head_rstd(i):
                def step(eng):
                    c = slice(15 * i, 15 * i + 15)
                    eng.wait_ge(ms_ready.sem, m0 + 1)
                    eng.tensor_tensor(headr[:, c], headms[:, c], half64[:, c], ALU.pow).then_inc(rstd_ready.sem, 1)
                return step

            def norm_heads(eng):
                eng.wait_ge(rstd_ready.sem, r0 + 4)
                for t, h0, h1 in parts:
                    z = heads_view(PO[:, t, h0 * 64:h1 * 64], h1 - h0)
                    dve_s.chain(eng.tensor_tensor(z, z, headr[:, t * 10 + h0:t * 10 + h1].unsqueeze(2).to_broadcast([P, h1 - h0, 64]), ALU.mult))
                    for which, lo, hi in ((0, h0, 8), (1, 8, 10)):
                        if lo < hi:
                            z = heads_view(PO[:, t, lo * 64:hi * 64], hi - lo)
                            ins = eng.tensor_tensor(z, z, qk_gain[:, which, :].unsqueeze(1).to_broadcast([P, hi - lo, 64]), ALU.mult)
                    dve_s.chain(ins)
                    if t < XT:
                        x = PO[:, t, 0:640]
                        dve_s.chain(rotate(eng, dve_s, x, x, *tables(64, t), 10, 2, 16, rope_tmp_odd))

            def rotate_diff(c0, chunk):
                def step(eng):
                    linear.wait_copied(eng, chunk)
                    for t in xt:
                        x = PO[:, t, c0:c0 + HALF]
                        dve_s.chain(rotate(eng, dve_s, x, x, *tables(64, t), 8, 2, 16, rope_tmp_odd))
                return step

            linear.beside["act"] = {2: [lambda_exp]}
            linear.beside["dve"] = {1: [lambda_sums], 2: [head_squares], 3: [lambda_total, rotate_diff(768, 2)], 4: [norm_heads, rotate_diff(1280, 3)]}
            linear.beside["pool"] = {3: [head_rstd(i) for i in range(4)]}
            groups = []
            for pair in range(4):
                groups.append(dict(ops=turn([PO[:, t, pair * P:(pair + 1) * P] for t in xt]), dsts=[(0, P, qcT[:, pair, :])]))
                groups.append(dict(ops=turn([PO[:, t, 768 + pair * P:768 + (pair + 1) * P] for t in xt]), dsts=[(0, 64, qfT[0:64, pair, 0, :]), (64, P, qfT[64:P, pair, 1, :])]))
                groups += both(lambda t: PO[:, t, 1280 + pair * P:1280 + (pair + 1) * P], [(0, P, lambda c, pair=pair: kfT[:, pair, c])])
            for kv in range(2):
                groups += both(lambda t: PO[:, t, 512 + 64 * kv:576 + 64 * kv],
                               [(0, 64, lambda c, kv=kv: kcT[0:64, kv, 0, c]), (0, 64, lambda c, kv=kv: kcT[64:P, kv, 1, c])])
            schedule.append(Pieces(groups, lambda eng: (clear_other_head(eng, kcT), clear_other_head(eng, qfT))))
            def plain_unit(t, h):
                return dict(q=qcT[:, h // 2, tok(t)], keys=[(kcT[:, h // 4, h % 2, c0:c0 + n], c0) for c0, n in ((0, S), (S, CTX))], mask=[],
                            values=[PO[:, b, 640 + 64 * (h // 4):704 + 64 * (h // 4)] for b in allt], scale=0.125, sink=None,
                            finish=("plain", PO[:, t, h * 64:h * 64 + 64], None))

            def diff_unit(t, h, i):
                return dict(q=qfT[:, h, i, tok(t)], keys=[(kfT[:, h, c0:c0 + n], c0) for c0, n in ((0, S), (S, CTX))], mask=[],
                            values=[PO[:, b, 1792 + h * P:1792 + (h + 1) * P] for b in allt], scale=0.125, sink=None,
                            finish=("plain", PO[:, t, 768 + h * P:768 + (h + 1) * P], None))

            units = []
            for t in xt:
                for h in range(4):
                    u = len(units)
                    units += [dict(diff_unit(t, h, 0), second=u + 2), plain_unit(t, 2 * h),
                              dict(diff_unit(t, h, 1), first=u), plain_unit(t, 2 * h + 1)]
            schedule.append(Attention(units, probs3, probs3_t, stats, neg_lambda=neg_lam[:, 0:1]))

            dsq = at("diff_squares", [P, XT, HALF], F32, ht_at)

            def dve(eng):
                dve_s.chain(eng.tensor_tensor(dsq[:], PO[:, 0:XT, 768:1280], PO[:, 0:XT, 768:1280], ALU.mult))
                dve_s.chain(eng.tensor_reduce(headsq[:, 0:16], dsq[:].rearrange("p t (h d) -> p (t h) d", d=P), AX, ALU.add))
                eng.tensor_scalar(headms[:, 0:16], headsq[:, 0:16], 1.0 / P, EPS, ALU.mult, ALU.add)

            schedule.append(Work(dve=dve))
            schedule.append(Work(pool=lambda eng: eng.tensor_tensor(headr[:, 0:16], headms[:, 0:16], half64[:, 0:16], ALU.pow)))

            def dve(eng):
                for t in xt:
                    for h in range(4):
                        z = PO[:, t, 768 + h * P:768 + (h + 1) * P]
                        eng.scalar_tensor_tensor(out=z, in0=z, scalar=headr[:, 4 * t + h:4 * t + h + 1], in1=sub_gain[:, :], op0=ALU.mult, op1=ALU.mult)

            schedule.append(Work(dve=dve))
            schedule.append(MixTransposed(lambda t, kt: PO[:, t, (kt * P if kt < 4 else 256 + kt * P):(kt * P if kt < 4 else 256 + kt * P) + P], XT))
            schedule.append(Linear(a["od_w_out_2"][0], [(n * HALF, HALF, xt) for n in range(2)], lambda t, c0, n: Y[:, t, c0:c0 + n]))
            schedule.append(Residual([0] * XT))
            schedule.append(NormTransposed(False, 6, 7, (4, GROUP)))
            schedule.append(FeedForward(a["ffn_w_in_2"][1], a["ffn_w_out_2"][1], XT))
            schedule.append(Residual([2] * XT, last=True))

        setup_phases()
        x_landed = signal("x_landed")

        def load_x(sp):
            for t in range(XT):
                sp.dma_start(X[:, t, :], a["x"][0, t * P:(t + 1) * P, :]).then_inc(x_landed.sem, 16)

        schedule.append(Modulation(mods_one(0, [(0, "shift", None, [0]), (1, "scale", a["pre_norm_gain"][0], [1])]), {2: load_x, 4: first_sp}))
        schedule.append(Work(act=lambda eng: eng.wait_ge(x_landed.sem, 16 * XT)))
        for l in range(DEPTH):
            layer_one(l)
        layer_even()
        layer_odd()

        block = ctx.enter_context(nc.Block())

        @block.sync
        def _(sp):
            for i, phase in enumerate(schedule):
                phase.sync(sp)
            for t in range(XT):
                sp.wait_ge(x_added.sem, schedule[-1].x0 + t + 1)
                sp.dma_start(out[0, t * P:(t + 1) * P, :], X[:, t, :]).then_inc(out_landed.sem, 16)
            sp.wait_ge(out_landed.sem, 16 * XT)

        @block.tensor
        def _(pe):
            for phase in schedule:
                phase.tensor(pe)
                if not flows(phase):
                    phase_end(pe, "pe")

        @block.scalar
        def _(act):
            nonlocal act_s
            act_s = Steps(act, act_step.sem)
            for phase in schedule:
                phase.scalar(act)
                if not flows(phase):
                    phase_end(act, "act")

        @block.vector
        def _(dve):
            nonlocal dve_s
            dve_s = Steps(dve, dve_step.sem)
            for phase in schedule:
                phase.vector(dve)
                if not flows(phase):
                    phase_end(dve, "dve")

        @block.gpsimd
        def _(pool):
            nonlocal pool_s
            pool_s = Steps(pool, pool_step.sem)
            for phase in schedule:
                phase.gpsimd(pool)
                if not flows(phase):
                    phase_end(pool, "pool")


_INS = ["x", "c", "positions", "w_mod", "b_mod", "pre_norm_gain", "post_norm_gain", "w_in", "attn_sinks", "gla_gate_w",
        "gla_gate_b", "gla_norm_gain", "w_out", "c_2", "ctx_2", "c_ctx_2", "ada_w_2", "ada_b_2", "norm_g_2", "ffn_w_in_2",
        "ffn_w_out_2", "ev_w_in_2", "ev_sink_2", "ev_q_norm_2", "ev_w_uq_2", "ev_kv_norm_2", "ev_w_ukv_2", "ev_w_out_2",
        "od_w_in_2", "od_qk_norm_2", "od_lambda_2", "od_subln_2", "od_w_out_2"]


def lay_out(nc, inputs):
    arrays, args = {}, {}
    tables = {"static": static_constants(), "one": block_one_constants(), "two": block_two_constants()}
    for name in _INS + list(tables):
        v = np.ascontiguousarray(tables[name] if name in tables else inputs[name])
        arrays[f"in_{name}_dram"] = v
        args[name] = nc.dram_tensor(f"in_{name}_dram", v.shape, mybir.dt.from_np(v.dtype), kind="ExternalInput").ap()
    return arrays, args


def kernel(**inputs):
    import concourse.bacc as bacc
    from concourse.bass_utils import run_bass_kernel_spmd

    nc = bacc.Bacc("TRN2", target_bir_lowering=False, num_devices=1)
    arrays, args = lay_out(nc, inputs)
    out = nc.dram_tensor("out_0_dram", (1, S, D), F32, kind="ExternalOutput").ap()
    build(nc, args, out)
    r = run_bass_kernel_spmd(nc, [arrays], core_ids=[0])
    return r.results[0]["out_0_dram"]
```
